# Optimizing a Trainium2 kernel written in Bass

```python
import math
import jax, jax.numpy as jnp
from jax import lax
import numpy as np

D_MODEL = 1024
BATCH = 1
SEQ = 512
DEPTH = 1

D_MIX = 1024
GDN_HEADS = 4
GDN_HEAD_DIM = 128
GDN_WIDTH = 512
GDN_CONV = 4
GDN_CHUNK = 64
DSA_HEADS = 4
DSA_HEAD_DIM = 64
DSA_WIDTH = 256
DSA_Q_RANK = 256
DSA_KV_RANK = 128
IDX_HEADS = 4
IDX_DIM = 64
DSA_TOPK_MAX = 256
Q_BLOCK = 128
CONV_CH = 256
CONV_WIDTH = 31
MEM_LEN = 256
XA_HEADS = 4
XA_HEAD_DIM = 128
XA_WIDTH = 512
D_FF = 4 * D_MODEL
EPS = 1e-6

IN_SPLITS = (3 * GDN_WIDTH, GDN_WIDTH, GDN_HEADS, GDN_HEADS,
             DSA_Q_RANK, DSA_KV_RANK, IDX_DIM, IDX_HEADS, 2 * CONV_CH)
N_IN = 3 * GDN_WIDTH + GDN_WIDTH + 2 * GDN_HEADS + DSA_Q_RANK + DSA_KV_RANK + IDX_DIM + IDX_HEADS + 2 * CONV_CH


def rms_norm(x, g):
    xf = x.astype(jnp.float32)
    y = xf * lax.rsqrt(jnp.mean(xf * xf, axis=-1, keepdims=True) + EPS)
    return (y * g.astype(jnp.float32)).astype(x.dtype)

def layer_norm(x, g, b):
    xf = x.astype(jnp.float32)
    mu = jnp.mean(xf, axis=-1, keepdims=True)
    xc = xf - mu
    var = jnp.mean(xc * xc, axis=-1, keepdims=True)
    y = xc * lax.rsqrt(var + EPS) * g.astype(jnp.float32) + b.astype(jnp.float32)
    return y.astype(x.dtype)

def l2_norm(x):
    return x * lax.rsqrt(jnp.sum(x * x, axis=-1, keepdims=True) + EPS)

def split_cols(t, sizes):
    out = []
    off = 0
    for n in sizes:
        out.append(t[..., off:off + n])
        off += n
    return out

def causal_depthwise_conv(x, w):
    k, c = w.shape
    return lax.conv_general_dilated(
        x, w[:, None, :].astype(x.dtype), window_strides=(1,), padding=((k - 1, 0),),
        dimension_numbers=("NWC", "WIO", "NWC"), feature_group_count=c)

def gated_delta_rule(q, k, v, g, beta):
    b, s, h, dk = q.shape
    dv = v.shape[-1]
    c = GDN_CHUNK
    n = s // c
    q = q * (dk ** -0.5)

    def chunk(t):
        return jnp.moveaxis(t.reshape((b, n, c) + t.shape[2:]), 3, 2)

    qc, kc, vc = chunk(q), chunk(k), chunk(v)
    gc, bc = chunk(g), chunk(beta)
    decay = jnp.cumsum(gc, axis=-1)
    tril = jnp.tril(jnp.ones((c, c), bool))
    strict = jnp.tril(jnp.ones((c, c), bool), -1)
    diff = decay[..., :, None] - decay[..., None, :]
    gamma = jnp.where(tril, jnp.exp(jnp.where(tril, diff, 0.0)), 0.0)
    kb = kc * bc[..., None]
    a_mat = jnp.where(strict, jnp.einsum("bnhid,bnhjd->bnhij", kb, kc) * gamma, 0.0)
    lhs = a_mat + jnp.eye(c, dtype=a_mat.dtype)
    rhs = jnp.concatenate([vc * bc[..., None], kb * jnp.exp(decay)[..., None]], axis=-1)
    sol = lax.linalg.triangular_solve(lhs, rhs, left_side=True, lower=True, unit_diagonal=True)
    u, w = sol[..., :dv], sol[..., dv:]
    qk = jnp.where(tril, jnp.einsum("bnhid,bnhjd->bnhij", qc, kc) * gamma, 0.0)

    def step(state, inp):
        q_i, k_i, u_i, w_i, qk_i, dec_i = inp
        v_new = u_i - jnp.einsum("bhcd,bhde->bhce", w_i, state)
        o = (jnp.einsum("bhcd,bhde->bhce", q_i * jnp.exp(dec_i)[..., None], state)
             + jnp.einsum("bhij,bhje->bhie", qk_i, v_new))
        last = dec_i[..., -1]
        k_dec = k_i * jnp.exp(last[..., None] - dec_i)[..., None]
        state = state * jnp.exp(last)[..., None, None] + jnp.einsum("bhcd,bhce->bhde", k_dec, v_new)
        return state, o

    xs = tuple(jnp.moveaxis(t, 1, 0) for t in (qc, kc, u, w, qk, decay))
    _, o = lax.scan(step, jnp.zeros((b, h, dk, dv), jnp.float32), xs)
    o = jnp.swapaxes(jnp.moveaxis(o, 0, 1), 2, 3)
    return o.reshape(b, s, h, dv)

def gdn_mixer(qkv, z, a_g, b_g, conv_w, a_log, dt_bias, norm_g):
    b, s, _ = qkv.shape
    dt = qkv.dtype
    qkv = jax.nn.silu(causal_depthwise_conv(qkv, conv_w)).astype(jnp.float32)
    q, k, v = jnp.split(qkv, 3, axis=-1)
    shp = (b, s, GDN_HEADS, GDN_HEAD_DIM)
    q = l2_norm(q.reshape(shp))
    k = l2_norm(k.reshape(shp))
    v = v.reshape(shp)
    g = -jnp.exp(a_log.astype(jnp.float32)) * jax.nn.softplus(a_g.astype(jnp.float32) + dt_bias.astype(jnp.float32))
    beta = jax.nn.sigmoid(b_g.astype(jnp.float32))
    o = gated_delta_rule(q, k, v, g, beta)
    o = rms_norm(o, norm_g) * jax.nn.silu(z.astype(jnp.float32).reshape(shp))
    return o.reshape(b, s, GDN_WIDTH).astype(dt)

def dsa_mixer(c_q, c_kv, k_idx, w_idx, w_qb, w_qi, w_kvb, q_norm_g, k_norm_g):
    b, s, _ = c_q.shape
    q = rms_norm((c_q @ w_qb).reshape(b, s, DSA_HEADS, DSA_HEAD_DIM), q_norm_g)
    kv = c_kv @ w_kvb
    k = rms_norm(kv[..., :DSA_HEAD_DIM], k_norm_g)
    v = kv[..., DSA_HEAD_DIM:]
    q_idx = (c_q @ w_qi).reshape(b, s, IDX_HEADS, IDX_DIM)
    w_idx = w_idx.astype(jnp.float32) * (IDX_HEADS ** -0.5 * IDX_DIM ** -0.5)
    k_idx = k_idx.astype(jnp.float32)
    topk = min(DSA_TOPK_MAX, s // 4)
    nb = s // Q_BLOCK
    pos = jnp.arange(s, dtype=jnp.int32)

    def blk(t):
        return jnp.moveaxis(t.reshape((b, nb, Q_BLOCK) + t.shape[2:]), 1, 0)

    def attend(inp):
        q_b, qi_b, w_b, t_b = inp
        causal = pos[None, :] <= t_b[:, None]
        idx_logits = jnp.einsum("bqhd,bsd->bqhs", qi_b.astype(jnp.float32), k_idx)
        score = jnp.einsum("bqh,bqhs->bqs", w_b, jax.nn.relu(idx_logits))
        score = jnp.where(causal[None], score, -jnp.inf)
        _, sel = lax.top_k(score, topk)
        k_sel = jax.vmap(lambda kk, ii: kk[ii])(k, sel)
        v_sel = jax.vmap(lambda vv, ii: vv[ii])(v, sel)
        valid = sel <= t_b[None, :, None]
        logits = jnp.einsum("bqhd,bqkd->bqhk", q_b.astype(jnp.float32), k_sel.astype(jnp.float32)) * (DSA_HEAD_DIM ** -0.5)
        logits = jnp.where(valid[:, :, None, :], logits, -jnp.inf)
        p = jax.nn.softmax(logits, axis=-1)
        return jnp.einsum("bqhk,bqkd->bqhd", p, v_sel.astype(jnp.float32)).astype(q_b.dtype)

    o = lax.map(attend, (blk(q), blk(q_idx), blk(w_idx), pos.reshape(nb, Q_BLOCK)))
    return jnp.moveaxis(o, 0, 1).reshape(b, s, DSA_WIDTH)

def conv_mixer(ug, dw, dw_b, ln_g, ln_b):
    u, gate = jnp.split(ug, 2, axis=-1)
    y = u * jax.nn.sigmoid(gate)
    y = causal_depthwise_conv(y, dw) + dw_b
    y = layer_norm(y, ln_g, ln_b)
    return jax.nn.silu(y)

def memory_cross_attention(h, mem_n, wq, wkv, q_g, k_g, wo):
    b, s, _ = h.shape
    m = mem_n.shape[1]
    q = rms_norm((h @ wq).reshape(b, s, XA_HEADS, XA_HEAD_DIM), q_g)
    kv = mem_n @ wkv
    k = rms_norm(kv[..., :XA_WIDTH].reshape(b, m, XA_HEADS, XA_HEAD_DIM), k_g)
    v = kv[..., XA_WIDTH:].reshape(b, m, XA_HEADS, XA_HEAD_DIM)
    logits = jnp.einsum("bshd,bmhd->bhsm", q.astype(jnp.float32), k.astype(jnp.float32)) * (XA_HEAD_DIM ** -0.5)
    p = jax.nn.softmax(logits, axis=-1)
    o = jnp.einsum("bhsm,bmhd->bshd", p, v.astype(jnp.float32)).astype(h.dtype)
    return o.reshape(b, s, XA_WIDTH) @ wo

def first_inputs(seed: int = 0) -> dict:
    key = jax.random.key(seed)
    ks = jax.random.split(key, 32)
    f32 = jnp.float32

    def nrm(k, shape, scale):
        return jax.random.normal(k, shape, f32) * scale

    def gain(k, shape):
        return 1.0 + 0.02 * jax.random.normal(k, shape, f32)

    dt = jnp.exp(jax.random.uniform(ks[5], (DEPTH, GDN_HEADS), f32, math.log(1e-3), math.log(1e-1)))
    dt_bias = dt + jnp.log(-jnp.expm1(-dt))
    return {
        "x": nrm(ks[0], (BATCH, SEQ, D_MODEL), 1.0),
        "mem": nrm(ks[1], (BATCH, MEM_LEN, D_MODEL), 1.0),
        "norm_mix": gain(ks[2], (DEPTH, D_MODEL)),
        "w_in": nrm(ks[3], (DEPTH, D_MODEL, N_IN), D_MODEL ** -0.5),
        "gdn_conv": nrm(ks[4], (DEPTH, GDN_CONV, 3 * GDN_WIDTH), GDN_CONV ** -0.5),
        "gdn_a_log": jnp.log(jax.random.uniform(ks[6], (DEPTH, GDN_HEADS), f32, 1.0, 16.0)),
        "gdn_dt_bias": dt_bias,
        "gdn_norm": gain(ks[7], (DEPTH, GDN_HEAD_DIM)),
        "dsa_w_qb": nrm(ks[8], (DEPTH, DSA_Q_RANK, DSA_WIDTH), DSA_Q_RANK ** -0.5),
        "dsa_w_qi": nrm(ks[9], (DEPTH, DSA_Q_RANK, IDX_HEADS * IDX_DIM), DSA_Q_RANK ** -0.5),
        "dsa_w_kvb": nrm(ks[10], (DEPTH, DSA_KV_RANK, 2 * DSA_HEAD_DIM), DSA_KV_RANK ** -0.5),
        "dsa_q_norm": gain(ks[11], (DEPTH, DSA_HEAD_DIM)),
        "dsa_k_norm": gain(ks[12], (DEPTH, DSA_HEAD_DIM)),
        "conv_dw": nrm(ks[13], (DEPTH, CONV_WIDTH, CONV_CH), CONV_WIDTH ** -0.5),
        "conv_dw_b": nrm(ks[14], (DEPTH, CONV_CH), 0.02),
        "conv_ln_g": gain(ks[15], (DEPTH, CONV_CH)),
        "conv_ln_b": nrm(ks[16], (DEPTH, CONV_CH), 0.02),
        "w_out": nrm(ks[17], (DEPTH, D_MIX, D_MODEL), D_MIX ** -0.5),
        "norm_mem": gain(ks[18], (D_MODEL,)),
        "norm_cross": gain(ks[19], (DEPTH, D_MODEL)),
        "xa_wq": nrm(ks[20], (DEPTH, D_MODEL, XA_WIDTH), D_MODEL ** -0.5),
        "xa_wkv": nrm(ks[21], (DEPTH, D_MODEL, 2 * XA_WIDTH), D_MODEL ** -0.5),
        "xa_q_norm": gain(ks[22], (DEPTH, XA_HEAD_DIM)),
        "xa_k_norm": gain(ks[23], (DEPTH, XA_HEAD_DIM)),
        "xa_wo": nrm(ks[24], (DEPTH, XA_WIDTH, D_MODEL), XA_WIDTH ** -0.5),
        "norm_mlp": gain(ks[25], (DEPTH, D_MODEL)),
        "mlp_w1": nrm(ks[26], (DEPTH, D_MODEL, D_FF), D_MODEL ** -0.5),
        "mlp_w2": nrm(ks[27], (DEPTH, D_FF, D_MODEL), D_FF ** -0.5),
    }

def first_block(x, mem, norm_mix, w_in, gdn_conv, gdn_a_log, gdn_dt_bias, gdn_norm,
              dsa_w_qb, dsa_w_qi, dsa_w_kvb, dsa_q_norm, dsa_k_norm,
              conv_dw, conv_dw_b, conv_ln_g, conv_ln_b, w_out,
              norm_mem, norm_cross, xa_wq, xa_wkv, xa_q_norm, xa_k_norm, xa_wo,
              norm_mlp, mlp_w1, mlp_w2):
    mem_n = rms_norm(mem, norm_mem)
    for l in range(DEPTH):
        h = rms_norm(x, norm_mix[l])
        proj = h @ w_in[l]
        qkv, z, a_g, b_g, c_q, c_kv, k_idx, w_idx, ug = split_cols(proj, IN_SPLITS)
        y_a = gdn_mixer(qkv, z, a_g, b_g, gdn_conv[l], gdn_a_log[l], gdn_dt_bias[l], gdn_norm[l])
        y_b = dsa_mixer(c_q, c_kv, k_idx, w_idx, dsa_w_qb[l], dsa_w_qi[l], dsa_w_kvb[l],
                        dsa_q_norm[l], dsa_k_norm[l])
        y_c = conv_mixer(ug, conv_dw[l], conv_dw_b[l], conv_ln_g[l], conv_ln_b[l])
        x = x + jnp.concatenate([y_a, y_b, y_c], axis=-1) @ w_out[l]
        x = x + memory_cross_attention(rms_norm(x, norm_cross[l]), mem_n, xa_wq[l], xa_wkv[l],
                                       xa_q_norm[l], xa_k_norm[l], xa_wo[l])
        hm = rms_norm(x, norm_mlp[l]) @ mlp_w1[l]
        x = x + jnp.square(jax.nn.relu(hm)) @ mlp_w2[l]
    return x


CHUNK = 64
CONV_WIDTH_2 = D_MODEL
CONV_GROUPS = 16
CONV_K = 3
LRU_WIDTH = D_MODEL
LRU_HEADS = 16
LRU_HEAD_DIM = LRU_WIDTH // LRU_HEADS
LRU_CONV_K = 4
LRU_C = 8.0
D_FF_2 = ((-(-8 * D_MODEL // 3)) + 255) // 256 * 256
RMS_EPS = 1e-6
IN_WIDTHS = (CONV_WIDTH_2, CONV_WIDTH_2, CONV_WIDTH_2, LRU_WIDTH, LRU_WIDTH, D_MODEL, D_MODEL)
IN_TOTAL = sum(IN_WIDTHS)
SPLIT_POINTS = tuple(int(v) for v in np.cumsum(IN_WIDTHS)[:-1])


def rmsnorm(x, g):
    xf = x.astype(jnp.float32)
    var = jnp.mean(xf * xf, axis=-1, keepdims=True)
    return (xf * lax.rsqrt(var + RMS_EPS) * g.astype(jnp.float32)).astype(x.dtype)

def causal_depthwise_conv_2(x, w, b=None):
    K = w.shape[0]
    S = x.shape[1]
    xp = jnp.pad(x, ((0, 0), (K - 1, 0), (0, 0)))
    y = xp[:, 0:S] * w[0]
    for k in range(1, K):
        y = y + xp[:, k:k + S] * w[k]
    if b is not None:
        y = y + b
    return y

def rg_lru(x, w_a, b_a, w_x, b_x, lam):
    Bsz, S, W = x.shape
    f32 = jnp.float32
    xf = x.astype(f32)
    xh = xf.reshape(Bsz, S, LRU_HEADS, LRU_HEAD_DIM)
    r = jax.nn.sigmoid(jnp.einsum('bshd,hde->bshe', xh, w_a.astype(f32)).reshape(Bsz, S, W) + b_a.astype(f32))
    i = jax.nn.sigmoid(jnp.einsum('bshd,hde->bshe', xh, w_x.astype(f32)).reshape(Bsz, S, W) + b_x.astype(f32))
    log_a = -LRU_C * r * jax.nn.softplus(-lam.astype(f32))
    a = jnp.exp(log_a)
    b = jnp.sqrt(-jnp.expm1(2.0 * log_a)) * (i * xf)
    n_chunks = S // CHUNK
    a_c = a.reshape(Bsz, n_chunks, CHUNK, W)
    b_c = b.reshape(Bsz, n_chunks, CHUNK, W)

    def combine(left, right):
        a_l, b_l = left
        a_r, b_r = right
        return a_l * a_r, a_r * b_l + b_r

    a_cum, h_loc = lax.associative_scan(combine, (a_c, b_c), axis=2)

    def step(h_prev, inp):
        a_cum_k, h_loc_k = inp
        h = h_loc_k + a_cum_k * h_prev[:, None, :]
        return h[:, -1], h

    h0 = jnp.zeros((Bsz, W), f32)
    _, hs = lax.scan(step, h0, (jnp.moveaxis(a_cum, 1, 0), jnp.moveaxis(h_loc, 1, 0)))
    return jnp.moveaxis(hs, 0, 1).reshape(Bsz, S, W).astype(x.dtype)

def second_inputs(seed: int = 0) -> dict:
    key = jax.random.key(seed)
    ks = jax.random.split(key, 24)
    f32 = jnp.float32
    nrm = lambda k, shape, fan_in: jax.random.normal(k, shape, f32) * (fan_in ** -0.5)
    x = jax.random.normal(ks[0], (BATCH, SEQ, D_MODEL), f32)
    ln1_g = 1.0 + 0.02 * jax.random.normal(ks[1], (DEPTH, D_MODEL), f32)
    w_in = nrm(ks[2], (DEPTH, D_MODEL, IN_TOTAL), D_MODEL)
    conv_a_w = nrm(ks[3], (DEPTH, CONV_K, CONV_WIDTH_2), CONV_K)
    conv_b_w = nrm(ks[4], (DEPTH, LRU_CONV_K, LRU_WIDTH), LRU_CONV_K)
    conv_b_b = 0.02 * jax.random.normal(ks[5], (DEPTH, LRU_WIDTH), f32)
    lru_wa = nrm(ks[6], (DEPTH, LRU_HEADS, LRU_HEAD_DIM, LRU_HEAD_DIM), LRU_HEAD_DIM)
    lru_ba = 0.02 * jax.random.normal(ks[7], (DEPTH, LRU_WIDTH), f32)
    lru_wx = nrm(ks[8], (DEPTH, LRU_HEADS, LRU_HEAD_DIM, LRU_HEAD_DIM), LRU_HEAD_DIM)
    lru_bx = 0.02 * jax.random.normal(ks[9], (DEPTH, LRU_WIDTH), f32)
    u = jax.random.uniform(ks[10], (DEPTH, LRU_WIDTH), f32, 0.9, 0.999)
    s = u ** (1.0 / LRU_C)
    lru_lambda = jnp.log(s) - jnp.log1p(-s)
    w_out_a = nrm(ks[11], (DEPTH, CONV_WIDTH_2, D_MODEL), CONV_WIDTH_2)
    w_out_b = nrm(ks[12], (DEPTH, LRU_WIDTH, D_MODEL), LRU_WIDTH)
    gate_bias = 0.02 * jax.random.normal(ks[13], (DEPTH, 2, D_MODEL), f32)
    w_o = nrm(ks[14], (DEPTH, D_MODEL, D_MODEL), D_MODEL)
    ln2_g = 1.0 + 0.02 * jax.random.normal(ks[15], (DEPTH, D_MODEL), f32)
    w_ffn_gate = nrm(ks[16], (DEPTH, D_MODEL, D_FF_2), D_MODEL)
    w_ffn_up = nrm(ks[17], (DEPTH, D_MODEL, D_FF_2), D_MODEL)
    w_ffn_down = nrm(ks[18], (DEPTH, D_FF_2, D_MODEL), D_FF_2)
    final_g = 1.0 + 0.02 * jax.random.normal(ks[19], (D_MODEL,), f32)
    return {"x": x, "ln1_g": ln1_g, "w_in": w_in, "conv_a_w": conv_a_w,
            "conv_b_w": conv_b_w, "conv_b_b": conv_b_b, "lru_wa": lru_wa,
            "lru_ba": lru_ba, "lru_wx": lru_wx, "lru_bx": lru_bx,
            "lru_lambda": lru_lambda, "w_out_a": w_out_a, "w_out_b": w_out_b,
            "gate_bias": gate_bias, "w_o": w_o, "ln2_g": ln2_g,
            "w_ffn_gate": w_ffn_gate, "w_ffn_up": w_ffn_up,
            "w_ffn_down": w_ffn_down, "final_g": final_g}

def second_block(x, ln1_g, w_in, conv_a_w, conv_b_w, conv_b_b, lru_wa, lru_ba,
              lru_wx, lru_bx, lru_lambda, w_out_a, w_out_b, gate_bias, w_o,
              ln2_g, w_ffn_gate, w_ffn_up, w_ffn_down, final_g):
    for l in range(DEPTH):
        h = rmsnorm(x, ln1_g[l])
        proj = h @ w_in[l]
        b_a, c_a, x_a, x_b, g_b, gate_a_logit, gate_b_logit = jnp.split(proj, SPLIT_POINTS, axis=-1)
        y_a = b_a * causal_depthwise_conv_2(c_a * x_a, conv_a_w[l])
        u_b = causal_depthwise_conv_2(x_b, conv_b_w[l], conv_b_b[l])
        y_b = rg_lru(u_b, lru_wa[l], lru_ba[l], lru_wx[l], lru_bx[l], lru_lambda[l])
        y_b = y_b * jax.nn.gelu(g_b)
        merged = (jax.nn.sigmoid(gate_a_logit + gate_bias[l, 0]) * (y_a @ w_out_a[l])
                  + jax.nn.sigmoid(gate_b_logit + gate_bias[l, 1]) * (y_b @ w_out_b[l]))
        x = x + merged @ w_o[l]
        h = rmsnorm(x, ln2_g[l])
        x = x + (jax.nn.silu(h @ w_ffn_gate[l]) * (h @ w_ffn_up[l])) @ w_ffn_down[l]
    return rmsnorm(x, final_g)


def setup_inputs(seed=0):
    out = dict(first_inputs(seed))
    for name, value in second_inputs(seed + 1).items():
        if name != "x":
            out[name + "_2"] = value
    return out


def reference(
    x, mem, norm_mix, w_in, gdn_conv, gdn_a_log, gdn_dt_bias, gdn_norm, dsa_w_qb, dsa_w_qi,
    dsa_w_kvb, dsa_q_norm, dsa_k_norm, conv_dw, conv_dw_b, conv_ln_g, conv_ln_b, w_out,
    norm_mem, norm_cross, xa_wq, xa_wkv, xa_q_norm, xa_k_norm, xa_wo, norm_mlp, mlp_w1, mlp_w2,
    ln1_g_2, w_in_2, conv_a_w_2, conv_b_w_2, conv_b_b_2, lru_wa_2, lru_ba_2, lru_wx_2, lru_bx_2,
    lru_lambda_2, w_out_a_2, w_out_b_2, gate_bias_2, w_o_2, ln2_g_2, w_ffn_gate_2, w_ffn_up_2,
    w_ffn_down_2, final_g_2,
):
    x = first_block(
        x, mem, norm_mix, w_in, gdn_conv, gdn_a_log, gdn_dt_bias, gdn_norm, dsa_w_qb, dsa_w_qi,
        dsa_w_kvb, dsa_q_norm, dsa_k_norm, conv_dw, conv_dw_b, conv_ln_g, conv_ln_b, w_out,
        norm_mem, norm_cross, xa_wq, xa_wkv, xa_q_norm, xa_k_norm, xa_wo, norm_mlp, mlp_w1,
        mlp_w2,
    )
    return second_block(
        x, ln1_g_2, w_in_2, conv_a_w_2, conv_b_w_2, conv_b_b_2, lru_wa_2, lru_ba_2, lru_wx_2,
        lru_bx_2, lru_lambda_2, w_out_a_2, w_out_b_2, gate_bias_2, w_o_2, ln2_g_2, w_ffn_gate_2,
        w_ffn_up_2, w_ffn_down_2, final_g_2,
    )


_drawn_inputs = setup_inputs


def setup_inputs(seed=0):
    import zlib

    import numpy as np

    out = dict(_drawn_inputs(seed))
    spreads = {}
    factors = {'norm_mix': 2.742,
     'gdn_norm': 5.854,
     'dsa_q_norm': 8.0,
     'dsa_k_norm': 8.0,
     'conv_dw_b': 3.782,
     'conv_ln_g': 7.198,
     'conv_ln_b': 6.812,
     'norm_mem': 8.0,
     'norm_cross': 8.0,
     'xa_q_norm': 8.0,
     'xa_k_norm': 8.0,
     'norm_mlp': 2.82,
     'ln1_g_2': 3.825,
     'conv_b_b_2': 12.574,
     'lru_ba_2': 64.0,
     'lru_bx_2': 49.001,
     'gate_bias_2': 8.0,
     'ln2_g_2': 21.993}
    for name, (base, spread) in spreads.items():
        noise = np.random.default_rng([zlib.crc32(name.encode()), seed]).standard_normal(out[name].shape)
        drawn = base * np.exp(spread * noise) if base else spread * noise
        out[name] = __import__('jax').numpy.asarray(drawn.astype(out[name].dtype))
    for name, factor in factors.items():
        out[name] = (out[name] * factor).astype(out[name].dtype)
    return out
```

```python
from contextlib import ExitStack

import concourse.bass as bass
from concourse import mybir

P = 128
T = 512
D = 1024
KT = D // P
MEM = 256
TT = T // P
HEADS = 4
EPS = 1e-6
BLK = 8
PANEL = BLK * P
RAW = 4
SPLIT = 2
LEVELS = 7
TOPK = 128
MASKED = -3.0e38
TAKEN = -3.3e38
MT1, MTH = 24, 16
FFN = 22
DOWN_CUTS = (0, 6, 12, 17, 22)
CONV_TAPS = 31

F32 = mybir.dt.float32
F32R = mybir.dt.float32r
ACT = mybir.ActivationFunctionType
ALU = mybir.AluOpType
AX = mybir.AxisListType

VEC_WIDTHS = [
    ("norm_mix", 8), ("norm_mem", 8), ("norm_cross", 8), ("norm_mlp", 8), ("ln1", 8), ("ln2", 8), ("final", 8),
    ("gdn_conv", 48), ("gdn_norm", 1), ("dsa_q", 1), ("dsa_k", 1), ("dw", 2 * CONV_TAPS), ("dw_b", 2),
    ("cln_g", 2), ("cln_b", 2), ("xa_q", 1), ("xa_k", 1), ("conv_a", 24), ("conv_b", 32), ("conv_bb", 8),
    ("lru_ba", 8), ("lru_bx", 8), ("lam", 8), ("gate_b", 16), ("a_log", 16), ("dt_bias", 16),
]
VEC = {}
_at = 0
for _n, _w in VEC_WIDTHS:
    VEC[_n] = (_at, _w)
    _at += _w
NVEC = _at
C_ID, C_ONE, C_BLK, C_TRI, C_LEV = 0, P, 2 * P, 3 * P, 4 * P
C_CAUS = C_LEV + LEVELS * P
NCONST = C_CAUS + T


TOK_A, TOK_W, TOK_G, TOK_BETA, TOK_DEC, TOK_LAST = 0, 48, 64, 80, 96, 112
TOK_EDEC, TOK_EKD, TOK_ELAST, TOK_SP = 128, 144, 160, 176
TOK_N8, TOK_P8, TOK_RTOK, TOK_MX, TOK_NM, TOK_SUM, TOK_R, TOK_EA, TOK_M8 = 296, 304, 312, 320, 328, 336, 344, 352, 368
NTOK = 376


NORM_DQ, NORM_G, NORM_GO, NORM_AQ = 1, 4, 12, 16


class Count:

    def __init__(self, start=0):
        self.base, self.i, self.per, self.n = start, None, 0, 0

    def enter(self, i, per):
        self.base += self.n
        self.i, self.per, self.n = i, per, 0

    def leave(self, times):
        assert self.n == self.per, (self.n, self.per)
        self.base += times * self.per
        self.i, self.n = None, 0

    def at(self, k=0):
        v = self.base + self.n + k
        return v if self.i is None else self.i * self.per + v

    def step(self, k=1):
        self.n += k
        return self.at()


class Chain:

    def __init__(self, engine, sem):
        self.e, self.sem, self.c = engine, sem, Count()

    def __call__(self, ins):
        ins.then_inc(self.sem, 1)
        self.e.wait_ge(self.sem, self.c.step())
        return ins


class Plan:
    pass


def plan_memory(nc, ctx):
    k = Plan()

    top = [0]

    def sb(name, cols, dt=F32, at=None):
        cols = -(-cols // 8) * 8
        if at is None:
            at = top[0]
            top[0] += cols * 4
        return nc.alloc_sbuf_tensor_at(name, [P, cols], dt, offset=at), at + cols * 4

    base = (nc.sbuf_base + 63) // 64 * 64
    top[0] = base
    k.raw, _ = sb("raw", RAW * PANEL)
    k.w_hi, _ = sb("w_hi", SPLIT * PANEL, F32R)
    k.w_lo, _ = sb("w_lo", SPLIT * PANEL, F32R)
    k.x, _ = sb("x", KT * T)
    k.const, _ = sb("const", NCONST)
    k.vec, _ = sb("vec", NVEC)
    k.eps, _ = sb("eps", 4)
    k.rstd, _ = sb("rstd", T)
    k.sqacc, _ = sb("sqacc", T)
    k.sq, _ = sb("sq", 2 * T)
    k.tok, _ = sb("tok", NTOK)
    h0 = top[0]
    k.h_hi, _ = sb("h_hi", KT * T, F32R)
    k.h_lo, _ = sb("h_lo", KT * T, F32R)
    r0 = top[0]
    k.limit = nc.sbuf_usable_end
    k.proj, a = sb("proj", MT1 * T, at=r0)
    proj_end = a
    k.xk, a = sb("xk", HEADS * MEM, at=a)
    k.xv, a = sb("xv", 2 * T, at=a)
    q0 = a
    k.qkv, a = sb("qkv", 12 * T, at=q0)
    y0 = a
    k.mem, b = sb("mem", KT * MEM, at=q0)
    k.m_hi, b = sb("m_hi", KT * MEM, F32R, at=b)
    k.m_lo, b = sb("m_lo", KT * MEM, F32R, at=b)
    k.m_rstd, b = sb("m_rstd", MEM, at=b)
    k.m_sqa, _ = sb("m_sqa", MEM, at=b)
    k.y_hi, a = sb("y_hi", KT * T, F32R, at=y0)
    k.y_lo, a = sb("y_lo", KT * T, F32R, at=a)
    k.small_w, a = sb("small_w", 2 * 512 + P + 64, at=a)
    assert a <= k.limit, (a, k.limit)
    k.d_q, b = sb("d_q", 2 * T, at=h0)
    k.d_qi, b = sb("d_qi", 2 * T, at=b)
    k.d_k, b = sb("d_k", T, at=b)
    k.d_ki, b = sb("d_ki", T, at=b)
    k.d_v, b = sb("d_v", 2 * T, at=b)
    k.d_score, b = sb("d_score", T, at=b)
    k.d_relu, b = sb("d_relu", 2 * T, at=b)
    k.d_bias, b = sb("d_bias", T, at=b)
    k.d_p, b = sb("d_p", 2 * T, at=b)
    k.d_pt, b = sb("d_pt", 2 * T, at=b)
    assert b <= r0, (b, r0)
    k.c_y, b = sb("c_y", 2 * T, at=h0)
    k.c_acc, b = sb("c_acc", 2 * T, at=b)
    k.c_r, b = sb("c_r", T, at=b)
    k.c_t, b = sb("c_t", 2 * T, at=b)
    assert b <= r0
    k.g_ek, b = sb("g_ek", HEADS * T, at=h0)
    k.g_kdec, b = sb("g_kdec", HEADS * T, at=b)
    k.g_v, b = sb("g_v", HEADS * T, at=b)
    k.g_at, b = sb("g_at", HEADS * T, at=b)
    assert b <= r0
    k.g_qk, b = sb("g_qk", HEADS * T, at=r0)
    k.g_x, b = sb("g_x", HEADS * T, at=b)
    k.g_xt, b = sb("g_xt", HEADS * T, at=b)
    k.g_b, _ = sb("g_b", 2 * T, at=y0)
    k.g_p, _ = sb("g_p", 2 * T, at=y0 + 2 * T * 4)
    k.g_vn, _ = sb("g_vn", 4 * P, at=y0 + KT * T * 4)
    k.g_s, _ = sb("g_s", 4 * P, at=y0 + KT * T * 4 + 4 * P * 4)
    k.g_d, _ = sb("g_d", T, at=y0 + KT * T * 4 + 8 * P * 4)
    k.g_r, _ = sb("g_r", T, at=y0 + KT * T * 4 + 12 * P * 4)
    k.a_q, b = sb("a_q", HEADS * T, at=r0)
    k.a_p, b = sb("a_p", 2 * T, at=b)
    k.a_pt, b = sb("a_pt", 2 * T, at=b)
    assert b <= proj_end
    k.ao_hi, b = sb("ao_hi", HEADS * T, F32R, at=q0)
    k.ao_lo, b = sb("ao_lo", HEADS * T, F32R, at=b)
    k.u_hi, b = sb("u_hi", MTH * T, F32R, at=r0)
    k.u_lo, b = sb("u_lo", MTH * T, F32R, at=b)
    k.u_t, b = sb("u_t", 4 * T, at=b)
    assert b <= k.limit
    k.ya_hi, b = sb("ya_hi", KT * T, F32R, at=r0)
    k.ya_lo, b = sb("ya_lo", KT * T, F32R, at=b)
    k.yb_hi, b = sb("yb_hi", KT * T, F32R, at=b)
    k.yb_lo, b = sb("yb_lo", KT * T, F32R, at=b)
    k.mg_hi, _ = sb("mg_hi", KT * T, F32R, at=b)
    k.mg_lo, _ = sb("mg_lo", KT * T, F32R, at=b + KT * T * 4)
    k.gates, b = sb("gates", 2 * KT * T, at=b)
    k.ub_hi, b = sb("ub_hi", T, F32R, at=b)
    k.ub_lo, b = sb("ub_lo", T, F32R, at=b)
    k.s_t, b = sb("s_t", 9 * T, at=b)
    assert b <= k.limit, (b, k.limit)
    k.f_hi, b = sb("f_hi", FFN * T, F32R, at=r0)
    k.f_lo, b = sb("f_lo", FFN * T, F32R, at=b)
    k.f_t, b = sb("f_t", 4 * T, at=b)
    assert b <= k.limit, (b, k.limit)
    k.ps = [ctx.enter_context(nc.psum_tensor(f"acc{i}", [P, T], F32)) for i in range(8)]
    return k


def signals(nc, ctx, k):

    def sem(name):
        return ctx.enter_context(nc.semaphore(name))

    k.s_ld_x = sem("ld_x")
    k.s_ld_mem = sem("ld_mem")
    k.s_ld_const = sem("ld_const")
    k.s_ld_vec = sem("ld_vec")
    k.s_ld_small = sem("ld_small")
    k.s_split_done = sem("split_done")
    k.s_weights_hi = sem("weights_hi")
    k.s_panel_used = sem("panel_used")
    k.s_fed_hi = sem("fed_hi")
    k.s_fed_sq = sem("fed_sq")
    k.s_fed_lo = sem("fed_lo")
    k.s_sq_used = sem("sq_used")
    k.s_ssq = sem("ssq")
    k.s_std = sem("std")
    k.s_rstd = sem("rstd")
    k.s_x_new = sem("x_new")
    k.s_zeroed = sem("zeroed")
    k.s_act_chain = sem("act_chain")
    k.s_dve_chain = sem("dve_chain")
    k.s_xk_raw = sem("xk_raw")
    k.s_tokr_t = sem("tokr_t")
    k.s_v_done = sem("v_done")
    k.s_xk_done = sem("xk_done")
    k.s_unit_sq = sem("unit_sq")
    k.s_unit_sum = sem("unit_sum")
    k.s_unit_std = sem("unit_std")
    k.s_proj_done = sem("proj_done")
    k.s_ki_dup = sem("ki_dup")
    k.s_dq_mm = sem("dq_mm")
    k.s_dq_raw = sem("dq_raw")
    k.s_d_gates = sem("d_gates")
    k.s_d_gates_tok = sem("d_gates_tok")
    k.s_dq_done = sem("dq_done")
    k.s_idx_mm = sem("idx_mm")
    k.s_idx_relu = sem("idx_relu")
    k.s_idx_used = sem("idx_used")
    k.s_lg_mm = sem("lg_mm")
    k.s_lg_masked = sem("lg_masked")
    k.s_p_exp = sem("p_exp")
    k.s_p_norm = sem("p_norm")
    k.s_pt_mm = sem("pt_mm")
    k.s_pt_copied = sem("pt_copied")
    k.s_o_mm = sem("o_mm")
    k.s_y_hi = sem("y_hi")
    k.s_y_lo = sem("y_lo")
    k.s_c_sig = sem("c_sig")
    k.s_c_conv = sem("c_conv")
    k.s_c_mean = sem("c_mean")
    k.s_c_cent = sem("c_cent")
    k.s_c_sq = sem("c_sq")
    k.s_c_var = sem("c_var")
    k.s_c_std = sem("c_std")
    k.s_c_norm = sem("c_norm")
    k.s_c_silu = sem("c_silu")
    k.s_g_conv = sem("g_conv")
    k.s_g_silu = sem("g_silu")
    k.s_g_qk_done = sem("g_qk_done")
    k.s_sp_in = sem("sp_in")
    k.s_sp_exp = sem("sp_exp")
    k.s_beta_done = sem("beta_done")
    k.s_g_ready = sem("g_ready")
    k.s_dec_mm = sem("dec_mm")
    k.s_dec_copied = sem("dec_copied")
    k.s_dec_exp = sem("dec_exp")
    k.s_gb_done = sem("gb_done")
    k.s_decrow = sem("decrow")
    k.s_gam_d = sem("gam_d")
    k.s_gam_e = sem("gam_e")
    k.s_edecrow = sem("edecrow")
    k.s_gam_done = sem("gam_done")
    k.s_qk_mm = sem("qk_mm")
    k.s_qk_done = sem("qk_done")
    k.s_kk_mm = sem("kk_mm")
    k.s_at_done = sem("at_done")
    k.s_kt_mm = sem("kt_mm")
    k.s_ek_done = sem("ek_done")
    k.s_vt_mm = sem("vt_mm")
    k.s_v_tok_done = sem("v_tok_done")
    k.s_x_init = sem("x_init")
    k.s_bt_done = sem("bt_done")
    k.s_p_mm = sem("p_mm")
    k.s_p_copied = sem("p_copied")
    k.s_xp_mm = sem("xp_mm")
    k.s_x_done = sem("x_done")
    k.s_wt_mm = sem("wt_mm")
    k.s_wt_done = sem("wt_done")
    k.s_vn_mm = sem("vn_mm")
    k.s_vn_done = sem("vn_done")
    k.s_o_part = sem("o_part")
    k.s_st_mm = sem("st_mm")
    k.s_st_done = sem("st_done")
    k.s_o_copied = sem("o_copied")
    k.s_go_norm = sem("go_norm")
    k.s_z_silu = sem("z_silu")
    k.s_aq_raw = sem("aq_raw")
    k.s_aq_done = sem("aq_done")
    k.s_al_mm = sem("al_mm")
    k.s_al_max = sem("al_max")
    k.s_al_exp = sem("al_exp")
    k.s_al_norm = sem("al_norm")
    k.s_apt_mm = sem("apt_mm")
    k.s_apt_copied = sem("apt_copied")
    k.s_av_mm = sem("av_mm")
    k.s_ao_hi_done = sem("ao_hi_done")
    k.s_ao_lo_done = sem("ao_lo_done")
    k.s_up_relu = sem("up_relu")
    k.s_up_sq = sem("up_sq")
    k.s_up_hi = sem("up_hi")
    k.s_up_lo = sem("up_lo")
    k.s_s2_u = sem("s2_u")
    k.s_s2_uhi = sem("s2_uhi")
    k.s_s2_ulo = sem("s2_ulo")
    k.s_s2_gl = sem("s2_gl")
    k.s_s2_gsq = sem("s2_gsq")
    k.s_s2_gt = sem("s2_gt")
    k.s_s2_gsig = sem("s2_gsig")
    k.s_s2_gate = sem("s2_gate")
    k.s_s2_gate_done = sem("s2_gate_done")
    k.s_s2_r = sem("s2_r")
    k.s_s2_i = sem("s2_i")
    k.s_s2_a = sem("s2_a")
    k.s_s2_th = sem("s2_th")
    k.s_s2_a2 = sem("s2_a2")
    k.s_s2_m = sem("s2_m")
    k.s_s2_s = sem("s2_s")
    k.s_s2_yb = sem("s2_yb")
    k.s_s2_yb_hi = sem("s2_yb_hi")
    k.s_s2_ya = sem("s2_ya")
    k.s_s2_ya_hi = sem("s2_ya_hi")
    k.s_s2_free = sem("s2_free")
    k.s_mg = sem("mg")
    k.s_mg_hi = sem("mg_hi")
    k.s_mg_lo = sem("mg_lo")
    k.s_f_g = sem("f_g")
    k.s_f_silu = sem("f_silu")
    k.s_f_hid = sem("f_hid")
    k.s_f_hi_done = sem("f_hi_done")
    k.s_f_lo_done = sem("f_lo_done")
    k.s_out_ready = sem("out_ready")
    k.s_out_sent = sem("out_sent")
    k.landed = [sem(f"landed{j}") for j in range(RAW)]
    k.acc_free = [sem(f"acc_free{b}") for b in range(8)]


STREAM = [("panels_a", 28, [PANEL] * 4),
          ("mix", 8, [PANEL] * 4 + [2 * P] + [PANEL] * 3),
          ("panels_b", 17, [PANEL] * 4),
          ("down", 8, [(b - a) * P for a, b in zip(DOWN_CUTS, DOWN_CUTS[1:])])]


class Panels(Count):

    def landed(self):
        v = 16 * (self.base // RAW) + 16 * (self.n // RAW) + 16
        return v if self.i is None else self.i * (16 * (self.per // RAW)) + v


def col(k, name, j=0, rows=slice(0, P)):
    at = VEC[name][0] + j
    return k.vec[rows, at:at + 1]


def til(buf, j, n=1, w=T):
    return buf[:, j * w:(j + n) * w]


def rtil(buf, j, w=T):
    return buf[:, bass.ds(j * w, w)]


def sync_program(nc, k, d):
    e = nc.sync
    e.dma_start(k.vec[:, 0:NVEC], d.vec).then_inc(k.s_ld_vec, 16)
    e.dma_start(k.mem[:].rearrange("p (k t) -> p k t", k=KT), d.mem.rearrange("(k p) t -> p k t", p=P)).then_inc(k.s_ld_mem, 16)
    e.dma_start(k.const[:], d.const).then_inc(k.s_ld_const, 16)
    pan = Panels()
    first = True
    for name, times, widths in STREAM:
        src = stream_array(d, name)
        with e.Fori(0, times) as i:
            pan.enter(i, len(widths))
            at = 0
            for j, w in enumerate(widths):
                e.wait_ge(k.s_split_done, pan.at(1))
                if name in ("panels_a", "panels_b"):
                    part = src[bass.ds(i * 4 + j, 1)].rearrange("a p n -> (a p) n")
                else:
                    part = src[bass.ds(i, 1)].rearrange("a p n -> (a p) n")[:, at:at + w]
                e.dma_start(k.raw[:, (j % RAW) * PANEL:(j % RAW) * PANEL + w], part).then_inc(k.landed[j % RAW], 16)
                at += w
                pan.step()
            pan.leave(times)


def stream_array(d, name):
    return {"panels_a": d.panels_a, "mix": d.mix, "panels_b": d.panels_b, "down": d.down}[name]


def gpsimd_program(nc, k):
    e = nc.gpsimd
    e.sem_inc(k.s_split_done, RAW)
    one = k.const[:, C_ONE:C_ONE + 1]
    e.wait_ge(k.s_ld_const, 16)
    pan = Panels()
    for name, times, widths in STREAM:
        with e.Fori(0, times) as i:
            pan.enter(i, len(widths))
            for j, w in enumerate(widths):
                raw = k.raw[:, (j % RAW) * PANEL:(j % RAW) * PANEL + w]
                hi = k.w_hi[:, (j % SPLIT) * PANEL:(j % SPLIT) * PANEL + w]
                lo = k.w_lo[:, (j % SPLIT) * PANEL:(j % SPLIT) * PANEL + w]
                e.wait_ge(k.landed[j % RAW], pan.landed())
                e.wait_ge(k.s_panel_used, pan.at(1))
                e.tensor_tensor(hi, raw, one.broadcast_to([P, w]), ALU.mult).then_inc(k.s_weights_hi, 1)
                e.wait_ge(k.s_weights_hi, pan.at(1))
                e.tensor_tensor(lo, raw, hi.bitcast(F32), ALU.subtract).then_inc(k.s_split_done, 1)
                pan.step()
            pan.leave(times)


class Acc:

    def __init__(self, k):
        self.k, self.c = k, [Count() for _ in range(8)]

    def enter(self, i, per):
        for c, n in zip(self.c, per):
            c.enter(i, n)

    def leave(self, times):
        for c in self.c:
            c.leave(times)

    def take(self, e, b):
        e.wait_ge(self.k.acc_free[b], self.c[b].step())
        return self.k.ps[b]


def tensor_program(nc, k):
    e = nc.tensor
    pan, acc = Panels(), Acc(k)
    e.sem_inc(k.s_panel_used, SPLIT)
    ident = k.const[:, C_ID:C_ID + P]
    ones = k.const[:, C_ONE:C_ONE + P]
    blk = k.const[:, C_BLK:C_BLK + P]
    tri = k.const[:, C_TRI:C_TRI + P]

    def products(out, w_at, wn, a_hi, a_lo, first, last):
        for n, (w, a) in enumerate(((k.w_hi, a_hi), (k.w_hi, a_lo), (k.w_lo, a_hi))):
            mm = e.matmul(out, w[:, w_at:w_at + wn], a, start=first and n == 0, stop=last and n == 2)
        return mm

    def panel(out, hi, lo, tiles, first=True, last=True, at=0, done=True, w=T):
        slot = (pan.n % SPLIT) * PANEL
        if at == 0:
            e.wait_ge(k.s_split_done, RAW + pan.at(1))
        for n, t in enumerate(tiles):
            mm = products(out, slot + (at + n) * P, P, hi[:, t * w:(t + 1) * w], lo[:, t * w:(t + 1) * w],
                          first and n == 0, last and n == len(tiles) - 1)
        if done:
            mm.then_inc(k.s_panel_used, 1)
            pan.step()

    def sum_squares(n_fed, n_norm, sqacc, w=T):
        e.wait_ge(k.s_sq_used, 2 + n_fed)
        if n_norm > 0:
            e.wait_ge(k.s_std, n_norm)
        e.matmul(k.ps[7][:, 0:w], ones, sqacc[:, 0:w], start=True, stop=True).then_inc(k.s_ssq, 1)

    e.wait_ge(k.s_ld_const, 16)
    sum_squares(KT, 0, k.m_sqa, MEM)
    e.wait_ge(k.s_fed_lo, KT)
    for m in range(HEADS):
        out = acc.take(e, m % 2)
        panel(out[:, 0:MEM], k.m_hi, k.m_lo, range(KT), w=MEM)
    for b in (2, 3):
        acc.take(e, b)
    for j in range(4):
        e.wait_ge(k.s_split_done, RAW + pan.at(1))
        slot = (pan.n % SPLIT) * PANEL
        for kk in range(2):
            t = 2 * j + kk
            for mt in range(2):
                a = t * MEM + mt * P
                for n, (m_, w) in enumerate(((k.m_hi, k.w_hi), (k.m_hi, k.w_lo), (k.m_lo, k.w_hi))):
                    mm = e.matmul(k.ps[2 + mt][:], m_[:, a:a + P], w[:, slot + kk * T:slot + (kk + 1) * T],
                                  start=t == 0 and n == 0, stop=t == KT - 1 and n == 2)
        mm.then_inc(k.s_panel_used, 1)
        pan.step()
    e.wait_ge(k.s_rstd, 1)
    for mt in range(2):
        mm = e.transpose(k.ps[4][:, mt * P:(mt + 1) * P], k.m_rstd[:, mt * P:(mt + 1) * P], ident)
    mm.then_inc(k.s_tokr_t, 1)
    e.wait_ge(k.s_unit_sq, 1)
    for j in range(2):
        mm = e.matmul(k.ps[5 + j][:], ones, k.mem[:, j * T:(j + 1) * T], start=True, stop=True)
    mm.then_inc(k.s_unit_sum, 1)

    sum_squares(2 * KT, 1, k.sqacc)
    e.wait_ge(k.s_fed_lo, 2 * KT)
    with e.Fori(0, 6) as i:
        pan.enter(i, 4)
        acc.enter(i, [1, 1, 1, 1, 0, 0, 0, 0])
        for j in range(4):
            panel(acc.take(e, j)[:], k.h_hi, k.h_lo, range(KT))
        pan.leave(6)
        acc.leave(6)

    e.wait_ge(k.s_proj_done, 1)
    e.wait_ge(k.s_ld_small, 16)
    for m in range(4):
        for kk in range(2):
            w_at = (0 if m < 2 else 512) + kk * 256 + (m % 2) * P
            mm = e.matmul(k.ps[m][:], k.small_w[:, w_at:w_at + P], til(k.proj, 20 + kk), start=kk == 0, stop=kk == 1)
        mm.then_inc(k.s_dq_mm, 1)
    e.wait_ge(k.s_v_done, 2)
    e.matmul(k.ps[4][:], k.small_w[:, 1024:1152], til(k.proj, 22), start=True, stop=True).then_inc(k.s_dq_mm, 1)
    e.wait_ge(k.s_unit_std, 1)
    for t in range(TT):
        mm = e.matmul(k.ps[5][:, t * 64:(t + 1) * 64], k.proj[:, 22 * T + t * P:22 * T + (t + 1) * P],
                      k.small_w[:, 1152:1216], start=True, stop=True)
    mm.then_inc(k.s_dq_mm, 1)
    for c in range(TT):
        mm = e.transpose(k.ps[6][:, c * P:(c + 1) * P], k.proj[:, 23 * T + c * P:23 * T + (c + 1) * P], ident)
    mm.then_inc(k.s_d_gates, 1)
    for m in range(3):
        e.wait_ge(k.s_unit_sq, NORM_DQ + m + 1)
        e.wait_ge(k.s_dq_raw, (1, 2, 5)[m])
        src = til(k.d_relu, m) if m < 2 else til(k.d_p, 0)
        e.matmul(k.ps[(0, 1, 4)[m]][:], blk, src, start=True, stop=True).then_inc(k.s_unit_sum, 1)

    e.wait_ge(k.s_ki_dup, 32)
    e.wait_ge(k.s_dq_raw, 6)
    e.wait_ge(k.s_unit_std, NORM_DQ + 3)
    e.wait_ge(k.s_dq_done, 3)
    for qt in range(TT):
        cw = (qt + 1) * P
        if qt:
            for h in range(HEADS):
                if qt > 1:
                    e.wait_ge(k.s_idx_relu, HEADS * (qt - 2) + h + 1)
                if h < 2:
                    e.wait_ge(k.s_y_lo, 2 * (qt - 1) + h + 1)
                r = slice(64 * (h % 2), 64 * (h % 2) + 64)
                e.matmul(k.ps[h][:, 0:cw], k.d_qi[r, (h // 2) * T + qt * P:(h // 2) * T + (qt + 1) * P],
                         k.d_ki[r, 0:cw], start=True, stop=True).then_inc(k.s_idx_mm, 1)

        def logits(h):
            u = qt * HEADS + h
            if u >= 2:
                e.wait_ge(k.s_lg_masked, u - 1)
            r = slice(64 * (h % 2), 64 * (h % 2) + 64)
            e.matmul(k.ps[4 + h % 2][:, 0:cw], k.d_q[r, (h // 2) * T + qt * P:(h // 2) * T + (qt + 1) * P],
                     k.d_k[r, 0:cw], start=True, stop=True).then_inc(k.s_lg_mm, 1)

        def outputs(h):
            u = qt * HEADS + h
            e.wait_ge(k.s_p_norm, u + 1)
            if u >= 2:
                e.wait_ge(k.s_pt_copied, u - 1)
            if u == 0:
                e.wait_ge(k.s_d_gates_tok, 1)
            for t in range(qt + 1):
                mm = e.transpose(k.ps[6 + h % 2][:, t * P:(t + 1) * P],
                                 k.d_p[:, (h % 2) * T + t * P:(h % 2) * T + (t + 1) * P], ident)
            mm.then_inc(k.s_pt_mm, 1)
            e.wait_ge(k.s_pt_copied, u + 1)
            if qt and h % 2 == 0:
                e.wait_ge(k.s_idx_relu, HEADS * qt)
            for t in range(qt + 1):
                mm = e.matmul(k.ps[h // 2][:, 0:P], k.d_v[:, (2 * t + h % 2) * P:(2 * t + h % 2 + 1) * P],
                              k.d_pt[:, (h % 2) * T + t * P:(h % 2) * T + (t + 1) * P],
                              start=h % 2 == 0 and t == 0, stop=h % 2 == 1 and t == qt)
            if h % 2:
                mm.then_inc(k.s_o_mm, 1)

        logits(0)
        for h in range(HEADS):
            if h + 1 < HEADS:
                logits(h + 1)
            outputs(h)

    e.wait_ge(k.s_y_lo, 2 * TT)
    for bank, ready in ((0, k.s_c_conv), (1, k.s_c_sq)):
        for j in range(2):
            e.wait_ge(ready, j + 1)
            src = til(k.c_acc, j) if bank == 0 else til(k.c_t, j)
            mm = e.matmul(k.ps[bank][:], ones, src, start=j == 0, stop=j == 1)
        mm.then_inc(k.s_c_mean if bank == 0 else k.s_c_var, 1)

    e.wait_ge(k.s_c_std, 1)
    e.wait_ge(k.s_c_cent, 2)
    e.wait_ge(k.s_pt_copied, HEADS * TT)
    for m in range(2 * HEADS):
        e.wait_ge(k.s_unit_sq, NORM_G + m + 1)
        e.matmul(k.ps[m][:], ones, til(k.sq, m % 2), start=True, stop=True).then_inc(k.s_unit_sum, 1)
    e.wait_ge(k.s_unit_std, NORM_G + 2 * HEADS)
    e.wait_ge(k.s_g_ready, 1)
    e.matmul(k.ps[7][:, 0:16], tri, k.tok[:, TOK_G:TOK_G + 16], start=True, stop=True)
    e.matmul(k.ps[7][:, 16:32], ones, k.tok[:, TOK_G:TOK_G + 16], start=True, stop=True).then_inc(k.s_dec_mm, 1)
    for h in range(HEADS):
        e.wait_ge(k.s_gb_done, h + 1)
        for c in range(TT):
            at = h * T + c * P
            mm = e.matmul(k.ps[h][:, c * P:(c + 1) * P], k.g_x[:, at:at + P], tri, start=True, stop=True)
        mm.then_inc(k.s_decrow, 1)
    e.wait_ge(k.s_g_qk_done, 2 * HEADS)
    for h in range(HEADS):
        if h >= 1:
            e.wait_ge(k.s_qk_done, h)
        for c in range(TT):
            at = c * P
            mm = e.matmul(k.ps[4][:, at:at + P], til(k.qkv, 4 + h)[:, at:at + P], til(k.qkv, h)[:, at:at + P],
                          start=True, stop=True)
        mm.then_inc(k.s_qk_mm, 1)
        if h >= 1:
            e.wait_ge(k.s_at_done, h)
        for c in range(TT):
            at = c * P
            mm = e.matmul(k.ps[5][:, at:at + P], til(k.qkv, 4 + h)[:, at:at + P], til(k.qkv, 4 + h)[:, at:at + P],
                          start=True, stop=True)
        mm.then_inc(k.s_kk_mm, 1)
        if h >= 1:
            e.wait_ge(k.s_ek_done, h)
        for c in range(TT):
            mm = e.transpose(k.ps[6][:, c * P:(c + 1) * P], til(k.qkv, 4 + h)[:, c * P:(c + 1) * P], ident)
        mm.then_inc(k.s_kt_mm, 1)
        if h >= 1:
            e.wait_ge(k.s_v_tok_done, h)
        else:
            e.wait_ge(k.s_dec_copied, 1)
        for c in range(TT):
            mm = e.transpose(k.ps[7][:, c * P:(c + 1) * P], til(k.qkv, 8 + h)[:, c * P:(c + 1) * P], ident)
        mm.then_inc(k.s_vt_mm, 1)
    e.wait_ge(k.s_gam_done, 2 * HEADS)
    e.wait_ge(k.s_edecrow, HEADS)
    e.wait_ge(k.s_qk_done, HEADS)
    e.wait_ge(k.s_at_done, HEADS)
    e.wait_ge(k.s_x_init, 1)
    with e.Fori(0, LEVELS) as lev:
        for h in range(HEADS):
            u = lev * HEADS + h + 1
            e.wait_ge(k.s_bt_done, u)
            e.wait_ge(k.s_p_copied, u)
            e.wait_ge(k.s_x_done, u)
            b = (h % 2) * T
            for c in range(TT):
                at = c * P
                mm = e.matmul(k.ps[h % 2][:, at:at + P], k.g_b[:, b + at:b + at + P],
                              til(k.g_x, h)[:, at:at + P], start=True, stop=True)
            mm.then_inc(k.s_p_mm, 1)
            e.wait_ge(k.s_p_copied, u + 2)
            e.wait_ge(k.s_x_done, u + 2)
            for c in range(TT):
                at = c * P
                e.matmul(k.ps[2 + h % 2][:, at:at + P], til(k.g_xt, h)[:, at:at + P],
                         k.g_p[:, b + at:b + at + P], start=True, stop=True)
            for c in range(TT):
                at = c * P
                mm = e.matmul(k.ps[4 + h % 2][:, at:at + P], k.g_p[:, b + at:b + at + P],
                              til(k.g_xt, h)[:, at:at + P], start=True, stop=True)
            mm.then_inc(k.s_xp_mm, 1)
    U = LEVELS * HEADS
    e.wait_ge(k.s_x_done, HEADS + U)
    e.wait_ge(k.s_ek_done, HEADS)
    e.wait_ge(k.s_v_tok_done, HEADS)
    for h in range(HEADS):
        if h >= 2:
            e.wait_ge(k.s_wt_done, h - 1)
        for c in range(TT):
            at = h * T + c * P
            mm = e.matmul(k.ps[6 + h % 2][:, c * P:(c + 1) * P], k.g_ek[:, at:at + P], k.g_xt[:, at:at + P],
                          start=True, stop=True)
        mm.then_inc(k.s_wt_mm, 1)
    e.wait_ge(k.s_wt_done, HEADS)
    for c in range(TT):
        for h in range(HEADS):
            u = c * HEADS + h
            at = h * T + c * P
            e.wait_ge(k.s_st_done, HEADS + u - HEADS + 1)
            if c:
                e.wait_ge(k.s_vn_done, u - HEADS + 1)
            e.matmul(k.ps[h][:, 0:P], k.g_xt[:, at:at + P], k.g_v[:, at:at + P], start=True, stop=False)
            e.matmul(k.ps[h][:, 0:P], til(k.qkv, 4 + h)[:, c * P:(c + 1) * P], k.g_s[:, h * P:(h + 1) * P],
                     start=False, stop=True).then_inc(k.s_vn_mm, 1)
        for h in range(HEADS):
            u = c * HEADS + h
            at = h * T + c * P
            vn = k.g_vn[:, h * P:(h + 1) * P]
            e.wait_ge(k.s_vn_done, u + 1)
            if u >= 2:
                e.wait_ge(k.s_o_copied, u - 1)
            e.matmul(k.ps[4 + h % 2][:, 0:P], k.g_s[:, h * P:(h + 1) * P], til(k.qkv, h)[:, c * P:(c + 1) * P],
                     start=True, stop=False)
            e.matmul(k.ps[4 + h % 2][:, 0:P], vn, k.g_qk[:, at:at + P], start=False, stop=True).then_inc(k.s_o_part, 1)
            if u >= 2:
                e.wait_ge(k.s_st_done, HEADS + u - 1)
            e.matmul(k.ps[6 + h % 2][:, 0:P], k.g_kdec[:, at:at + P], vn, start=True, stop=True).then_inc(k.s_st_mm, 1)
    for h in range(HEADS):
        e.wait_ge(k.s_unit_sq, NORM_GO + h + 1)
        e.matmul(k.ps[h][:], ones, til(k.g_x, h), start=True, stop=True).then_inc(k.s_unit_sum, 1)

    e.wait_ge(k.s_y_lo, 2 * TT + 2 + HEADS)
    e.wait_ge(k.s_unit_std, NORM_GO + HEADS)
    e.wait_ge(k.s_y_lo, 2 * TT + 2)
    with e.Fori(0, 2) as i:
        pan.enter(i, 4)
        acc.enter(i, [2, 2, 0, 0, 0, 0, 0, 0])
        for j in range(4):
            panel(acc.take(e, j % 2)[:], k.y_hi, k.y_lo, range(KT))
        pan.leave(2)
        acc.leave(2)

    sum_squares(3 * KT, 2, k.sqacc)
    e.wait_ge(k.s_fed_lo, 3 * KT)
    for j in range(4):
        panel(acc.take(e, j)[:], k.h_hi, k.h_lo, range(KT))
    for h in range(HEADS):
        e.wait_ge(k.s_unit_sq, NORM_AQ + h + 1)
        e.matmul(k.ps[4 + h % 2][:], ones, til(k.sq, h % 2), start=True, stop=True).then_inc(k.s_unit_sum, 1)
        e.wait_ge(k.s_unit_std, NORM_AQ + h + 1)
    e.wait_ge(k.s_aq_done, HEADS)
    e.wait_ge(k.s_xk_done, 1)
    for h in range(HEADS):
        for half in range(2):
            u = 2 * h + half
            if u >= 2:
                e.wait_ge(k.s_al_exp, u - 1)
            for n in range(2):
                qt = 2 * half + n
                mm = e.matmul(k.ps[half][:, n * MEM:(n + 1) * MEM], til(k.a_q, h)[:, qt * P:(qt + 1) * P],
                              k.xk[:, h * MEM:(h + 1) * MEM], start=True, stop=True)
            mm.then_inc(k.s_al_mm, 1)
        e.wait_ge(k.s_al_norm, 2 * h + 2)
        if h:
            e.wait_ge(k.s_apt_copied, 2 * h)
        for mt in range(2):
            for qt in range(TT):
                at = qt * MEM + mt * P
                mm = e.transpose(k.ps[2 + mt][:, qt * P:(qt + 1) * P], k.a_p[:, at:at + P], ident)
            mm.then_inc(k.s_apt_mm, 1)
        if h >= 2:
            e.wait_ge(k.s_ao_lo_done, h - 1)
        for mt in range(2):
            e.wait_ge(k.s_apt_copied, 2 * h + mt + 1)
            mm = e.matmul(k.ps[4 + h % 2][:], k.xv[:, mt * T + h * P:mt * T + (h + 1) * P], til(k.a_pt, mt),
                          start=mt == 0, stop=mt == 1)
        mm.then_inc(k.s_av_mm, 1)
    e.wait_ge(k.s_ao_lo_done, HEADS)
    for j in range(4):
        for n in range(2):
            panel(acc.take(e, n)[:], k.ao_hi, k.ao_lo, range(HEADS), at=HEADS * n, done=n == 1)

    sum_squares(4 * KT, 3, k.sqacc)
    e.wait_ge(k.s_fed_lo, 4 * KT)
    for half in range(2):
        with e.Fori(0, MTH // 4) as i:
            pan.enter(i, 4)
            acc.enter(i, [2, 2, 0, 0, 0, 0, 0, 0])
            for j in range(4):
                panel(acc.take(e, j % 2)[:], k.h_hi, k.h_lo, range(KT))
            pan.leave(MTH // 4)
            acc.leave(MTH // 4)
        e.wait_ge(k.s_up_lo, MTH * (half + 1))
        with e.Fori(0, KT // 2) as i:
            pan.enter(i, 4)
            acc.enter(i, [1, 1, 0, 0, 0, 0, 0, 0])
            for j in range(2):
                out = acc.take(e, j)[:]
                panel(out, k.u_hi, k.u_lo, range(0, 8), last=False)
                panel(out, k.u_hi, k.u_lo, range(8, 16), first=False)
            pan.leave(KT // 2)
            acc.leave(KT // 2)

    sum_squares(5 * KT, 4, k.sqacc)
    e.wait_ge(k.s_fed_lo, 5 * KT)
    with e.Fori(0, KT) as i:
        pan.enter(i, 8)
        acc.enter(i, [2, 1, 1, 1, 1, 1, 1, 1])
        for b in (0, 1, 4, 5):
            panel(acc.take(e, b)[:], k.h_hi, k.h_lo, range(KT))
        e.wait_ge(k.s_s2_ulo, i + 1)
        panel(acc.take(e, 2)[:], k.ub_hi, k.ub_lo, range(1), done=False)
        panel(acc.take(e, 3)[:], k.ub_hi, k.ub_lo, range(1), at=1)
        for b in (6, 7, 0):
            panel(acc.take(e, b)[:], k.h_hi, k.h_lo, range(KT))
        pan.leave(KT)
        acc.leave(KT)

    e.wait_ge(k.s_s2_free, KT)
    with e.Fori(0, KT // 2) as i:
        pan.enter(i, 4)
        acc.enter(i, [1, 1, 1, 1, 0, 0, 0, 0])
        for j in range(2):
            panel(acc.take(e, 2 * j)[:], k.ya_hi, k.ya_lo, range(KT))
            panel(acc.take(e, 2 * j + 1)[:], k.yb_hi, k.yb_lo, range(KT))
        pan.leave(KT // 2)
        acc.leave(KT // 2)

    e.wait_ge(k.s_mg_lo, KT)
    with e.Fori(0, 2) as i:
        pan.enter(i, 4)
        acc.enter(i, [2, 2, 0, 0, 0, 0, 0, 0])
        for j in range(4):
            panel(acc.take(e, j % 2)[:], k.mg_hi, k.mg_lo, range(KT))
        pan.leave(2)
        acc.leave(2)

    sum_squares(6 * KT, 5, k.sqacc)
    e.wait_ge(k.s_fed_lo, 6 * KT)
    with e.Fori(0, FFN // 2) as i:
        pan.enter(i, 4)
        acc.enter(i, [1, 1, 1, 1, 0, 0, 0, 0])
        for j in range(4):
            panel(acc.take(e, j)[:], k.h_hi, k.h_lo, range(KT))
        pan.leave(FFN // 2)
        acc.leave(FFN // 2)
    e.wait_ge(k.s_f_lo_done, FFN)
    with e.Fori(0, KT // 2) as i:
        pan.enter(i, 8)
        acc.enter(i, [1, 1, 0, 0, 0, 0, 0, 0])
        for j in range(2):
            out = acc.take(e, j)[:]
            for a, b in zip(DOWN_CUTS, DOWN_CUTS[1:]):
                panel(out, k.f_hi, k.f_lo, range(a, b), first=a == 0, last=b == FFN)
        pan.leave(KT // 2)
        acc.leave(KT // 2)
    sum_squares(7 * KT, 6, k.sqacc)


def scalar_program(nc, k, d):
    e = nc.scalar
    A = e.activation
    chain = Chain(e, k.s_act_chain)
    e.dma_start(k.x[:].rearrange("p (k t) -> p k t", k=KT), d.x.rearrange("(k p) t -> p k t", p=P)).then_inc(k.s_ld_x, 16)
    e.dma_start(k.small_w[:], d.small_w).then_inc(k.s_ld_small, 16)
    fed = Count()

    def feed(src, gain, hi, w=T, split=True):
        e.wait_ge(k.s_sq_used, fed.at(1))
        if split:
            A(hi, src, ACT.Copy, scale=gain).then_inc(k.s_fed_hi, 1)
        A(k.sq[:, (fed.n % 2) * T:(fed.n % 2) * T + w], src, ACT.Square).then_inc(k.s_fed_sq, 1)
        fed.step()

    def root(n_norm, dst, w=T):
        e.wait_ge(k.s_ssq, n_norm)
        A(dst[:, 0:w], k.ps[7][:, 0:w], ACT.Sqrt, bias=k.eps[:, 0:1], scale=1.0 / D).then_inc(k.s_std, 1)

    e.wait_ge(k.s_ld_vec, 16)
    e.wait_ge(k.s_ld_mem, 16)
    for m in range(KT):
        feed(til(k.mem, m, w=MEM), col(k, "norm_mem", m), til(k.m_hi, m, w=MEM), MEM)
    e.wait_ge(k.s_zeroed, 1)
    root(1, k.m_rstd, MEM)
    e.wait_ge(k.s_ld_x, 16)
    for m in range(KT):
        feed(til(k.x, m), col(k, "norm_mix", m), til(k.h_hi, m))
    e.wait_ge(k.s_tokr_t, 1)
    for mt in range(2):
        ins = A(k.tok[:, TOK_RTOK + mt:TOK_RTOK + mt + 1], k.ps[4][:, mt * P:mt * P + 1], ACT.Copy)
    ins.then_inc(k.s_v_done, 1)
    e.wait_ge(k.s_xk_raw, 1)
    A(k.mem[:, 0:HEADS * MEM], k.xk[:], ACT.Square).then_inc(k.s_unit_sq, 1)
    root(2, k.rstd)
    e.wait_ge(k.s_unit_sum, 1)
    for j in range(2):
        ins = A(k.mem[:, HEADS * MEM + j * T:HEADS * MEM + (j + 1) * T], k.ps[5 + j][:], ACT.Sqrt,
                bias=k.eps[:, 0:1], scale=1.0 / P)
    ins.then_inc(k.s_unit_std, 1)

    e.wait_ge(k.s_proj_done, 1)
    for half in range(2):
        e.dma_start(k.d_ki[64 * half:64 * half + 64, :], k.proj[0:64, 23 * T:24 * T]).then_inc(k.s_ki_dup, 16)
    for n, (src, dst) in enumerate(((til(k.d_q, 0), til(k.d_relu, 0)), (til(k.d_q, 1), til(k.d_relu, 1)),
                                    (k.d_k[:], til(k.d_p, 0)))):
        e.wait_ge(k.s_dq_raw, (1, 2, 5)[n])
        A(dst, src, ACT.Square).then_inc(k.s_unit_sq, 1)
    e.wait_ge(k.s_d_gates, 1)
    A(k.tok[:, TOK_A:TOK_A + 48].rearrange("p (c w) -> p c w", c=TT),
      k.ps[6][:].rearrange("p (c w) -> p c w", c=TT)[:, :, 64:76], ACT.Copy).then_inc(k.s_d_gates_tok, 1)
    for n, (bank, dst) in enumerate(((0, til(k.d_relu, 0)), (1, til(k.d_relu, 1)), (4, til(k.d_p, 0)))):
        e.wait_ge(k.s_unit_sum, NORM_DQ + n + 1)
        A(dst, k.ps[bank][:], ACT.Sqrt, bias=k.eps[:, 0:1], scale=1.0 / 64).then_inc(k.s_unit_std, 1)
    e.wait_ge(k.s_dq_done, 3)
    for qt in range(TT):
        cw = (qt + 1) * P
        if qt:
            for h in range(HEADS):
                v = HEADS * (qt - 1) + h
                e.wait_ge(k.s_idx_mm, v + 1)
                if v >= 2:
                    e.wait_ge(k.s_idx_used, v - 1)
                A(k.d_relu[:, (h % 2) * T:(h % 2) * T + cw], k.ps[h][:, 0:cw], ACT.Relu).then_inc(k.s_idx_relu, 1)

        def exps(h):
            u = qt * HEADS + h
            p = k.d_p[:, (h % 2) * T:(h % 2) * T + cw]
            e.wait_ge(k.s_lg_masked, u + 1)
            A(p, p, ACT.Exp, bias=k.tok[:, TOK_NM + h % 2:TOK_NM + h % 2 + 1],
              accum_out=k.tok[:, TOK_SUM + h % 2:TOK_SUM + h % 2 + 1]).then_inc(k.s_p_exp, 1)

        exps(0)
        for h in range(HEADS):
            u = qt * HEADS + h
            if h + 1 < HEADS:
                exps(h + 1)
            e.wait_ge(k.s_pt_mm, u + 1)
            A(k.d_pt[:, (h % 2) * T:(h % 2) * T + cw], k.ps[6 + h % 2][:, 0:cw], ACT.Copy).then_inc(k.s_pt_copied, 1)
            if h % 2:
                j = h // 2
                at = (4 + j) * T + qt * P
                e.wait_ge(k.s_o_mm, 2 * qt + j + 1)
                A(k.y_hi[:, at:at + P], k.ps[j][:, 0:P], ACT.Copy).then_inc(k.s_y_hi, 1)

    e.wait_ge(k.s_y_lo, 2 * TT)
    A(k.c_y[:], til(k.proj, 18, 2), ACT.Sigmoid).then_inc(k.s_c_sig, 1)
    for j in range(2):
        e.wait_ge(k.s_c_cent, j + 1)
        A(til(k.c_t, j), til(k.c_acc, j), ACT.Square).then_inc(k.s_c_sq, 1)
    e.wait_ge(k.s_c_var, 1)
    A(k.c_r[:], k.ps[1][:], ACT.Sqrt, bias=k.eps[:, 0:1], scale=1.0 / 256).then_inc(k.s_c_std, 1)
    for j in range(2):
        e.wait_ge(k.s_c_norm, j + 1)
        A(til(k.c_t, j), til(k.c_acc, j), ACT.Silu, bias=col(k, "cln_b", j)).then_inc(k.s_c_silu, 1)
    for j in range(2):
        e.wait_ge(k.s_c_silu, j + 1)
        A(til(k.y_hi, 6 + j), til(k.c_t, j), ACT.Copy).then_inc(k.s_y_hi, 1)

    for m in range(12):
        e.wait_ge(k.s_g_conv, m + 1)
        A(til(k.qkv, m), til(k.qkv, m), ACT.Silu).then_inc(k.s_g_silu, 1)
    for m in range(2 * HEADS):
        e.wait_ge(k.s_g_silu, m + 1)
        if m >= 2:
            e.wait_ge(k.s_unit_sum, NORM_G + m - 1)
        A(til(k.sq, m % 2), til(k.qkv, m), ACT.Square).then_inc(k.s_unit_sq, 1)
    A(k.tok[:, TOK_BETA:TOK_BETA + 16].rearrange("p (c h) -> p c h", c=TT),
      k.tok[:, TOK_A:TOK_A + 48].rearrange("p (c w) -> p c w", c=TT)[:, :, 4:8], ACT.Sigmoid).then_inc(k.s_beta_done, 1)
    e.wait_ge(k.s_sp_in, 1)
    A(k.tok[:, TOK_SP + 24:TOK_SP + 48], k.tok[:, TOK_SP + 24:TOK_SP + 48], ACT.Exp, scale=-1.0)
    A(k.tok[:, TOK_EA:TOK_EA + 16], k.vec[:, VEC["a_log"][0]:VEC["a_log"][0] + 16],
      ACT.Exp).then_inc(k.s_sp_exp, 1)
    for m in range(2 * HEADS):
        e.wait_ge(k.s_unit_sum, NORM_G + m + 1)
        if m >= 2:
            e.wait_ge(k.s_g_qk_done, m - 1)
        A(k.g_d[:] if m % 2 == 0 else k.g_r[:], k.ps[m][:], ACT.Sqrt, bias=k.eps[:, 0:1]).then_inc(k.s_unit_std, 1)
    e.wait_ge(k.s_dec_copied, 1)
    A(k.tok[:, TOK_EDEC:TOK_EDEC + 16], k.tok[:, TOK_DEC:TOK_DEC + 16], ACT.Exp)
    A(k.tok[:, TOK_EKD:TOK_EKD + 16], k.tok[:, TOK_EKD:TOK_EKD + 16], ACT.Exp)
    A(k.tok[:, TOK_ELAST:TOK_ELAST + 16], k.tok[:, TOK_LAST:TOK_LAST + 16], ACT.Exp).then_inc(k.s_dec_exp, 1)
    for h in range(HEADS):
        e.wait_ge(k.s_gam_d, h + 1)
        A(til(k.g_xt, h), k.ps[h][:], ACT.Exp).then_inc(k.s_edecrow, 1)
        A(til(k.g_at, h), til(k.g_at, h), ACT.Exp).then_inc(k.s_gam_e, 1)
    e.wait_ge(k.s_dec_exp, 1)
    for h in range(HEADS):
        e.wait_ge(k.s_kt_mm, h + 1)
        for c in range(TT):
            t = TOK_EDEC + c * HEADS + h
            A(k.g_ek[:, h * T + c * P:h * T + (c + 1) * P], k.ps[6][:, c * P:(c + 1) * P], ACT.Copy,
              scale=k.tok[:, t:t + 1])
        for c in range(TT):
            t = TOK_EKD + c * HEADS + h
            ins = A(k.g_kdec[:, h * T + c * P:h * T + (c + 1) * P], k.ps[6][:, c * P:(c + 1) * P], ACT.Copy,
                    scale=k.tok[:, t:t + 1])
        ins.then_inc(k.s_ek_done, 1)
        e.wait_ge(k.s_vt_mm, h + 1)
        A(til(k.g_v, h), k.ps[7][:], ACT.Copy).then_inc(k.s_v_tok_done, 1)
    e.sem_inc(k.s_p_copied, 2)
    with e.Fori(0, LEVELS) as lev:
        for h in range(HEADS):
            e.wait_ge(k.s_p_mm, lev * HEADS + h + 1)
            e.wait_ge(k.s_x_done, lev * HEADS + h + 3)
            A(til(k.g_p, h % 2), k.ps[h % 2][:], ACT.Copy).then_inc(k.s_p_copied, 1)
    for h in range(HEADS):
        e.wait_ge(k.s_wt_mm, h + 1)
        A(til(k.qkv, 4 + h), k.ps[6 + h % 2][:], ACT.Copy, scale=-1.0).then_inc(k.s_wt_done, 1)
    for c in range(TT):
        for h in range(HEADS):
            e.wait_ge(k.s_o_part, c * HEADS + h + 1)
            A(til(k.qkv, 8 + h)[:, c * P:(c + 1) * P], k.ps[4 + h % 2][:, 0:P], ACT.Copy).then_inc(k.s_o_copied, 1)
    e.wait_ge(k.s_o_copied, HEADS * TT)
    for h in range(HEADS):
        A(til(k.g_x, h), til(k.qkv, 8 + h), ACT.Square).then_inc(k.s_unit_sq, 1)
    for h in range(HEADS):
        e.wait_ge(k.s_unit_sum, NORM_GO + h + 1)
        A(til(k.g_xt, h), k.ps[h][:], ACT.Sqrt, bias=k.eps[:, 0:1], scale=1.0 / P).then_inc(k.s_unit_std, 1)
    for h in range(HEADS):
        A(til(k.proj, 12 + h), til(k.proj, 12 + h), ACT.Silu).then_inc(k.s_z_silu, 1)
    for h in range(HEADS):
        e.wait_ge(k.s_go_norm, h + 1)
        A(til(k.y_hi, h), til(k.qkv, 8 + h), ACT.Copy).then_inc(k.s_y_hi, 1)

    def residual_feeds(gain, times=KT, split=True, per=4):
        with e.Fori(0, times // per) as i:
            fed.enter(i, per)
            for j in range(per):
                e.wait_ge(k.s_x_new, fed.at(1) - 2 * KT)
                g = k.vec[:, bass.ds(i * per + (VEC[gain][0] + j), 1)]
                feed(rtil(k.x, i * per + j), g, rtil(k.h_hi, i * per + j), split=split)
            fed.leave(times // per)

    residual_feeds("norm_cross")

    root(3, k.rstd)
    for h in range(HEADS):
        e.wait_ge(k.s_aq_raw, h + 1)
        if h >= 2:
            e.wait_ge(k.s_unit_sum, NORM_AQ + h - 1)
        else:
            e.wait_ge(k.s_sq_used, 2 + 3 * KT)
        A(til(k.sq, h % 2), til(k.a_q, h), ACT.Square).then_inc(k.s_unit_sq, 1)
        e.wait_ge(k.s_unit_sum, NORM_AQ + h + 1)
        if h >= 2:
            e.wait_ge(k.s_aq_done, h - 1)
        A(til(k.a_p, h % 2), k.ps[4 + h % 2][:], ACT.Sqrt, bias=k.eps[:, 0:1], scale=1.0 / P).then_inc(k.s_unit_std, 1)
    for h in range(HEADS):
        for half in range(2):
            u = 2 * h + half
            e.wait_ge(k.s_al_max, u + 1)
            if h:
                e.wait_ge(k.s_apt_mm, 2 * h)
            else:
                e.wait_ge(k.s_aq_done, HEADS)
            for n in range(2):
                c = 2 * half + n
                ins = A(k.a_p[:, c * MEM:(c + 1) * MEM], k.ps[half][:, n * MEM:(n + 1) * MEM], ACT.Exp,
                        scale=XA_SCALE, bias=k.tok[:, TOK_NM + c:TOK_NM + c + 1],
                        accum_out=k.tok[:, TOK_SUM + c:TOK_SUM + c + 1])
            ins.then_inc(k.s_al_exp, 1)
        for mt in range(2):
            e.wait_ge(k.s_apt_mm, 2 * h + mt + 1)
            if h:
                e.wait_ge(k.s_av_mm, h)
            A(til(k.a_pt, mt), k.ps[2 + mt][:], ACT.Copy).then_inc(k.s_apt_copied, 1)
        e.wait_ge(k.s_av_mm, h + 1)
        A(til(k.ao_hi, h), k.ps[4 + h % 2][:], ACT.Copy).then_inc(k.s_ao_hi_done, 1)
    residual_feeds("norm_mlp")

    root(4, k.rstd)
    for half in range(2):
        with e.Fori(0, MTH // 4) as i:
            for j in range(4):
                m = i * 4 + j
                e.wait_ge(k.s_up_relu, m + (half * MTH + 1))
                A(k.u_t[:, (2 + j % 2) * T:(3 + j % 2) * T], k.u_t[:, (j % 2) * T:(j % 2 + 1) * T],
                  ACT.Square).then_inc(k.s_up_sq, 1)
                e.wait_ge(k.s_up_sq, m + (half * MTH + 1))
                A(rtil(k.u_hi, m), k.u_t[:, (2 + j % 2) * T:(3 + j % 2) * T], ACT.Copy).then_inc(k.s_up_hi, 1)
    residual_feeds("ln1")

    root(5, k.rstd)
    st = lambda n: til(k.s_t, n)
    with e.Fori(0, KT) as i:
        e.wait_ge(k.s_s2_u, i + 1)
        A(k.ub_hi[:], st(0), ACT.Copy).then_inc(k.s_s2_uhi, 1)
        e.wait_ge(k.s_s2_gl, i + 1)
        A(st(2), st(1), ACT.Square).then_inc(k.s_s2_gsq, 1)
        e.wait_ge(k.s_s2_gt, i + 1)
        A(st(2), st(2), ACT.Sigmoid, scale=GELU_SCALE).then_inc(k.s_s2_gsig, 1)
        for n in range(2):
            e.wait_ge(k.s_s2_gate, i * 2 + n + 1)
            g = rtil(k.gates, i + n * KT)
            A(g, g, ACT.Sigmoid, bias=k.vec[:, bass.ds(i + (VEC["gate_b"][0] + n * KT), 1)]).then_inc(k.s_s2_gate_done, 1)
        e.wait_ge(k.s_panel_used, i * 8 + (SPLIT + PAN_S6 + 5))
        A(st(3), k.ps[2][:], ACT.Sigmoid, bias=k.vec[:, bass.ds(i + VEC["lru_ba"][0], 1)]).then_inc(k.s_s2_r, 1)
        A(st(4), k.ps[3][:], ACT.Sigmoid, bias=k.vec[:, bass.ds(i + VEC["lru_bx"][0], 1)]).then_inc(k.s_s2_i, 1)
        e.wait_ge(k.s_s2_r, i + 1)
        A(st(6), st(3), ACT.Tanh, scale=k.tok[:, bass.ds(i + TOK_P8, 1)]).then_inc(k.s_s2_th, 1)
        A(st(5), st(3), ACT.Exp, scale=k.tok[:, bass.ds(i + TOK_N8, 1)]).then_inc(k.s_s2_a, 1)
        e.wait_ge(k.s_s2_a, i + 1)
        A(st(7), st(5), ACT.Square).then_inc(k.s_s2_a2, 1)
        e.wait_ge(k.s_s2_m, i + 1)
        A(st(7), st(7), ACT.Sqrt, bias=k.eps[:, 1:2]).then_inc(k.s_s2_s, 1)
        e.wait_ge(k.s_s2_yb, i + 1)
        A(rtil(k.yb_hi, i), st(8), ACT.Copy).then_inc(k.s_s2_yb_hi, 1)
        e.wait_ge(k.s_s2_ya, i + 1)
        A(rtil(k.ya_hi, i), st(3), ACT.Copy).then_inc(k.s_s2_ya_hi, 1)
    with e.Fori(0, KT // 2) as i:
        for j in range(2):
            e.wait_ge(k.s_mg, i * 2 + j + 1)
            A(rtil(k.mg_hi, i * 2 + j), st(2 * j), ACT.Copy).then_inc(k.s_mg_hi, 1)
    residual_feeds("ln2")

    root(6, k.rstd)
    with e.Fori(0, FFN // 2) as i:
        for j in range(2):
            e.wait_ge(k.s_f_g, i * 2 + j + 1)
            A(til(k.f_t, j), til(k.f_t, j), ACT.Silu).then_inc(k.s_f_silu, 1)
            e.wait_ge(k.s_f_hid, i * 2 + j + 1)
            A(rtil(k.f_hi, i * 2 + j), til(k.f_t, j), ACT.Copy).then_inc(k.s_f_hi_done, 1)
    residual_feeds("final", split=False)
    root(7, k.rstd)


GELU_SCALE = 2.0 * 0.7978845608028654
XA_SCALE = 128 ** -0.5
PAN_S6 = 112
PAN_S7 = PAN_S6 + 64
PAN_S8 = PAN_S7 + 16
PAN_S9 = PAN_S8 + 8
PAN_DOWN = PAN_S9 + 44


def vector_program(nc, k):
    e = nc.vector
    chain = Chain(e, k.s_dve_chain)
    fed = Count()
    TS, TTn, STT = e.tensor_scalar, e.tensor_tensor, e.scalar_tensor_tensor
    for b in range(8):
        e.sem_inc(k.acc_free[b], 1)
    e.memset(k.eps[:, 0:1], EPS)
    e.memset(k.eps[:, 1:2], 1e-30)
    e.memset(k.m_sqa[:], 0.0)
    e.sem_inc(k.s_sq_used, 2)
    chain(e.memset(k.sqacc[:], 0.0))
    e.sem_inc(k.s_zeroed, 1)

    def feed(src, gain, hi, lo, w=T, split=True, sqacc=None):
        acc = (sqacc or k.sqacc)[:, 0:w]
        if split:
            e.wait_ge(k.s_fed_hi, fed.at(1))
            STT(out=lo, in0=src, scalar=gain, in1=hi.bitcast(F32), op0=ALU.mult,
                op1=ALU.subtract).then_inc(k.s_fed_lo, 1)
        e.wait_ge(k.s_fed_sq, fed.at(1))
        TTn(acc, acc, k.sq[:, (fed.n % 2) * T:(fed.n % 2) * T + w], ALU.add).then_inc(k.s_sq_used, 1)
        fed.step()
        e.wait_ge(k.s_sq_used, 2 + fed.at())

    def invert(n_norm, dst, w=T):
        e.wait_ge(k.s_std, n_norm)
        e.reciprocal(dst[:, 0:w], dst[:, 0:w]).then_inc(k.s_rstd, 1)
        e.wait_ge(k.s_rstd, n_norm)

    freed = [1 + 2 + 6, 1 + 2 + 6, 1 + 1 + 6, 1 + 1 + 6, 1, 1, 1, 1]

    e.wait_ge(k.s_ld_vec, 16)
    e.wait_ge(k.s_ld_mem, 16)
    for m in range(KT):
        feed(til(k.mem, m, w=MEM), col(k, "norm_mem", m), til(k.m_hi, m, w=MEM), til(k.m_lo, m, w=MEM), MEM,
             sqacc=k.m_sqa)
    invert(1, k.m_rstd, MEM)
    for m in range(HEADS):
        e.wait_ge(k.s_panel_used, SPLIT + m + 1)
        ins = TTn(til(k.xk, m, w=MEM), k.ps[m % 2][:, 0:MEM], k.m_rstd[:], ALU.mult)
        ins.then_inc(k.acc_free[m % 2], 1)
    e.wait_ge(k.acc_free[0], 3)
    e.wait_ge(k.acc_free[1], 3)
    e.sem_inc(k.s_xk_raw, 1)
    e.wait_ge(k.s_ld_x, 16)
    for m in range(KT):
        feed(til(k.x, m), col(k, "norm_mix", m), til(k.h_hi, m), til(k.h_lo, m))
    e.wait_ge(k.s_panel_used, SPLIT + 8)
    e.wait_ge(k.s_v_done, 1)
    for mt in range(2):
        TS(til(k.xv, mt), k.ps[2 + mt][:], k.tok[:, TOK_RTOK + mt:TOK_RTOK + mt + 1], None,
           ALU.mult).then_inc(k.acc_free[2 + mt], 1)
        e.wait_ge(k.acc_free[2 + mt], 2)
    e.sem_inc(k.s_v_done, 1)
    invert(2, k.rstd)
    e.wait_ge(k.s_unit_std, 1)
    xk_r = k.mem[:, HEADS * MEM:2 * HEADS * MEM]
    chain(e.reciprocal(xk_r, xk_r))
    STT(out=k.xk[:], in0=k.xk[:], scalar=col(k, "xa_k"), in1=xk_r, op0=ALU.mult, op1=ALU.mult).then_inc(k.s_xk_done, 1)

    with e.Fori(0, 6) as i:
        for j in range(4):
            e.wait_ge(k.s_panel_used, i * 4 + (SPLIT + 8 + j + 1))
            TTn(rtil(k.proj, i * 4 + j), k.ps[j][:], k.rstd[:], ALU.mult).then_inc(k.acc_free[j], 1)
    for j in range(4):
        e.wait_ge(k.acc_free[j], freed[j])
    e.sem_inc(k.s_proj_done, 1)
    e.memset(k.d_v[:], 0.0).then_inc(k.s_dve_chain, 1)
    e.wait_ge(k.s_dve_chain, chain.c.step())
    for n, (bank, dst) in enumerate(((0, til(k.d_q, 0)), (1, til(k.d_q, 1)), (2, til(k.d_qi, 0)), (3, til(k.d_qi, 1)),
                                     (4, k.d_k[:]))):
        e.wait_ge(k.s_dq_mm, n + 1)
        e.tensor_copy(dst, k.ps[bank][:]).then_inc(k.s_dq_raw, 1)
    e.wait_ge(k.s_dq_mm, 6)
    for par in range(2):
        dst = k.d_v[:].rearrange("p (t q w) -> p t q w", t=TT, q=2)[:, :, par, 64 * par:64 * par + 64]
        ins = e.tensor_copy(dst, k.ps[5][:, 0:256].rearrange("p (t w) -> p t w", t=TT))
    ins.then_inc(k.s_dq_raw, 1)
    e.wait_ge(k.s_d_gates_tok, 1)
    chain(TS(k.tok[:, TOK_W:TOK_W + 16].rearrange("p (c h) -> p c h", c=TT),
             k.tok[:, TOK_A:TOK_A + 48].rearrange("p (c w) -> p c w", c=TT)[:, :, 8:12], 1.0 / 16, None, ALU.mult))
    for n, (raw, root, gain) in enumerate(((til(k.d_q, 0), til(k.d_relu, 0), "dsa_q"),
                                           (til(k.d_q, 1), til(k.d_relu, 1), "dsa_q"),
                                           (k.d_k[:], til(k.d_p, 0), "dsa_k"))):
        e.wait_ge(k.s_unit_std, NORM_DQ + n + 1)
        chain(e.reciprocal(root, root))
        STT(out=raw, in0=raw, scalar=col(k, gain), in1=root, op0=ALU.mult, op1=ALU.mult).then_inc(k.s_dq_done, 1)
    e.wait_ge(k.s_dq_done, 3)
    m8 = k.tok[:, TOK_M8:TOK_M8 + 8]
    for qt in range(TT):
        cw = (qt + 1) * P
        causal = k.const[:, C_CAUS + T - cw:C_CAUS + T]
        bias = causal
        if qt:
            score = k.d_score[:, 0:cw]
            for h in range(HEADS):
                v = HEADS * (qt - 1) + h
                w = TOK_W + qt * HEADS + h
                e.wait_ge(k.s_idx_relu, v + 1)
                STT(out=score, in0=k.d_relu[:, (h % 2) * T:(h % 2) * T + cw], scalar=k.tok[:, w:w + 1],
                    in1=causal if h == 0 else score, op0=ALU.mult, op1=ALU.add).then_inc(k.s_idx_used, 1)
                e.wait_ge(k.s_idx_used, v + 1)
            for _ in range(TOPK // 8):
                chain(e.max(m8, score))
                chain(e.match_replace(score, m8, score, TAKEN))
            bias = k.d_bias[:, 0:cw]
            chain(TS(bias, score, TAKEN, MASKED, ALU.not_equal, ALU.mult))

        def soften(h):
            u = qt * HEADS + h
            p, mx = k.d_p[:, (h % 2) * T:(h % 2) * T + cw], k.tok[:, TOK_MX + h % 2:TOK_MX + h % 2 + 1]
            e.wait_ge(k.s_lg_mm, u + 1)
            if u >= 2:
                e.wait_ge(k.s_pt_mm, u - 1)
            chain(STT(out=p, in0=k.ps[4 + h % 2][:, 0:cw], scalar=0.125, in1=bias, op0=ALU.mult, op1=ALU.add))
            chain(e.tensor_reduce(mx, p, AX.X, ALU.max))
            TS(k.tok[:, TOK_NM + h % 2:TOK_NM + h % 2 + 1], mx, -1.0, None, ALU.mult).then_inc(k.s_lg_masked, 1)

        soften(0)
        for h in range(HEADS):
            u = qt * HEADS + h
            if h + 1 < HEADS:
                soften(h + 1)
            p = k.d_p[:, (h % 2) * T:(h % 2) * T + cw]
            r = k.tok[:, TOK_R + h % 2:TOK_R + h % 2 + 1]
            e.wait_ge(k.s_p_exp, u + 1)
            chain(e.reciprocal(r, k.tok[:, TOK_SUM + h % 2:TOK_SUM + h % 2 + 1]))
            TS(p, p, r, None, ALU.mult).then_inc(k.s_p_norm, 1)
            if h % 2:
                j = h // 2
                at = (4 + j) * T + qt * P
                e.wait_ge(k.s_y_hi, 2 * qt + j + 1)
                TTn(k.y_lo[:, at:at + P], k.ps[j][:, 0:P], k.y_hi[:, at:at + P].bitcast(F32),
                    ALU.subtract).then_inc(k.s_y_lo, 1)

    e.wait_ge(k.s_c_sig, 1)
    chain(TTn(k.c_y[:], til(k.proj, 16, 2), k.c_y[:], ALU.mult))
    for tap in range(CONV_TAPS):
        s = tap
        for j in range(2):
            y, acc = til(k.c_y, j), til(k.c_acc, j)
            w = col(k, "dw", j * CONV_TAPS + CONV_TAPS - 1 - s)
            if s == 0:
                ins = TS(acc, y, w, col(k, "dw_b", j), ALU.mult, ALU.add)
            else:
                ins = STT(out=acc[:, s:T], in0=y[:, 0:T - s], scalar=w, in1=acc[:, s:T], op0=ALU.mult, op1=ALU.add)
            if s == CONV_TAPS - 1:
                ins.then_inc(k.s_c_conv, 1)
            elif j == 1:
                chain(ins)
            else:
                ins.then_inc(k.s_dve_chain, 1)
                chain.c.step()
    for j in range(2):
        e.wait_ge(k.s_c_mean, 1)
        e.wait_ge(k.s_c_conv, 2)
        acc = til(k.c_acc, j)
        STT(out=acc, in0=k.ps[0][:], scalar=-1.0 / 256, in1=acc, op0=ALU.mult, op1=ALU.add).then_inc(k.s_c_cent, 1)
    e.wait_ge(k.s_c_std, 1)
    chain(e.reciprocal(k.c_r[:], k.c_r[:]))
    for j in range(2):
        e.wait_ge(k.s_c_cent, 2)
        e.wait_ge(k.s_c_sq, 2)
        acc = til(k.c_acc, j)
        STT(out=acc, in0=acc, scalar=col(k, "cln_g", j), in1=k.c_r[:], op0=ALU.mult, op1=ALU.mult).then_inc(k.s_c_norm, 1)
    for j in range(2):
        e.wait_ge(k.s_y_hi, 2 * TT + j + 1)
        TTn(til(k.y_lo, 6 + j), til(k.c_t, j), til(k.y_hi, 6 + j).bitcast(F32), ALU.subtract).then_inc(k.s_y_lo, 1)

    for m in range(12):
        src, dst = til(k.proj, m), til(k.qkv, m)
        for s in range(4):
            w = col(k, "gdn_conv", m * 4 + 3 - s)
            if s == 0:
                ins = TS(dst, src, w, None, ALU.mult)
            else:
                ins = STT(out=dst[:, s:T], in0=src[:, 0:T - s], scalar=w, in1=dst[:, s:T], op0=ALU.mult, op1=ALU.add)
            if s == 3:
                ins.then_inc(k.s_g_conv, 1)
            else:
                chain(ins)
    e.wait_ge(k.s_g_conv, 12)
    tok = lambda at, n: k.tok[:, at:at + n]
    v, z, t, w2, s_ = (tok(TOK_SP + 24 * n, 24) for n in range(5))
    TTn(tok(TOK_SP, 16).rearrange("p (c h) -> p c h", c=TT),
        k.tok[:, TOK_A:TOK_A + 48].rearrange("p (c w) -> p c w", c=TT)[:, :, 0:4],
        k.vec[:, VEC["dt_bias"][0]:VEC["dt_bias"][0] + 16].rearrange("p (c h) -> p c h", c=TT), ALU.add)
    chain(TS(tok(TOK_SP + 16, 8), k.vec[:, VEC["lam"][0]:VEC["lam"][0] + 8], -1.0, None, ALU.mult))
    STT(out=z, in0=v, scalar=-1.0, in1=v, op0=ALU.mult, op1=ALU.max).then_inc(k.s_sp_in, 1)
    e.wait_ge(k.s_sp_exp, 1)
    chain(TS(t, z, 2.0, None, ALU.add))
    chain(e.reciprocal(t, t))
    chain(TTn(z, z, t, ALU.mult))
    chain(TTn(w2, z, z, ALU.mult))
    chain(TS(s_, w2, 1.0 / 15, 1.0 / 13, ALU.mult, ALU.add))
    for n in (11, 9, 7, 5, 3, 1):
        chain(TTn(s_, s_, w2, ALU.mult))
        chain(TS(s_, s_, 1.0 / n, None, ALU.add))
    chain(TTn(s_, s_, z, ALU.mult))
    chain(TS(v, v, 0.0, None, ALU.max))
    chain(STT(out=s_, in0=s_, scalar=2.0, in1=v, op0=ALU.mult, op1=ALU.add))
    TS(tok(TOK_N8, 8), s_[:, 16:24], -8.0, None, ALU.mult)
    TS(tok(TOK_P8, 8), s_[:, 16:24], 8.0, None, ALU.mult)
    STT(out=tok(TOK_G, 16), in0=s_[:, 0:16], scalar=-1.0, in1=tok(TOK_EA, 16), op0=ALU.mult,
        op1=ALU.mult).then_inc(k.s_g_ready, 1)
    e.wait_ge(k.s_g_ready, 1)
    for h in range(HEADS):
        for c in range(TT):
            t_ = TOK_G + c * HEADS + h
            ins = TS(k.g_x[:, h * T + c * P:h * T + (c + 1) * P], k.const[:, C_ONE:C_ONE + P], k.tok[:, t_:t_ + 1], None,
                     ALU.mult)
        ins.then_inc(k.s_gb_done, 1)
    for m in range(2 * HEADS):
        r = k.g_d if m % 2 == 0 else k.g_r
        e.wait_ge(k.s_unit_std, NORM_G + m + 1)
        chain(e.reciprocal(r[:], r[:]))
        q = til(k.qkv, m)
        STT(out=q, in0=q, scalar=P ** -0.5 if m < HEADS else 1.0, in1=r[:], op0=ALU.mult,
            op1=ALU.mult).then_inc(k.s_g_qk_done, 1)
    e.wait_ge(k.s_dec_mm, 1)
    chain(e.tensor_copy(tok(TOK_DEC, 32), k.ps[7][:, 0:32]))
    TTn(tok(TOK_EKD, 16), tok(TOK_LAST, 16), tok(TOK_DEC, 16), ALU.subtract).then_inc(k.s_dec_copied, 1)
    tri4 = k.const[:, C_TRI:C_TRI + P].unsqueeze(1).broadcast_to([P, TT, P])
    for h in range(HEADS):
        e.wait_ge(k.s_decrow, h + 1)
        for c in range(TT):
            t_ = TOK_DEC + c * HEADS + h
            ins = TS(k.g_at[:, h * T + c * P:h * T + (c + 1) * P], k.ps[h][:, c * P:(c + 1) * P], k.tok[:, t_:t_ + 1],
                     0.0, ALU.subtract, ALU.min)
        ins.then_inc(k.s_gam_d, 1)
    for h in range(HEADS):
        e.wait_ge(k.s_gam_e, h + 1)
        g3 = til(k.g_at, h).rearrange("p (c i) -> p c i", c=TT)
        TTn(g3, g3, tri4, ALU.mult).then_inc(k.s_gam_done, 1)
    e.wait_ge(k.s_gam_done, HEADS)
    e.wait_ge(k.s_beta_done, 1)
    for h in range(HEADS):
        e.wait_ge(k.s_qk_mm, h + 1)
        TTn(til(k.g_qk, h), k.ps[4][:], til(k.g_at, h), ALU.mult).then_inc(k.s_qk_done, 1)
        e.wait_ge(k.s_qk_done, h + 1)
        e.wait_ge(k.s_kk_mm, h + 1)
        for c in range(TT):
            t_ = TOK_BETA + c * HEADS + h
            a = k.g_at[:, h * T + c * P:h * T + (c + 1) * P]
            ins = STT(out=a, in0=k.ps[5][:, c * P:(c + 1) * P], scalar=k.tok[:, t_:t_ + 1], in1=a, op0=ALU.mult,
                      op1=ALU.mult)
        ins.then_inc(k.s_at_done, 1)
    e.wait_ge(k.s_at_done, HEADS)
    for h in range(HEADS):
        e.wait_ge(k.s_edecrow, h + 1)
        e.wait_ge(k.s_kk_mm, HEADS)
        q = til(k.qkv, h)
        TTn(q, q, til(k.g_xt, h), ALU.mult).then_inc(k.s_gam_done, 1)
    id16 = k.const[:, C_ID:C_ID + P].unsqueeze(1).broadcast_to([P, HEADS * TT, P])
    e.wait_ge(k.s_gam_done, 2 * HEADS)
    e.tensor_copy(k.g_x[:].rearrange("p (n i) -> p n i", i=P), id16)
    e.tensor_copy(k.g_xt[:].rearrange("p (n i) -> p n i", i=P), id16)
    chain(e.memset(k.g_s[:], 0.0))
    e.sem_inc(k.s_x_init, 1)
    e.sem_inc(k.s_x_done, HEADS)
    e.sem_inc(k.s_st_done, HEADS)

    with e.Fori(0, LEVELS) as lev:
        mask = k.const[:, bass.ds(lev * P + C_LEV, P)].unsqueeze(1).broadcast_to([P, TT, P])

        def blocks(h):
            TTn(til(k.g_b, h % 2).rearrange("p (c i) -> p c i", c=TT),
                til(k.g_at, h).rearrange("p (c i) -> p c i", c=TT), mask, ALU.mult).then_inc(k.s_bt_done, 1)

        blocks(0)
        for h in range(HEADS):
            if h + 1 < HEADS:
                blocks(h + 1)
            e.wait_ge(k.s_xp_mm, lev * HEADS + h + 1)
            TTn(til(k.g_x, h), til(k.g_x, h), k.ps[2 + h % 2][:], ALU.subtract)
            TTn(til(k.g_xt, h), til(k.g_xt, h), k.ps[4 + h % 2][:], ALU.subtract).then_inc(k.s_x_done, 1)
    for c in range(TT):
        for h in range(HEADS):
            u = c * HEADS + h
            t_ = c * HEADS + h
            e.wait_ge(k.s_vn_mm, u + 1)
            TS(k.g_vn[:, h * P:(h + 1) * P], k.ps[h][:, 0:P], k.tok[:, TOK_BETA + t_:TOK_BETA + t_ + 1], None,
               ALU.mult).then_inc(k.s_vn_done, 1)
        for h in range(HEADS):
            u = c * HEADS + h
            t_ = c * HEADS + h
            s = k.g_s[:, h * P:(h + 1) * P]
            e.wait_ge(k.s_st_mm, u + 1)
            STT(out=s, in0=s, scalar=k.tok[:, TOK_ELAST + t_:TOK_ELAST + t_ + 1], in1=k.ps[6 + h % 2][:, 0:P],
                op0=ALU.mult, op1=ALU.add).then_inc(k.s_st_done, 1)
        e.wait_ge(k.s_st_done, HEADS + HEADS * (c + 1))
    for h in range(HEADS):
        e.wait_ge(k.s_unit_std, NORM_GO + h + 1)
        r = til(k.g_xt, h)
        chain(e.reciprocal(r, r))
        o = til(k.qkv, 8 + h)
        chain(STT(out=o, in0=o, scalar=col(k, "gdn_norm"), in1=r, op0=ALU.mult, op1=ALU.mult))
        e.wait_ge(k.s_z_silu, h + 1)
        TTn(o, o, til(k.proj, 12 + h), ALU.mult).then_inc(k.s_go_norm, 1)
    e.wait_ge(k.s_go_norm, HEADS)
    for h in range(HEADS):
        e.wait_ge(k.s_y_hi, 2 * TT + 2 + h + 1)
        TTn(til(k.y_lo, h), til(k.qkv, 8 + h), til(k.y_hi, h).bitcast(F32), ALU.subtract).then_inc(k.s_y_lo, 1)

    def residual(pan0, panels_per_tile, gain, banks=2, split=True, feeds=True, per=4):
        chain(e.memset(k.sqacc[:], 0.0))
        with e.Fori(0, KT // per) as i:
            fed.enter(i, per if feeds else 0)
            for j in range(per):
                m = i * per + j
                num, den = panels_per_tile
                e.wait_ge(k.s_panel_used, i * (per * num // den) + (SPLIT + pan0 + (j * num) // den + num))
                x = rtil(k.x, m)
                ins = TTn(x, x, k.ps[j % banks][:], ALU.add)
                ins.then_inc(k.acc_free[j % banks], 1)
                e.wait_ge(k.acc_free[j % banks], acc_value(i, j, banks, per))
                if feeds:
                    e.sem_inc(k.s_x_new, 1)
                    g = k.vec[:, bass.ds(i * per + (VEC[gain][0] + j), 1)]
                    feed(x, g, rtil(k.h_hi, m), rtil(k.h_lo, m), split=split)
            fed.leave(KT // per)
        for b in range(banks):
            freed[b] += KT // banks


    def acc_value(i, j, banks, per):
        return i * (per // banks) + (freed[j % banks] + j // banks + 1)

    residual(32, (1, 1), "norm_cross")

    invert(3, k.rstd)
    for j in range(HEADS):
        e.wait_ge(k.s_panel_used, SPLIT + 40 + j + 1)
        TTn(til(k.a_q, j), k.ps[j][:], k.rstd[:], ALU.mult).then_inc(k.acc_free[j], 1)
        freed[j] += 1
        e.wait_ge(k.acc_free[j], freed[j])
        e.sem_inc(k.s_aq_raw, 1)
    for h in range(HEADS):
        e.wait_ge(k.s_unit_std, NORM_AQ + h + 1)
        r = til(k.a_p, h % 2)
        chain(e.reciprocal(r, r))
        q = til(k.a_q, h)
        STT(out=q, in0=q, scalar=col(k, "xa_q"), in1=r, op0=ALU.mult, op1=ALU.mult).then_inc(k.s_aq_done, 1)
    for h in range(HEADS):
        for half in range(2):
            u = 2 * h + half
            e.wait_ge(k.s_al_mm, u + 1)
            if h:
                e.wait_ge(k.s_al_exp, u - 1)
            chain(e.tensor_reduce(tok(TOK_MX + 2 * half, 2), k.ps[half][:].rearrange("p (n m) -> p n m", n=2), AX.X,
                                  ALU.max))
            TS(tok(TOK_NM + 2 * half, 2), tok(TOK_MX + 2 * half, 2), -XA_SCALE, None, ALU.mult).then_inc(k.s_al_max, 1)
        for half in range(2):
            u = 2 * h + half
            e.wait_ge(k.s_al_exp, u + 1)
            chain(e.reciprocal(tok(TOK_R + 2 * half, 2), tok(TOK_SUM + 2 * half, 2)))
            for n in range(2):
                c = 2 * half + n
                p = k.a_p[:, c * MEM:(c + 1) * MEM]
                ins = TS(p, p, tok(TOK_R + c, 1), None, ALU.mult)
            ins.then_inc(k.s_al_norm, 1)
        e.wait_ge(k.s_ao_hi_done, h + 1)
        TTn(til(k.ao_lo, h), k.ps[4 + h % 2][:], til(k.ao_hi, h).bitcast(F32), ALU.subtract).then_inc(k.s_ao_lo_done, 1)
    residual(44, (1, 2), "norm_mlp")

    invert(4, k.rstd)
    for half in range(2):
        pan0 = 48 + 32 * half
        with e.Fori(0, MTH // 4) as i:
            for j in range(4):
                m = i * 4 + j
                e.wait_ge(k.s_panel_used, m + (SPLIT + pan0 + 1))
                STT(out=til(k.u_t, j % 2), in0=k.ps[j % 2][:], scalar=0.0, in1=k.rstd[:], op0=ALU.max,
                    op1=ALU.mult).then_inc(k.acc_free[j % 2], 1)
                e.wait_ge(k.acc_free[j % 2], i * 2 + (freed[j % 2] + j // 2 + 1))
                e.sem_inc(k.s_up_relu, 1)
                e.wait_ge(k.s_up_hi, m + (half * MTH + 1))
                TTn(rtil(k.u_lo, m), til(k.u_t, 2 + j % 2), rtil(k.u_hi, m).bitcast(F32),
                    ALU.subtract).then_inc(k.s_up_lo, 1)
        for b in range(2):
            freed[b] += MTH // 2
        residual(pan0 + 16, (2, 1), "ln1", feeds=half == 1)

    invert(5, k.rstd)
    st = lambda n: til(k.s_t, n)
    with e.Fori(0, KT) as i:
        chain.c.enter(i, 12)

        def leave(dst, bank, panel_no):
            e.wait_ge(k.s_panel_used, i * 8 + (SPLIT + PAN_S6 + panel_no + 1))
            TTn(dst, k.ps[bank][:], k.rstd[:], ALU.mult).then_inc(k.acc_free[bank], 1)
            e.wait_ge(k.acc_free[bank], i * (2 if bank == 0 else 1) + (freed[bank] + (2 if panel_no == 7 else 1)))

        leave(st(7), 0, 0)
        u = st(0)
        for s in range(4):
            w = k.vec[:, bass.ds(i * 4 + (VEC["conv_b"][0] + 3 - s), 1)]
            if s == 0:
                ins = TS(u, st(7), w, k.vec[:, bass.ds(i + VEC["conv_bb"][0], 1)], ALU.mult, ALU.add)
            else:
                ins = STT(out=u[:, s:T], in0=st(7)[:, 0:T - s], scalar=w, in1=u[:, s:T], op0=ALU.mult, op1=ALU.add)
            if s == 3:
                ins.then_inc(k.s_s2_u, 1)
            else:
                chain(ins)
        e.wait_ge(k.s_s2_uhi, i + 1)
        TTn(k.ub_lo[:], u, k.ub_hi[:].bitcast(F32), ALU.subtract).then_inc(k.s_s2_ulo, 1)
        leave(st(1), 1, 1)
        e.sem_inc(k.s_s2_gl, 1)
        e.wait_ge(k.s_s2_gsq, i + 1)
        chain(TS(st(2), st(2), 0.044715, 1.0, ALU.mult, ALU.add))
        TTn(st(2), st(2), st(1), ALU.mult).then_inc(k.s_s2_gt, 1)
        for n in range(2):
            leave(rtil(k.gates, i + n * KT), 4 + n, 2 + n)
            e.sem_inc(k.s_s2_gate, 1)
        e.wait_ge(k.s_s2_gsig, i + 1)
        chain(TTn(st(1), st(1), st(2), ALU.mult))
        e.wait_ge(k.s_s2_i, i + 1)
        e.sem_inc(k.acc_free[2], 1)
        e.sem_inc(k.acc_free[3], 1)
        e.wait_ge(k.s_s2_a2, i + 1)
        e.wait_ge(k.s_s2_th, i + 1)
        STT(out=st(7), in0=st(7), scalar=1.0, in1=st(6), op0=ALU.add, op1=ALU.mult).then_inc(k.s_s2_m, 1)
        chain(TTn(st(4), st(4), st(0), ALU.mult))
        e.wait_ge(k.s_s2_s, i + 1)
        chain(TTn(st(4), st(4), st(7), ALU.mult))
        chain(e.tensor_tensor_scan(st(8), st(5), st(4), 0.0, ALU.mult, ALU.add))
        TTn(st(8), st(8), st(1), ALU.mult).then_inc(k.s_s2_yb, 1)
        e.wait_ge(k.s_s2_yb_hi, i + 1)
        TTn(rtil(k.yb_lo, i), st(8), rtil(k.yb_hi, i).bitcast(F32), ALU.subtract)
        leave(st(0), 6, 5)
        leave(st(1), 7, 6)
        leave(st(2), 0, 7)
        chain(TTn(st(2), st(2), st(1), ALU.mult))
        for s in range(3):
            w = k.vec[:, bass.ds(i * 3 + (VEC["conv_a"][0] + 2 - s), 1)]
            if s == 0:
                chain(TS(st(3), st(2), w, None, ALU.mult))
            else:
                chain(STT(out=st(3)[:, s:T], in0=st(2)[:, 0:T - s], scalar=w, in1=st(3)[:, s:T], op0=ALU.mult,
                          op1=ALU.add))
        TTn(st(3), st(3), st(0), ALU.mult).then_inc(k.s_s2_ya, 1)
        e.wait_ge(k.s_s2_ya_hi, i + 1)
        TTn(rtil(k.ya_lo, i), st(3), rtil(k.ya_hi, i).bitcast(F32), ALU.subtract).then_inc(k.s_s2_free, 1)
        assert chain.c.n == 12, chain.c.n
        chain.c.leave(KT)
    for b in range(8):
        freed[b] += KT * (2 if b == 0 else 1)

    e.wait_ge(k.s_s2_gate_done, 2 * KT)
    with e.Fori(0, KT // 2) as i:
        chain.c.enter(i, 4)
        for j in range(2):
            for n in range(2):
                b = 2 * j + n
                e.wait_ge(k.s_panel_used, i * 4 + (SPLIT + PAN_S7 + b + 1))
                TTn(st(b), k.ps[b][:], rtil(k.gates, i * 2 + (j + n * KT)), ALU.mult).then_inc(k.acc_free[b], 1)
                e.wait_ge(k.acc_free[b], i + (freed[b] + 1))
            chain(TTn(st(2 * j), st(2 * j), st(2 * j + 1), ALU.add))
            e.sem_inc(k.s_mg, 1)
            e.wait_ge(k.s_mg_hi, i * 2 + j + 1)
            ins = TTn(rtil(k.mg_lo, i * 2 + j), st(2 * j), rtil(k.mg_hi, i * 2 + j).bitcast(F32), ALU.subtract)
            chain(ins)
            e.sem_inc(k.s_mg_lo, 1)
        chain.c.leave(KT // 2)
    for b in range(4):
        freed[b] += KT // 2
    residual(PAN_S8, (1, 1), "ln2")

    invert(6, k.rstd)
    with e.Fori(0, FFN // 2) as i:
        for j in range(2):
            for n in range(2):
                b = 2 * j + n
                e.wait_ge(k.s_panel_used, i * 4 + (SPLIT + PAN_S9 + b + 1))
                TTn(til(k.f_t, j + 2 * n), k.ps[b][:], k.rstd[:], ALU.mult).then_inc(k.acc_free[b], 1)
                e.wait_ge(k.acc_free[b], i + (freed[b] + 1))
                if n == 0:
                    e.sem_inc(k.s_f_g, 1)
            e.wait_ge(k.s_f_silu, i * 2 + j + 1)
            TTn(til(k.f_t, j), til(k.f_t, j), til(k.f_t, 2 + j), ALU.mult).then_inc(k.s_f_hid, 1)
            e.wait_ge(k.s_f_hi_done, i * 2 + j + 1)
            TTn(rtil(k.f_lo, i * 2 + j), til(k.f_t, j), rtil(k.f_hi, i * 2 + j).bitcast(F32),
                ALU.subtract).then_inc(k.s_f_lo_done, 1)
    for b in range(4):
        freed[b] += FFN // 2
    residual(PAN_DOWN, (4, 1), "final", split=False)

    invert(7, k.rstd)
    for m in range(KT):
        x = til(k.x, m)
        STT(out=x, in0=x, scalar=col(k, "final", m), in1=k.rstd[:], op0=ALU.mult, op1=ALU.mult).then_inc(k.s_out_ready, 1)


def program(nc, d, out):
    with ExitStack() as ctx:
        k = plan_memory(nc, ctx)
        signals(nc, ctx, k)
        block = ctx.enter_context(nc.Block())

        @block.sync
        def _(sp):
            sync_program(nc, k, d)
            for m in range(KT):
                sp.wait_ge(k.s_out_ready, m + 1)
                sp.dma_start(out[m * P:(m + 1) * P, :], til(k.x, m)).then_inc(k.s_out_sent, 16)
            sp.wait_ge(k.s_out_sent, 16 * KT)

        @block.gpsimd
        def _(pool):
            gpsimd_program(nc, k)

        @block.scalar
        def _(act):
            scalar_program(nc, k, d)

        @block.vector
        def _(dve):
            vector_program(nc, k)

        @block.tensor
        def _(pe):
            tensor_program(nc, k)


def constants():
    import numpy as np

    j, i = np.arange(P)[:, None], np.arange(P)[None, :]
    parts = [j == i, np.ones((P, P)), j // 64 == i // 64, j <= i]
    for lev in range(LEVELS):
        s = 1 << lev
        parts.append((j // (2 * s) == i // (2 * s)) & (j % (2 * s) < s) & (i % (2 * s) >= s))
    parts.append(np.zeros((P, T - P)))
    c = np.concatenate([p.astype(np.float32) for p in parts], 1)
    return np.concatenate([c, np.where(i <= j, 0.0, MASKED).astype(np.float32)], 1)


def panels(w):
    kk, m = w.shape
    return w.reshape(kk // P, P, m // P, P).transpose(2, 1, 0, 3).reshape(m // P, P, kk)


def kernel(**inputs):
    import numpy as np
    import concourse.bacc as bacc
    from concourse.bass_utils import run_bass_kernel_spmd

    a = {n: np.asarray(v) for n, v in inputs.items()}
    f = np.float32
    cat = np.concatenate
    w = a["w_in"][0]
    last = cat([w[:, 2440:2504], w[:, 2048:2056], w[:, 2504:2508], np.zeros((D, 52), f)], 1)
    w_in = cat([w[:, 0:2048], w[:, 2508:3020], w[:, 2056:2440], last], 1)
    kv = a["xa_wkv"][0]
    wk = panels(kv[:, 0:512])
    wv = kv[:, 512:].reshape(4, 2, P, T).transpose(0, 2, 1, 3).reshape(4, P, 2 * T)
    wo = panels(a["xa_wo"][0]).reshape(4, 2, P, T).transpose(0, 2, 1, 3).reshape(4, P, 2 * T)
    up = panels(a["mlp_w1"][0])
    dn = panels(a["mlp_w2"][0]).reshape(KT, P, 2, 2, D).transpose(2, 0, 3, 1, 4).reshape(2, 2 * KT, P, D)
    panels_a = cat([wk, wv, panels(w_in), panels(a["w_out"][0]), panels(a["xa_wq"][0]), wo,
                    up[:MTH], dn[0], up[MTH:], dn[1]], 0)
    w2 = panels(a["w_in_2"][0]).reshape(7, KT, P, D)
    lru = np.zeros((KT, 2, 64, 2, 2, 64), f)
    for n, name in enumerate(("lru_wa_2", "lru_wx_2")):
        g = a[name][0].reshape(KT, 2, 64, 64)
        for b in range(2):
            lru[:, b, :, n, b, :] = g[:, b]
    lru = lru.reshape(KT, P, 2 * P)
    mix = cat([w2[3], w2[4], w2[5], w2[6], lru, w2[0], w2[1], w2[2]], 2)
    merge = np.stack([panels(a["w_out_a_2"][0]), panels(a["w_out_b_2"][0])], 1).reshape(2 * KT, P, D)
    ffn = np.stack([panels(a["w_ffn_gate_2"][0]), panels(a["w_ffn_up_2"][0])], 1).reshape(2 * FFN, P, D)
    panels_b = cat([merge, panels(a["w_o_2"][0]), ffn], 0)
    down = panels(a["w_ffn_down_2"][0])
    kvb = a["dsa_w_kvb"][0]
    two = lambda m: m.reshape(2, P, 256).transpose(1, 0, 2).reshape(P, 512)
    small = cat([two(a["dsa_w_qb"][0]), two(a["dsa_w_qi"][0]), kvb[:, :64], kvb[:, :64], kvb[:, 64:]], 1)

    def cols(v):
        return v.reshape(-1, P).T

    def taps(v):
        n, c = v.shape
        return v.reshape(n, c // P, P).transpose(2, 1, 0).reshape(P, -1)

    def rows(v):
        return np.broadcast_to(np.tile(v, TT)[None], (P, 16))

    vec = cat([cols(a["norm_mix"]), cols(a["norm_mem"]), cols(a["norm_cross"]), cols(a["norm_mlp"]), cols(a["ln1_g_2"]),
               cols(a["ln2_g_2"]), cols(a["final_g_2"]), taps(a["gdn_conv"][0]), cols(a["gdn_norm"]),
               cols(np.tile(a["dsa_q_norm"], (1, 2))), cols(np.tile(a["dsa_k_norm"], (1, 2))), taps(a["conv_dw"][0]),
               cols(a["conv_dw_b"]), cols(a["conv_ln_g"]), cols(a["conv_ln_b"]), cols(a["xa_q_norm"]),
               cols(a["xa_k_norm"]), taps(a["conv_a_w_2"][0]), taps(a["conv_b_w_2"][0]), cols(a["conv_b_b_2"]),
               cols(a["lru_ba_2"]), cols(a["lru_bx_2"]), cols(a["lru_lambda_2"]), cols(a["gate_bias_2"]),
               rows(a["gdn_a_log"][0]), rows(a["gdn_dt_bias"][0])], 1)
    arrays = {
        "xT": a["x"][0].T, "memT": a["mem"][0].T, "const": constants(), "vec": vec, "small_w": small,
        "panels_a": panels_a, "mix": mix, "panels_b": panels_b, "down": down,
    }
    arrays = {n: np.ascontiguousarray(v) for n, v in arrays.items()}
    nc = bacc.Bacc("TRN2", target_bir_lowering=False, num_devices=1, dynamic_dma_scratch_size=1024)
    ap = {n: nc.dram_tensor(n, v.shape, F32, kind="ExternalInput").ap() for n, v in arrays.items()}
    d = Plan()
    d.x, d.mem, d.const, d.vec, d.small_w = ap["xT"], ap["memT"], ap["const"], ap["vec"], ap["small_w"]
    d.panels_a, d.mix, d.panels_b, d.down = ap["panels_a"], ap["mix"], ap["panels_b"], ap["down"]
    out = nc.dram_tensor("outT", (D, T), F32, kind="ExternalOutput").ap()
    program(nc, d, out)
    got = run_bass_kernel_spmd(nc, [arrays], core_ids=[0]).results[0]["outT"]
    return np.ascontiguousarray(got.T)[None]
```

```python
from contextlib import ExitStack

import concourse.bass as bass
from concourse import mybir

P = 128
T = 512
D = 1024
KT = D // P
MEM = 256
TT = T // P
HEADS = 4
EPS = 1e-6
BLK = 8
PANEL = BLK * P
RAW = 4
SPLIT = 2
LEVELS = 7
TOPK = 128
MASKED = -3.0e38
TAKEN = -3.3e38
MT1, MTH = 24, 16
FFN = 22
DOWN_CUTS = (0, 6, 12, 17, 22)
MIX_CUTS = (0, 7, 14, 21, 28, 36, 43, 50, 58)
MIX_TILES = [(0, 8), (8, 16), (16, 24), (24, 32), (34, 42), (42, 50), (50, 58)]
MIX_LAST = [next(p for p in range(8) if b <= MIX_CUTS[p + 1]) for _, b in MIX_TILES]
MIX_GATES = next(p for p in range(8) if 34 <= MIX_CUTS[p + 1])
CONV_TAPS = 31
PAD = 32
CQ, CKV, REST, UG, QKV, Z = 0, 2, 3, 4, 8, 20

F32 = mybir.dt.float32
F32R = mybir.dt.float32r
ACT = mybir.ActivationFunctionType
ALU = mybir.AluOpType
AX = mybir.AxisListType

VEC_WIDTHS = [
    ("norm_mix", 8), ("norm_mem", 8), ("norm_cross", 8), ("norm_mlp", 8), ("ln1", 8), ("ln2", 8), ("final", 8),
    ("gdn_conv", 48), ("gdn_norm", 1), ("dsa_q", 1), ("dsa_k", 1), ("dw", 2 * CONV_TAPS), ("dw_b", 2),
    ("cln_g", 2), ("cln_b", 2), ("xa_q", 1), ("xa_k", 1), ("conv_a", 24), ("conv_b", 32), ("conv_bb", 8),
    ("lru_ba", 8), ("lru_bx", 8), ("lam", 8), ("gate_b", 16), ("a_log", 16), ("dt_bias", 16),
]
VEC = {}
_at = 0
for _n, _w in VEC_WIDTHS:
    VEC[_n] = (_at, _w)
    _at += _w
NVEC = _at
C_ID, C_ONE, C_BLK, C_TRI, C_LEV = 0, P, 2 * P, 3 * P, 4 * P
C_CAUS = C_LEV + LEVELS * P
NCONST = C_CAUS + T


TOK_A, TOK_W, TOK_G, TOK_BETA, TOK_DEC, TOK_LAST = 0, 48, 64, 80, 96, 112
TOK_EDEC, TOK_EKD, TOK_ELAST, TOK_SP = 128, 144, 160, 176
TOK_N8, TOK_P8, TOK_RTOK, TOK_MX, TOK_NM, TOK_SUM, TOK_R, TOK_EA, TOK_M8 = 296, 304, 312, 320, 328, 336, 344, 352, 368
NTOK = 392


NORM_DQ, NORM_G, NORM_GO, NORM_AQ = 1, 4, 12, 16


class Count:

    def __init__(self, start=0):
        self.base, self.i, self.per, self.n = start, None, 0, 0

    def enter(self, i, per):
        self.base += self.n
        self.i, self.per, self.n = i, per, 0

    def leave(self, times):
        assert self.n == self.per, (self.n, self.per)
        self.base += times * self.per
        self.i, self.n = None, 0

    def at(self, k=0):
        v = self.base + self.n + k
        return v if self.i is None else self.i * self.per + v

    def step(self, k=1):
        self.n += k
        return self.at()


class Chain:

    def __init__(self, engine, sem):
        self.e, self.sem, self.c = engine, sem, Count()

    def __call__(self, ins):
        ins.then_inc(self.sem, 1)
        self.e.wait_ge(self.sem, self.c.step())
        return ins


class Plan:
    pass


def plan_memory(nc, ctx):
    k = Plan()

    top = [0]

    def sb(name, cols, dt=F32, at=None):
        cols = -(-cols // 8) * 8
        if at is None:
            at = top[0]
            top[0] += cols * 4
        return nc.alloc_sbuf_tensor_at(name, [P, cols], dt, offset=at), at + cols * 4

    base = (nc.sbuf_base + 63) // 64 * 64
    top[0] = base
    k.raw, _ = sb("raw", RAW * PANEL)
    k.w_hi, _ = sb("w_hi", SPLIT * PANEL, F32R)
    k.w_lo, _ = sb("w_lo", SPLIT * PANEL, F32R)
    k.x, _ = sb("x", KT * T)
    k.const, _ = sb("const", NCONST)
    k.vec, _ = sb("vec", NVEC)
    k.eps, _ = sb("eps", 4)
    k.rstd, _ = sb("rstd", T)
    k.sqacc, _ = sb("sqacc", T)
    k.sq, _ = sb("sq", 2 * T)
    k.tok, _ = sb("tok", NTOK)
    h0 = top[0]
    k.h_hi, _ = sb("h_hi", KT * T, F32R)
    k.h_lo, _ = sb("h_lo", KT * T, F32R)
    r0 = top[0]
    k.limit = nc.sbuf_usable_end
    k.proj, a = sb("proj", MT1 * T, at=r0)
    proj_end = a
    k.xk, a = sb("xk", HEADS * MEM, at=a)
    k.xv, a = sb("xv", 2 * T, at=a)
    q0 = a
    k.qkv, a = sb("qkv", 12 * T, at=q0)
    y0 = a
    k.mem, b = sb("mem", KT * MEM, at=q0)
    k.m_hi, b = sb("m_hi", KT * MEM, F32R, at=b)
    k.m_lo, b = sb("m_lo", KT * MEM, F32R, at=b)
    k.m_rstd, b = sb("m_rstd", MEM, at=b)
    k.m_sqa, _ = sb("m_sqa", MEM, at=b)
    k.y_hi, a = sb("y_hi", KT * T, F32R, at=y0)
    k.y_lo, a = sb("y_lo", KT * T, F32R, at=a)
    k.small_w, a = sb("small_w", 2 * 512 + P + 64, at=a)
    assert a <= k.limit, (a, k.limit)
    k.d_qi, b = sb("d_qi", 2 * T, at=h0)
    k.d_ki, b = sb("d_ki", T, at=b)
    k.d_relu, b = sb("d_relu", 2 * T, at=b)
    k.d_rk, b = sb("d_rk", T, at=b)
    k.d_v, b = sb("d_v", 2 * T, at=r0 + CQ * T * 4)
    k.d_score_a, b = sb("d_score_a", 5 * P, at=b)
    k.d_q, b = sb("d_q", 2 * T, at=r0 + UG * T * 4)
    k.d_k, b = sb("d_k", T, at=b)
    k.d_score_b, b = sb("d_score_b", T, at=b)
    assert b <= r0 + QKV * T * 4
    k.d_p, b = sb("d_p", 2 * T, at=y0)
    k.d_pt, b = sb("d_pt", 2 * T, at=b)
    k.c_acc, b = sb("c_acc", 2 * T, at=y0)
    k.c_t, b = sb("c_t", 2 * T, at=b)
    k.c_y, b = sb("c_y", 2 * (PAD + T), at=y0 + KT * T * 4)
    k.c_r, b = sb("c_r", T, at=b)
    assert b <= y0 + (KT + 4) * T * 4
    k.g_ek, b = sb("g_ek", HEADS * T, at=h0)
    k.g_kdec, b = sb("g_kdec", HEADS * T, at=b)
    k.g_v, b = sb("g_v", HEADS * T, at=b)
    k.g_at, b = sb("g_at", HEADS * T, at=b)
    assert b <= r0
    k.g_qk, b = sb("g_qk", HEADS * T, at=r0 + QKV * T * 4)
    k.g_x, b = sb("g_x", HEADS * T, at=b)
    k.g_xt, b = sb("g_xt", HEADS * T, at=b)
    k.g_b, _ = sb("g_b", 2 * T, at=y0)
    k.g_p, _ = sb("g_p", 2 * T, at=y0 + 2 * T * 4)
    k.g_vn, _ = sb("g_vn", 4 * P, at=y0 + KT * T * 4)
    k.g_s, _ = sb("g_s", 4 * P, at=y0 + KT * T * 4 + 4 * P * 4)
    k.g_d, _ = sb("g_d", T, at=y0 + KT * T * 4 + 8 * P * 4)
    k.g_r, _ = sb("g_r", T, at=y0 + KT * T * 4 + 12 * P * 4)
    k.a_q, b = sb("a_q", HEADS * T, at=r0)
    k.a_p, b = sb("a_p", 2 * T, at=b)
    k.a_pt, b = sb("a_pt", 2 * T, at=b)
    assert b <= proj_end
    k.ao_hi, b = sb("ao_hi", HEADS * T, F32R, at=q0)
    k.ao_lo, b = sb("ao_lo", HEADS * T, F32R, at=b)
    k.u_hi, b = sb("u_hi", MTH * T, F32R, at=r0)
    k.u_lo, b = sb("u_lo", MTH * T, F32R, at=b)
    k.u_t, b = sb("u_t", 4 * T, at=b)
    assert b <= k.limit
    k.ya_hi, b = sb("ya_hi", KT * T, F32R, at=r0)
    k.ya_lo, b = sb("ya_lo", KT * T, F32R, at=b)
    k.yb_hi, b = sb("yb_hi", KT * T, F32R, at=b)
    k.yb_lo, b = sb("yb_lo", KT * T, F32R, at=b)
    k.mg_hi, _ = sb("mg_hi", KT * T, F32R, at=b)
    k.mg_lo, _ = sb("mg_lo", KT * T, F32R, at=b + KT * T * 4)
    k.gates, b = sb("gates", 2 * KT * T, at=b)
    k.ub_hi, b = sb("ub_hi", T, F32R, at=b)
    k.ub_lo, b = sb("ub_lo", T, F32R, at=b)
    k.s_t, b = sb("s_t", 9 * T, at=b)
    assert b <= k.limit, (b, k.limit)
    k.f_hi, b = sb("f_hi", FFN * T, F32R, at=r0)
    k.f_lo, b = sb("f_lo", FFN * T, F32R, at=b)
    k.f_t, b = sb("f_t", 4 * T, at=b)
    assert b <= k.limit, (b, k.limit)
    k.ps = [ctx.enter_context(nc.psum_tensor(f"acc{i}", [P, T], F32)) for i in range(8)]
    return k


def signals(nc, ctx, k):

    def sem(name):
        return ctx.enter_context(nc.semaphore(name))

    k.s_ld_x = sem("ld_x")
    k.s_ld_mem = sem("ld_mem")
    k.s_ld_const = sem("ld_const")
    k.s_ld_vec = sem("ld_vec")
    k.s_ld_small = sem("ld_small")
    k.s_split_done = sem("split_done")
    k.s_weights_hi = sem("weights_hi")
    k.s_panel_used = sem("panel_used")
    k.s_fed_hi = sem("fed_hi")
    k.s_fed_sq = sem("fed_sq")
    k.s_fed_lo = sem("fed_lo")
    k.s_sq_used = sem("sq_used")
    k.s_ssq = sem("ssq")
    k.s_std = sem("std")
    k.s_rstd = sem("rstd")
    k.s_x_new = sem("x_new")
    k.s_zeroed = sem("zeroed")
    k.s_act_chain = sem("act_chain")
    k.s_dve_chain = sem("dve_chain")
    k.s_xk_raw = sem("xk_raw")
    k.s_tokr_t = sem("tokr_t")
    k.s_v_done = sem("v_done")
    k.s_xk_done = sem("xk_done")
    k.s_unit_sq = sem("unit_sq")
    k.s_unit_sum = sem("unit_sum")
    k.s_unit_std = sem("unit_std")
    k.s_proj_done = sem("proj_done")
    k.s_ki_dup = sem("ki_dup")
    k.s_dq_mm = sem("dq_mm")
    k.s_dq_raw = sem("dq_raw")
    k.s_d_gates = sem("d_gates")
    k.s_d_gates_tok = sem("d_gates_tok")
    k.s_dq_done = sem("dq_done")
    k.s_dv_done = sem("dv_done")
    k.s_idx_mm = sem("idx_mm")
    k.s_idx_relu = sem("idx_relu")
    k.s_idx_used = sem("idx_used")
    k.s_lg_mm = sem("lg_mm")
    k.s_lg_masked = sem("lg_masked")
    k.s_p_exp = sem("p_exp")
    k.s_p_norm = sem("p_norm")
    k.s_pt_mm = sem("pt_mm")
    k.s_pt_copied = sem("pt_copied")
    k.s_o_mm = sem("o_mm")
    k.s_y_hi = sem("y_hi")
    k.s_y_lo = sem("y_lo")
    k.s_c_sig = sem("c_sig")
    k.s_c_conv = sem("c_conv")
    k.s_c_mean = sem("c_mean")
    k.s_c_cent = sem("c_cent")
    k.s_c_sq = sem("c_sq")
    k.s_c_var = sem("c_var")
    k.s_c_std = sem("c_std")
    k.s_c_norm = sem("c_norm")
    k.s_c_silu = sem("c_silu")
    k.s_g_conv = sem("g_conv")
    k.s_g_silu = sem("g_silu")
    k.s_g_qk_done = sem("g_qk_done")
    k.s_sp_in = sem("sp_in")
    k.s_sp_exp = sem("sp_exp")
    k.s_beta_done = sem("beta_done")
    k.s_g_ready = sem("g_ready")
    k.s_dec_mm = sem("dec_mm")
    k.s_dec_copied = sem("dec_copied")
    k.s_dec_exp = sem("dec_exp")
    k.s_gb_done = sem("gb_done")
    k.s_decrow = sem("decrow")
    k.s_gam_d = sem("gam_d")
    k.s_gam_e = sem("gam_e")
    k.s_edecrow = sem("edecrow")
    k.s_gam_done = sem("gam_done")
    k.s_qk_mm = sem("qk_mm")
    k.s_qk_done = sem("qk_done")
    k.s_kk_mm = sem("kk_mm")
    k.s_at_done = sem("at_done")
    k.s_kt_mm = sem("kt_mm")
    k.s_ek_done = sem("ek_done")
    k.s_vt_mm = sem("vt_mm")
    k.s_v_tok_done = sem("v_tok_done")
    k.s_x_init = sem("x_init")
    k.s_x_turned = sem("x_turned")
    k.s_x_first = sem("x_first")
    k.s_bt_done = sem("bt_done")
    k.s_p_mm = sem("p_mm")
    k.s_p_copied = sem("p_copied")
    k.s_xp_mm = sem("xp_mm")
    k.s_x_done = sem("x_done")
    k.s_wt_mm = sem("wt_mm")
    k.s_wt_done = sem("wt_done")
    k.s_vn_mm = sem("vn_mm")
    k.s_vn_done = sem("vn_done")
    k.s_o_part = sem("o_part")
    k.s_st_mm = sem("st_mm")
    k.s_st_done = sem("st_done")
    k.s_o_copied = sem("o_copied")
    k.s_go_norm = sem("go_norm")
    k.s_z_silu = sem("z_silu")
    k.s_aq_raw = sem("aq_raw")
    k.s_aq_done = sem("aq_done")
    k.s_al_mm = sem("al_mm")
    k.s_al_max = sem("al_max")
    k.s_al_exp = sem("al_exp")
    k.s_al_norm = sem("al_norm")
    k.s_apt_mm = sem("apt_mm")
    k.s_apt_copied = sem("apt_copied")
    k.s_av_mm = sem("av_mm")
    k.s_ao_hi_done = sem("ao_hi_done")
    k.s_ao_lo_done = sem("ao_lo_done")
    k.s_up_relu = sem("up_relu")
    k.s_up_sq = sem("up_sq")
    k.s_up_hi = sem("up_hi")
    k.s_up_lo = sem("up_lo")
    k.s_s2_u = sem("s2_u")
    k.s_s2_uhi = sem("s2_uhi")
    k.s_s2_ulo = sem("s2_ulo")
    k.s_s2_gl = sem("s2_gl")
    k.s_s2_gsq = sem("s2_gsq")
    k.s_s2_gt = sem("s2_gt")
    k.s_s2_gsig = sem("s2_gsig")
    k.s_s2_gate = sem("s2_gate")
    k.s_s2_gate_done = sem("s2_gate_done")
    k.s_s2_r = sem("s2_r")
    k.s_s2_i = sem("s2_i")
    k.s_s2_a = sem("s2_a")
    k.s_s2_th = sem("s2_th")
    k.s_s2_a2 = sem("s2_a2")
    k.s_s2_m = sem("s2_m")
    k.s_s2_s = sem("s2_s")
    k.s_s2_yb = sem("s2_yb")
    k.s_s2_yb_hi = sem("s2_yb_hi")
    k.s_s2_ya = sem("s2_ya")
    k.s_s2_ya_hi = sem("s2_ya_hi")
    k.s_s2_free = sem("s2_free")
    k.s_mg = sem("mg")
    k.s_mg_hi = sem("mg_hi")
    k.s_mg_lo = sem("mg_lo")
    k.s_f_g = sem("f_g")
    k.s_f_silu = sem("f_silu")
    k.s_f_hid = sem("f_hid")
    k.s_f_hi_done = sem("f_hi_done")
    k.s_f_lo_done = sem("f_lo_done")
    k.s_out_ready = sem("out_ready")
    k.s_out_sent = sem("out_sent")
    k.landed = [sem(f"landed{j}") for j in range(RAW)]
    k.acc_free = [sem(f"acc_free{b}") for b in range(8)]


STREAM = [("panels_a", 28, [PANEL] * 4),
          ("mix", 8, [(b - a) * P for a, b in zip(MIX_CUTS, MIX_CUTS[1:])]),
          ("panels_b", 17, [PANEL] * 4),
          ("down", 8, [(b - a) * P for a, b in zip(DOWN_CUTS, DOWN_CUTS[1:])])]


class Panels(Count):

    def landed(self):
        v = 16 * (self.base // RAW) + 16 * (self.n // RAW) + 16
        return v if self.i is None else self.i * (16 * (self.per // RAW)) + v


def col(k, name, j=0, rows=slice(0, P)):
    at = VEC[name][0] + j
    return k.vec[rows, at:at + 1]


def til(buf, j, n=1, w=T):
    return buf[:, j * w:(j + n) * w]


def rtil(buf, j, w=T):
    return buf[:, bass.ds(j * w, w)]


def sync_program(nc, k, d):
    e = nc.sync
    e.dma_start(k.vec[:, 0:NVEC], d.vec).then_inc(k.s_ld_vec, 16)
    e.dma_start(k.mem[:].rearrange("p (k t) -> p k t", k=KT), d.mem.rearrange("(k p) t -> p k t", p=P)).then_inc(k.s_ld_mem, 16)
    e.dma_start(k.const[:], d.const).then_inc(k.s_ld_const, 16)
    pan = Panels()
    first = True
    for name, times, widths in STREAM:
        src = stream_array(d, name)
        with e.Fori(0, times) as i:
            pan.enter(i, len(widths))
            at = 0
            for j, w in enumerate(widths):
                e.wait_ge(k.s_split_done, pan.at(1))
                if name in ("panels_a", "panels_b"):
                    part = src[bass.ds(i * 4 + j, 1)].rearrange("a p n -> (a p) n")
                else:
                    part = src[bass.ds(i, 1)].rearrange("a p n -> (a p) n")[:, at:at + w]
                e.dma_start(k.raw[:, (j % RAW) * PANEL:(j % RAW) * PANEL + w], part).then_inc(k.landed[j % RAW], 16)
                at += w
                pan.step()
            pan.leave(times)


def stream_array(d, name):
    return {"panels_a": d.panels_a, "mix": d.mix, "panels_b": d.panels_b, "down": d.down}[name]


def gpsimd_program(nc, k):
    e = nc.gpsimd
    e.sem_inc(k.s_split_done, RAW)
    one = k.const[:, C_ONE:C_ONE + 1]
    e.wait_ge(k.s_ld_const, 16)
    pan = Panels()
    for name, times, widths in STREAM:
        with e.Fori(0, times) as i:
            pan.enter(i, len(widths))
            for j, w in enumerate(widths):
                raw = k.raw[:, (j % RAW) * PANEL:(j % RAW) * PANEL + w]
                hi = k.w_hi[:, (j % SPLIT) * PANEL:(j % SPLIT) * PANEL + w]
                lo = k.w_lo[:, (j % SPLIT) * PANEL:(j % SPLIT) * PANEL + w]
                e.wait_ge(k.landed[j % RAW], pan.landed())
                e.wait_ge(k.s_panel_used, pan.at(1))
                e.tensor_tensor(hi, raw, one.broadcast_to([P, w]), ALU.mult).then_inc(k.s_weights_hi, 1)
                e.wait_ge(k.s_weights_hi, pan.at(1))
                e.tensor_tensor(lo, raw, hi.bitcast(F32), ALU.subtract).then_inc(k.s_split_done, 1)
                pan.step()
            pan.leave(times)


class Acc:

    def __init__(self, k):
        self.k, self.c = k, [Count() for _ in range(8)]

    def enter(self, i, per):
        for c, n in zip(self.c, per):
            c.enter(i, n)

    def leave(self, times):
        for c in self.c:
            c.leave(times)

    def take(self, e, b):
        e.wait_ge(self.k.acc_free[b], self.c[b].step())
        return self.k.ps[b]


def tensor_program(nc, k):
    e = nc.tensor
    pan, acc = Panels(), Acc(k)
    e.sem_inc(k.s_panel_used, SPLIT)
    ident = k.const[:, C_ID:C_ID + P]
    ones = k.const[:, C_ONE:C_ONE + P]
    blk = k.const[:, C_BLK:C_BLK + P]
    tri = k.const[:, C_TRI:C_TRI + P]

    def products(out, w_at, wn, a_hi, a_lo, first, last):
        for n, (w, a) in enumerate(((k.w_hi, a_hi), (k.w_hi, a_lo), (k.w_lo, a_hi))):
            mm = e.matmul(out, w[:, w_at:w_at + wn], a, start=first and n == 0, stop=last and n == 2)
        return mm

    def panel(out, hi, lo, tiles, first=True, last=True, at=0, done=True, w=T):
        slot = (pan.n % SPLIT) * PANEL
        if at == 0:
            e.wait_ge(k.s_split_done, RAW + pan.at(1))
        for n, t in enumerate(tiles):
            mm = products(out, slot + (at + n) * P, P, hi[:, t * w:(t + 1) * w], lo[:, t * w:(t + 1) * w],
                          first and n == 0, last and n == len(tiles) - 1)
        if done:
            mm.then_inc(k.s_panel_used, 1)
            pan.step()

    def sum_squares(n_fed, n_norm, sqacc, w=T):
        e.wait_ge(k.s_sq_used, 2 + n_fed)
        if n_norm > 0:
            e.wait_ge(k.s_std, n_norm)
        e.matmul(k.ps[7][:, 0:w], ones, sqacc[:, 0:w], start=True, stop=True).then_inc(k.s_ssq, 1)

    e.wait_ge(k.s_ld_const, 16)
    sum_squares(KT, 0, k.m_sqa, MEM)
    e.wait_ge(k.s_fed_lo, KT)
    for m in range(HEADS):
        out = acc.take(e, m % 2)
        panel(out[:, 0:MEM], k.m_hi, k.m_lo, range(KT), w=MEM)
    for b in (2, 3):
        acc.take(e, b)
    for j in range(4):
        e.wait_ge(k.s_split_done, RAW + pan.at(1))
        slot = (pan.n % SPLIT) * PANEL
        for kk in range(2):
            t = 2 * j + kk
            for mt in range(2):
                a = t * MEM + mt * P
                for n, (m_, w) in enumerate(((k.m_hi, k.w_hi), (k.m_hi, k.w_lo), (k.m_lo, k.w_hi))):
                    mm = e.matmul(k.ps[2 + mt][:], m_[:, a:a + P], w[:, slot + kk * T:slot + (kk + 1) * T],
                                  start=t == 0 and n == 0, stop=t == KT - 1 and n == 2)
        mm.then_inc(k.s_panel_used, 1)
        pan.step()
    e.wait_ge(k.s_rstd, 1)
    for mt in range(2):
        mm = e.transpose(k.ps[4][:, mt * P:(mt + 1) * P], k.m_rstd[:, mt * P:(mt + 1) * P], ident)
    mm.then_inc(k.s_tokr_t, 1)
    e.wait_ge(k.s_unit_sq, 1)
    for j in range(2):
        mm = e.matmul(k.ps[5 + j][:], ones, k.mem[:, j * T:(j + 1) * T], start=True, stop=True)
    mm.then_inc(k.s_unit_sum, 1)

    sum_squares(2 * KT, 1, k.sqacc)
    e.wait_ge(k.s_fed_lo, 2 * KT)
    with e.Fori(0, 6) as i:
        pan.enter(i, 4)
        acc.enter(i, [1, 1, 1, 1, 0, 0, 0, 0])
        for j in range(4):
            panel(acc.take(e, j)[:], k.h_hi, k.h_lo, range(KT))
        pan.leave(6)
        acc.leave(6)

    e.wait_ge(k.s_proj_done, 1)
    e.wait_ge(k.s_ld_small, 16)
    for b in range(4):
        e.wait_ge(k.acc_free[b], acc.c[b].at(1))
    for m in range(4):
        for kk in range(2):
            w_at = (0 if m < 2 else 512) + kk * 256 + (m % 2) * P
            mm = e.matmul(k.ps[m][:], k.small_w[:, w_at:w_at + P], til(k.proj, CQ + kk), start=kk == 0, stop=kk == 1)
        mm.then_inc(k.s_dq_mm, 1)
    e.wait_ge(k.s_v_done, 2)
    e.matmul(k.ps[4][:], k.small_w[:, 1024:1152], til(k.proj, CKV), start=True, stop=True).then_inc(k.s_dq_mm, 1)
    e.wait_ge(k.s_unit_std, 1)
    for t in range(TT):
        mm = e.matmul(k.ps[5][:, t * 64:(t + 1) * 64], k.proj[:, CKV * T + t * P:CKV * T + (t + 1) * P],
                      k.small_w[:, 1152:1216], start=True, stop=True)
    mm.then_inc(k.s_dq_mm, 1)
    for c in range(TT):
        mm = e.transpose(k.ps[6][:, c * P:(c + 1) * P], k.proj[:, REST * T + c * P:REST * T + (c + 1) * P], ident)
    mm.then_inc(k.s_d_gates, 1)
    e.wait_ge(k.s_d_gates_tok, 1)
    for j in range(2):
        e.wait_ge(k.s_c_conv, j + 1)
        mm = e.matmul(k.ps[6][:], ones, til(k.c_acc, j), start=j == 0, stop=j == 1)
    mm.then_inc(k.s_c_mean, 1)
    for m in range(3):
        e.wait_ge(k.s_unit_sq, NORM_DQ + m + 1)
        e.wait_ge(k.s_dq_raw, (1, 2, 5)[m])
        src = til(k.d_relu, m) if m < 2 else k.d_rk[:]
        e.matmul(k.ps[(0, 1, 4)[m]][:], blk, src, start=True, stop=True).then_inc(k.s_unit_sum, 1)
    e.wait_ge(k.s_std, 2)
    for j in range(2):
        e.wait_ge(k.s_c_sq, j + 1)
        mm = e.matmul(k.ps[7][:], ones, til(k.c_t, j), start=j == 0, stop=j == 1)
    mm.then_inc(k.s_c_var, 1)

    e.wait_ge(k.s_unit_std, NORM_DQ + 3)
    e.wait_ge(k.s_dv_done, 1)
    e.wait_ge(k.s_c_cent, 2)
    e.wait_ge(k.s_c_std, 1)
    for m in range(2 * HEADS):
        e.wait_ge(k.s_unit_sq, NORM_G + m + 1)
        if m >= 4:
            e.wait_ge(k.s_unit_std, NORM_G + m - 3)
        e.matmul(k.ps[4 + m % 4][:], ones, til(k.sq, m % 2), start=True, stop=True).then_inc(k.s_unit_sum, 1)

    e.wait_ge(k.s_ki_dup, 32)
    e.wait_ge(k.s_dq_raw, 5)
    for qt in range(1, TT):
        cw = (qt + 1) * P
        for h in range(HEADS):
            if qt > 1:
                e.wait_ge(k.s_idx_relu, HEADS * (qt - 2) + h + 1)
            r = slice(64 * (h % 2), 64 * (h % 2) + 64)
            e.matmul(k.ps[h][:, 0:cw], k.d_qi[r, (h // 2) * T + qt * P:(h // 2) * T + (qt + 1) * P],
                     k.d_ki[r, 0:cw], start=True, stop=True).then_inc(k.s_idx_mm, 1)

    e.wait_ge(k.s_unit_std, NORM_G + 2 * HEADS)
    e.wait_ge(k.s_g_ready, 1)
    e.matmul(k.ps[7][:, 0:16], tri, k.tok[:, TOK_G:TOK_G + 16], start=True, stop=True)
    e.matmul(k.ps[7][:, 16:32], ones, k.tok[:, TOK_G:TOK_G + 16], start=True, stop=True).then_inc(k.s_dec_mm, 1)
    e.wait_ge(k.s_idx_relu, 3 * HEADS)
    for h in range(HEADS):
        e.wait_ge(k.s_gb_done, h + 1)
        for c in range(TT):
            at = h * T + c * P
            mm = e.matmul(k.ps[h][:, c * P:(c + 1) * P], k.g_x[:, at:at + P], tri, start=True, stop=True)
        mm.then_inc(k.s_decrow, 1)
    e.wait_ge(k.s_g_qk_done, 2 * HEADS)
    for h in range(HEADS):
        if h >= 1:
            e.wait_ge(k.s_qk_done, h)
        for c in range(TT):
            at = c * P
            mm = e.matmul(k.ps[4][:, at:at + P], til(k.qkv, 4 + h)[:, at:at + P], til(k.qkv, h)[:, at:at + P],
                          start=True, stop=True)
        mm.then_inc(k.s_qk_mm, 1)
        if h >= 1:
            e.wait_ge(k.s_at_done, h)
        for c in range(TT):
            at = c * P
            mm = e.matmul(k.ps[5][:, at:at + P], til(k.qkv, 4 + h)[:, at:at + P], til(k.qkv, 4 + h)[:, at:at + P],
                          start=True, stop=True)
        mm.then_inc(k.s_kk_mm, 1)
        if h >= 1:
            e.wait_ge(k.s_ek_done, h)
        for c in range(TT):
            mm = e.transpose(k.ps[6][:, c * P:(c + 1) * P], til(k.qkv, 4 + h)[:, c * P:(c + 1) * P], ident)
        mm.then_inc(k.s_kt_mm, 1)
        if h >= 1:
            e.wait_ge(k.s_v_tok_done, h)
        else:
            e.wait_ge(k.s_dec_copied, 1)
        for c in range(TT):
            mm = e.transpose(k.ps[7][:, c * P:(c + 1) * P], til(k.qkv, 8 + h)[:, c * P:(c + 1) * P], ident)
        mm.then_inc(k.s_vt_mm, 1)
    e.wait_ge(k.s_gam_done, 2 * HEADS)
    e.wait_ge(k.s_edecrow, HEADS)
    e.wait_ge(k.s_qk_done, HEADS)
    e.wait_ge(k.s_at_done, HEADS)
    for h in range(HEADS):
        e.wait_ge(k.s_x_init, h + 1)
        for c in range(TT):
            mm = e.transpose(k.ps[h][:, c * P:(c + 1) * P], k.g_xt[:, h * T + c * P:h * T + (c + 1) * P], ident)
        mm.then_inc(k.s_x_turned, 1)
    e.wait_ge(k.s_x_first, HEADS)

    def level(lev, last):
        for h in range(HEADS):
            u = lev * HEADS + h + 1
            e.wait_ge(k.s_bt_done, u)
            e.wait_ge(k.s_p_copied, u)
            e.wait_ge(k.s_x_done, u)
            b = (h % 2) * T
            for c in range(TT):
                at = c * P
                mm = e.matmul(k.ps[h % 2][:, at:at + P], k.g_b[:, b + at:b + at + P],
                              til(k.g_x, h)[:, at:at + P], start=True, stop=True)
            mm.then_inc(k.s_p_mm, 1)
            e.wait_ge(k.s_p_copied, u + 2)
            e.wait_ge(k.s_x_done, u + 2)
            for c in range(0 if last else TT):
                at = c * P
                e.matmul(k.ps[2 + h % 2][:, at:at + P], til(k.g_xt, h)[:, at:at + P],
                         k.g_p[:, b + at:b + at + P], start=True, stop=True)
            for c in range(TT):
                at = c * P
                mm = e.matmul(k.ps[4 + h % 2][:, at:at + P], k.g_p[:, b + at:b + at + P],
                              til(k.g_xt, h)[:, at:at + P], start=True, stop=True)
            mm.then_inc(k.s_xp_mm, 1)

    with e.Fori(0, LEVELS - 2) as lev:
        level(lev, False)
    level(LEVELS - 2, True)
    U = (LEVELS - 1) * HEADS
    e.wait_ge(k.s_x_done, HEADS + U)
    e.wait_ge(k.s_ek_done, HEADS)
    e.wait_ge(k.s_v_tok_done, HEADS)
    for h in range(HEADS):
        if h >= 2:
            e.wait_ge(k.s_wt_done, h - 1)
        for c in range(TT):
            at = h * T + c * P
            mm = e.matmul(k.ps[6 + h % 2][:, c * P:(c + 1) * P], k.g_ek[:, at:at + P], k.g_xt[:, at:at + P],
                          start=True, stop=True)
        mm.then_inc(k.s_wt_mm, 1)
    e.wait_ge(k.s_wt_done, HEADS)

    def logits(qt, h):
        cw, u = (qt + 1) * P, qt * HEADS + h
        if u >= 2:
            e.wait_ge(k.s_lg_masked, u - 1)
        r = slice(64 * (h % 2), 64 * (h % 2) + 64)
        e.matmul(k.ps[4 + h % 2][:, 0:cw], k.d_q[r, (h // 2) * T + qt * P:(h // 2) * T + (qt + 1) * P],
                 k.d_k[r, 0:cw], start=True, stop=True).then_inc(k.s_lg_mm, 1)

    def outputs(qt, h):
        u = qt * HEADS + h
        e.wait_ge(k.s_p_norm, u + 1)
        for t in range(qt + 1):
            mm = e.transpose(k.ps[6][:, t * P:(t + 1) * P],
                             k.d_p[:, (h % 2) * T + t * P:(h % 2) * T + (t + 1) * P], ident)
        mm.then_inc(k.s_pt_mm, 1)
        e.wait_ge(k.s_pt_copied, u + 1)
        if qt and h == 0:
            e.wait_ge(k.s_y_lo, 2 + qt)
        for t in range(qt + 1):
            mm = e.matmul(k.ps[7][:, (h // 2) * P:(h // 2 + 1) * P],
                          k.d_v[:, (2 * t + h % 2) * P:(2 * t + h % 2 + 1) * P],
                          k.d_pt[:, (h % 2) * T + t * P:(h % 2) * T + (t + 1) * P],
                          start=h % 2 == 0 and t == 0, stop=h % 2 == 1 and t == qt)
        if h == HEADS - 1:
            mm.then_inc(k.s_o_mm, 1)

    for c in range(TT):
        e.wait_ge(k.s_st_done, c + 1)
        for h in range(HEADS):
            at = h * T + c * P
            out = k.ps[c % 2][:, h * P:(h + 1) * P]
            e.matmul(out, k.g_xt[:, at:at + P], k.g_v[:, at:at + P], start=True, stop=False)
            mm = e.matmul(out, til(k.qkv, 4 + h)[:, c * P:(c + 1) * P], k.g_s[:, h * P:(h + 1) * P],
                          start=False, stop=True)
        mm.then_inc(k.s_vn_mm, 1)
        logits(c, 0)
        logits(c, 1)
        e.wait_ge(k.s_vn_done, c + 1)
        if c:
            e.wait_ge(k.s_o_copied, c)
        for h in range(HEADS):
            at = h * T + c * P
            out = k.ps[2][:, h * P:(h + 1) * P]
            vn = k.g_vn[:, h * P:(h + 1) * P]
            e.matmul(out, k.g_s[:, h * P:(h + 1) * P], til(k.qkv, h)[:, c * P:(c + 1) * P], start=True, stop=False)
            mm = e.matmul(out, vn, k.g_qk[:, at:at + P], start=False, stop=True)
        mm.then_inc(k.s_o_part, 1)
        for h in range(HEADS):
            at = h * T + c * P
            mm = e.matmul(k.ps[3][:, h * P:(h + 1) * P], k.g_kdec[:, at:at + P], k.g_vn[:, h * P:(h + 1) * P],
                          start=True, stop=True)
        mm.then_inc(k.s_st_mm, 1)
        for h in range(HEADS):
            outputs(c, h)
            if h + 2 < HEADS:
                logits(c, h + 2)
    e.wait_ge(k.s_st_done, TT + 1)
    for h in range(HEADS):
        e.wait_ge(k.s_unit_sq, NORM_GO + h + 1)
        e.matmul(k.ps[h][:], ones, til(k.g_x, h), start=True, stop=True).then_inc(k.s_unit_sum, 1)

    e.wait_ge(k.s_y_lo, 2 + TT + HEADS)
    e.wait_ge(k.s_unit_std, NORM_GO + HEADS)
    with e.Fori(0, 2) as i:
        pan.enter(i, 4)
        acc.enter(i, [2, 2, 0, 0, 0, 0, 0, 0])
        for j in range(4):
            panel(acc.take(e, j % 2)[:], k.y_hi, k.y_lo, range(KT))
        pan.leave(2)
        acc.leave(2)

    sum_squares(3 * KT, 2, k.sqacc)
    e.wait_ge(k.s_fed_lo, 3 * KT)
    for j in range(4):
        panel(acc.take(e, j)[:], k.h_hi, k.h_lo, range(KT))
    for h in range(HEADS):
        e.wait_ge(k.s_unit_sq, NORM_AQ + h + 1)
        e.matmul(k.ps[4 + h % 2][:], ones, til(k.sq, h % 2), start=True, stop=True).then_inc(k.s_unit_sum, 1)
        e.wait_ge(k.s_unit_std, NORM_AQ + h + 1)
    e.wait_ge(k.s_aq_done, HEADS)
    e.wait_ge(k.s_xk_done, 1)
    for h in range(HEADS):
        for half in range(2):
            u = 2 * h + half
            if u >= 2:
                e.wait_ge(k.s_al_exp, u - 1)
            for n in range(2):
                qt = 2 * half + n
                mm = e.matmul(k.ps[half][:, n * MEM:(n + 1) * MEM], til(k.a_q, h)[:, qt * P:(qt + 1) * P],
                              k.xk[:, h * MEM:(h + 1) * MEM], start=True, stop=True)
            mm.then_inc(k.s_al_mm, 1)
        e.wait_ge(k.s_al_norm, 2 * h + 2)
        if h:
            e.wait_ge(k.s_apt_copied, 2 * h)
        for mt in range(2):
            for qt in range(TT):
                at = qt * MEM + mt * P
                mm = e.transpose(k.ps[2 + mt][:, qt * P:(qt + 1) * P], k.a_p[:, at:at + P], ident)
            mm.then_inc(k.s_apt_mm, 1)
        if h >= 2:
            e.wait_ge(k.s_ao_lo_done, h - 1)
        for mt in range(2):
            e.wait_ge(k.s_apt_copied, 2 * h + mt + 1)
            mm = e.matmul(k.ps[4 + h % 2][:], k.xv[:, mt * T + h * P:mt * T + (h + 1) * P], til(k.a_pt, mt),
                          start=mt == 0, stop=mt == 1)
        mm.then_inc(k.s_av_mm, 1)
    e.wait_ge(k.s_ao_lo_done, HEADS)
    for j in range(4):
        for n in range(2):
            panel(acc.take(e, n)[:], k.ao_hi, k.ao_lo, range(HEADS), at=HEADS * n, done=n == 1)

    sum_squares(4 * KT, 3, k.sqacc)
    e.wait_ge(k.s_fed_lo, 4 * KT)
    for half in range(2):
        with e.Fori(0, MTH // 4) as i:
            pan.enter(i, 4)
            acc.enter(i, [2, 2, 0, 0, 0, 0, 0, 0])
            for j in range(4):
                panel(acc.take(e, j % 2)[:], k.h_hi, k.h_lo, range(KT))
            pan.leave(MTH // 4)
            acc.leave(MTH // 4)
        e.wait_ge(k.s_up_lo, MTH * (half + 1))
        with e.Fori(0, KT // 2) as i:
            pan.enter(i, 4)
            acc.enter(i, [1, 1, 0, 0, 0, 0, 0, 0])
            for j in range(2):
                out = acc.take(e, j)[:]
                panel(out, k.u_hi, k.u_lo, range(0, 8), last=False)
                panel(out, k.u_hi, k.u_lo, range(8, 16), first=False)
            pan.leave(KT // 2)
            acc.leave(KT // 2)

    sum_squares(5 * KT, 4, k.sqacc)
    e.wait_ge(k.s_fed_lo, 5 * KT)
    with e.Fori(0, KT) as i:
        pan.enter(i, 8)
        acc.enter(i, [2, 1, 1, 1, 1, 1, 1, 1])
        blocks = [(b, k.h_hi, k.h_lo, t, t == 0, t == KT - 1) for b in (0, 1, 4, 5) for t in range(KT)]
        blocks += [(b, k.ub_hi, k.ub_lo, 0, True, True) for b in (2, 3)]
        blocks += [(b, k.h_hi, k.h_lo, t, t == 0, t == KT - 1) for b in (6, 7, 0) for t in range(KT)]
        for a, b in zip(MIX_CUTS, MIX_CUTS[1:]):
            e.wait_ge(k.s_split_done, RAW + pan.at(1))
            slot = (pan.n % SPLIT) * PANEL
            for n, (bank, hi, lo, t, first, last) in enumerate(blocks[a:b]):
                if bank == 2:
                    e.wait_ge(k.s_s2_ulo, i + 1)
                out = acc.take(e, bank) if first else k.ps[bank]
                mm = products(out[:], slot + n * P, P, til(hi, t), til(lo, t), first, last)
            mm.then_inc(k.s_panel_used, 1)
            pan.step()
        pan.leave(KT)
        acc.leave(KT)

    e.wait_ge(k.s_s2_free, KT)
    with e.Fori(0, KT // 2) as i:
        pan.enter(i, 4)
        acc.enter(i, [1, 1, 1, 1, 0, 0, 0, 0])
        for j in range(2):
            panel(acc.take(e, 2 * j)[:], k.ya_hi, k.ya_lo, range(KT))
            panel(acc.take(e, 2 * j + 1)[:], k.yb_hi, k.yb_lo, range(KT))
        pan.leave(KT // 2)
        acc.leave(KT // 2)

    e.wait_ge(k.s_mg_lo, KT)
    with e.Fori(0, 2) as i:
        pan.enter(i, 4)
        acc.enter(i, [2, 2, 0, 0, 0, 0, 0, 0])
        for j in range(4):
            panel(acc.take(e, j % 2)[:], k.mg_hi, k.mg_lo, range(KT))
        pan.leave(2)
        acc.leave(2)

    sum_squares(6 * KT, 5, k.sqacc)
    e.wait_ge(k.s_fed_lo, 6 * KT)
    with e.Fori(0, FFN // 2) as i:
        pan.enter(i, 4)
        acc.enter(i, [1, 1, 1, 1, 0, 0, 0, 0])
        for j in range(4):
            panel(acc.take(e, j)[:], k.h_hi, k.h_lo, range(KT))
        pan.leave(FFN // 2)
        acc.leave(FFN // 2)
    e.wait_ge(k.s_f_lo_done, FFN)
    with e.Fori(0, KT // 2) as i:
        pan.enter(i, 8)
        acc.enter(i, [1, 1, 0, 0, 0, 0, 0, 0])
        for j in range(2):
            out = acc.take(e, j)[:]
            for a, b in zip(DOWN_CUTS, DOWN_CUTS[1:]):
                panel(out, k.f_hi, k.f_lo, range(a, b), first=a == 0, last=b == FFN)
        pan.leave(KT // 2)
        acc.leave(KT // 2)
    sum_squares(7 * KT, 6, k.sqacc)


def scalar_program(nc, k, d):
    e = nc.scalar
    A = e.activation
    chain = Chain(e, k.s_act_chain)
    e.dma_start(k.x[:].rearrange("p (k t) -> p k t", k=KT), d.x.rearrange("(k p) t -> p k t", p=P)).then_inc(k.s_ld_x, 16)
    e.dma_start(k.small_w[:], d.small_w).then_inc(k.s_ld_small, 16)
    fed = Count()

    def feed(src, gain, hi, w=T, split=True):
        e.wait_ge(k.s_sq_used, fed.at(1))
        if split:
            A(hi, src, ACT.Copy, scale=gain).then_inc(k.s_fed_hi, 1)
        A(k.sq[:, (fed.n % 2) * T:(fed.n % 2) * T + w], src, ACT.Square).then_inc(k.s_fed_sq, 1)
        fed.step()

    def root(n_norm, dst, w=T):
        e.wait_ge(k.s_ssq, n_norm)
        A(dst[:, 0:w], k.ps[7][:, 0:w], ACT.Sqrt, bias=k.eps[:, 0:1], scale=1.0 / D).then_inc(k.s_std, 1)

    e.wait_ge(k.s_ld_vec, 16)
    e.wait_ge(k.s_ld_mem, 16)
    for m in range(KT):
        feed(til(k.mem, m, w=MEM), col(k, "norm_mem", m), til(k.m_hi, m, w=MEM), MEM)
    e.wait_ge(k.s_zeroed, 1)
    root(1, k.m_rstd, MEM)
    e.wait_ge(k.s_ld_x, 16)
    for m in range(KT):
        feed(til(k.x, m), col(k, "norm_mix", m), til(k.h_hi, m))
    e.wait_ge(k.s_tokr_t, 1)
    for mt in range(2):
        ins = A(k.tok[:, TOK_RTOK + mt:TOK_RTOK + mt + 1], k.ps[4][:, mt * P:mt * P + 1], ACT.Copy)
    ins.then_inc(k.s_v_done, 1)
    e.wait_ge(k.s_xk_raw, 1)
    A(k.mem[:, 0:HEADS * MEM], k.xk[:], ACT.Square).then_inc(k.s_unit_sq, 1)
    root(2, k.rstd)
    e.wait_ge(k.s_unit_sum, 1)
    for j in range(2):
        ins = A(k.mem[:, HEADS * MEM + j * T:HEADS * MEM + (j + 1) * T], k.ps[5 + j][:], ACT.Sqrt,
                bias=k.eps[:, 0:1], scale=1.0 / P)
    ins.then_inc(k.s_unit_std, 1)

    e.wait_ge(k.s_proj_done, 1)
    A(k.c_t[:], til(k.proj, UG + 2, 2), ACT.Sigmoid).then_inc(k.s_c_sig, 1)
    with e.Fori(0, 12) as m:
        e.wait_ge(k.s_g_conv, m + 1)
        A(rtil(k.qkv, m), rtil(k.qkv, m), ACT.Silu).then_inc(k.s_g_silu, 1)
    e.wait_ge(k.s_proj_done, 2)
    for h in range(HEADS):
        A(til(k.proj, Z + h), til(k.proj, Z + h), ACT.Silu).then_inc(k.s_z_silu, 1)

    for half in range(2):
        e.dma_start(k.d_ki[64 * half:64 * half + 64, :],
                    k.proj[0:64, REST * T:(REST + 1) * T]).then_inc(k.s_ki_dup, 16)
    for n, (bank, dst) in enumerate(((0, til(k.d_q, 0)), (1, til(k.d_q, 1)), (2, til(k.d_qi, 0)), (3, til(k.d_qi, 1)),
                                     (4, k.d_k[:]))):
        e.wait_ge(k.s_dq_mm, n + 1)
        A(dst, k.ps[bank][:], ACT.Copy).then_inc(k.s_dq_raw, 1)
    for n, (src, dst) in enumerate(((til(k.d_q, 0), til(k.d_relu, 0)), (til(k.d_q, 1), til(k.d_relu, 1)),
                                    (k.d_k[:], k.d_rk[:]))):
        e.wait_ge(k.s_dq_raw, (1, 2, 5)[n])
        A(dst, src, ACT.Square).then_inc(k.s_unit_sq, 1)
    e.wait_ge(k.s_d_gates, 1)
    A(k.tok[:, TOK_A:TOK_A + 48].rearrange("p (c w) -> p c w", c=TT),
      k.ps[6][:].rearrange("p (c w) -> p c w", c=TT)[:, :, 64:76], ACT.Copy).then_inc(k.s_d_gates_tok, 1)
    for j in range(2):
        e.wait_ge(k.s_c_cent, j + 1)
        A(til(k.c_t, j), til(k.c_acc, j), ACT.Square).then_inc(k.s_c_sq, 1)
    for n, (bank, dst) in enumerate(((0, til(k.d_relu, 0)), (1, til(k.d_relu, 1)), (4, k.d_rk[:]))):
        e.wait_ge(k.s_unit_sum, NORM_DQ + n + 1)
        A(dst, k.ps[bank][:], ACT.Sqrt, bias=k.eps[:, 0:1], scale=1.0 / 64).then_inc(k.s_unit_std, 1)

    e.wait_ge(k.s_c_var, 1)
    A(k.c_r[:], k.ps[7][:], ACT.Sqrt, bias=k.eps[:, 0:1], scale=1.0 / 256).then_inc(k.s_c_std, 1)
    for m in range(2):
        e.wait_ge(k.s_g_silu, 12)
        A(til(k.sq, m), til(k.qkv, m), ACT.Square).then_inc(k.s_unit_sq, 1)
    e.wait_ge(k.s_sp_in, 1)
    A(k.tok[:, TOK_SP + 24:TOK_SP + 48], k.tok[:, TOK_SP + 24:TOK_SP + 48], ACT.Exp, scale=-1.0)
    A(k.tok[:, TOK_EA:TOK_EA + 16], k.vec[:, VEC["a_log"][0]:VEC["a_log"][0] + 16],
      ACT.Exp).then_inc(k.s_sp_exp, 1)
    for j in range(2):
        e.wait_ge(k.s_c_norm, j + 1)
        A(til(k.c_t, j), til(k.c_acc, j), ACT.Silu, bias=col(k, "cln_b", j)).then_inc(k.s_c_silu, 1)
    for j in range(2):
        e.wait_ge(k.s_c_silu, j + 1)
        A(til(k.y_hi, 6 + j), til(k.c_t, j), ACT.Copy).then_inc(k.s_y_hi, 1)

    for m in range(2 * HEADS):
        if m >= 2:
            e.wait_ge(k.s_g_qk_done, m - 1)
        e.wait_ge(k.s_unit_sum, NORM_G + m + 1)
        A(k.g_d[:] if m % 2 == 0 else k.g_r[:], k.ps[4 + m % 4][:], ACT.Sqrt, bias=k.eps[:, 0:1]).then_inc(k.s_unit_std, 1)
        if m + 2 < 2 * HEADS:
            A(til(k.sq, m % 2), til(k.qkv, m + 2), ACT.Square).then_inc(k.s_unit_sq, 1)
    A(k.tok[:, TOK_BETA:TOK_BETA + 16].rearrange("p (c h) -> p c h", c=TT),
      k.tok[:, TOK_A:TOK_A + 48].rearrange("p (c w) -> p c w", c=TT)[:, :, 4:8], ACT.Sigmoid).then_inc(k.s_beta_done, 1)

    for qt in range(1, TT):
        cw = (qt + 1) * P
        for h in range(HEADS):
            v = HEADS * (qt - 1) + h
            e.wait_ge(k.s_idx_mm, v + 1)
            if v >= 2:
                e.wait_ge(k.s_idx_used, v - 1)
            else:
                e.wait_ge(k.s_dq_done, 3)
            A(k.d_relu[:, (h % 2) * T:(h % 2) * T + cw], k.ps[h][:, 0:cw], ACT.Relu).then_inc(k.s_idx_relu, 1)

    e.wait_ge(k.s_dec_copied, 1)
    A(k.tok[:, TOK_EDEC:TOK_EDEC + 16], k.tok[:, TOK_DEC:TOK_DEC + 16], ACT.Exp)
    A(k.tok[:, TOK_EKD:TOK_EKD + 16], k.tok[:, TOK_EKD:TOK_EKD + 16], ACT.Exp)
    A(k.tok[:, TOK_ELAST:TOK_ELAST + 16], k.tok[:, TOK_LAST:TOK_LAST + 16], ACT.Exp).then_inc(k.s_dec_exp, 1)
    for h in range(HEADS):
        e.wait_ge(k.s_gam_d, h + 1)
        A(til(k.g_xt, h), k.ps[h][:], ACT.Exp).then_inc(k.s_edecrow, 1)
        A(til(k.g_at, h), til(k.g_at, h), ACT.Exp).then_inc(k.s_gam_e, 1)
    e.wait_ge(k.s_dec_exp, 1)
    e.wait_ge(k.s_idx_used, 3 * HEADS)
    for h in range(HEADS):
        e.wait_ge(k.s_kt_mm, h + 1)
        for c in range(TT):
            t = TOK_EDEC + c * HEADS + h
            A(k.g_ek[:, h * T + c * P:h * T + (c + 1) * P], k.ps[6][:, c * P:(c + 1) * P], ACT.Copy,
              scale=k.tok[:, t:t + 1])
        for c in range(TT):
            t = TOK_EKD + c * HEADS + h
            ins = A(k.g_kdec[:, h * T + c * P:h * T + (c + 1) * P], k.ps[6][:, c * P:(c + 1) * P], ACT.Copy,
                    scale=k.tok[:, t:t + 1])
        ins.then_inc(k.s_ek_done, 1)
        e.wait_ge(k.s_vt_mm, h + 1)
        A(til(k.g_v, h), k.ps[7][:], ACT.Copy).then_inc(k.s_v_tok_done, 1)
    for h in range(HEADS):
        e.wait_ge(k.s_x_turned, h + 1)
        A(til(k.g_x, h), k.ps[h][:], ACT.Copy).then_inc(k.s_x_first, 1)
    e.sem_inc(k.s_p_copied, 2)
    with e.Fori(0, LEVELS - 1) as lev:
        for h in range(HEADS):
            e.wait_ge(k.s_p_mm, lev * HEADS + h + 1)
            e.wait_ge(k.s_x_done, lev * HEADS + h + 3)
            A(til(k.g_p, h % 2), k.ps[h % 2][:], ACT.Copy).then_inc(k.s_p_copied, 1)
    for h in range(HEADS):
        e.wait_ge(k.s_wt_mm, h + 1)
        A(til(k.qkv, 4 + h), k.ps[6 + h % 2][:], ACT.Copy, scale=-1.0).then_inc(k.s_wt_done, 1)

    def exps(qt, h):
        u, cw = qt * HEADS + h, (qt + 1) * P
        p = k.d_p[:, (h % 2) * T:(h % 2) * T + cw]
        e.wait_ge(k.s_lg_masked, u + 1)
        A(p, p, ACT.Exp, bias=k.tok[:, TOK_NM + h % 2:TOK_NM + h % 2 + 1],
          accum_out=k.tok[:, TOK_SUM + h % 2:TOK_SUM + h % 2 + 1]).then_inc(k.s_p_exp, 1)

    def turned(qt, h):
        u, cw = qt * HEADS + h, (qt + 1) * P
        e.wait_ge(k.s_pt_mm, u + 1)
        A(k.d_pt[:, (h % 2) * T:(h % 2) * T + cw], k.ps[6][:, 0:cw], ACT.Copy).then_inc(k.s_pt_copied, 1)

    for c in range(TT):
        exps(c, 0)
        exps(c, 1)
        e.wait_ge(k.s_o_part, c + 1)
        A(k.qkv[:, 8 * T:12 * T].rearrange("p (h t) -> p h t", h=HEADS)[:, :, c * P:(c + 1) * P],
          k.ps[2][:].rearrange("p (h t) -> p h t", h=HEADS), ACT.Copy).then_inc(k.s_o_copied, 1)
        for h in range(HEADS):
            turned(c, h)
            if h + 2 < HEADS:
                exps(c, h + 2)
        e.wait_ge(k.s_o_mm, c + 1)
        A(k.y_hi[:, 4 * T:6 * T].rearrange("p (j t) -> p j t", j=2)[:, :, c * P:(c + 1) * P],
          k.ps[7][:, 0:2 * P].rearrange("p (j t) -> p j t", j=2), ACT.Copy).then_inc(k.s_y_hi, 1)
    e.wait_ge(k.s_o_copied, TT)
    for h in range(HEADS):
        A(til(k.g_x, h), til(k.qkv, 8 + h), ACT.Square).then_inc(k.s_unit_sq, 1)
    for h in range(HEADS):
        e.wait_ge(k.s_unit_sum, NORM_GO + h + 1)
        A(til(k.g_xt, h), k.ps[h][:], ACT.Sqrt, bias=k.eps[:, 0:1], scale=1.0 / P).then_inc(k.s_unit_std, 1)
    for h in range(HEADS):
        e.wait_ge(k.s_go_norm, h + 1)
        A(til(k.y_hi, h), til(k.qkv, 8 + h), ACT.Copy).then_inc(k.s_y_hi, 1)

    def residual_feeds(gain, times=KT, split=True, per=4):
        with e.Fori(0, times // per) as i:
            fed.enter(i, per)
            for j in range(per):
                e.wait_ge(k.s_x_new, fed.at(1) - 2 * KT)
                g = k.vec[:, bass.ds(i * per + (VEC[gain][0] + j), 1)]
                feed(rtil(k.x, i * per + j), g, rtil(k.h_hi, i * per + j), split=split)
            fed.leave(times // per)

    residual_feeds("norm_cross")

    root(3, k.rstd)
    for h in range(HEADS):
        e.wait_ge(k.s_aq_raw, h + 1)
        if h >= 2:
            e.wait_ge(k.s_unit_sum, NORM_AQ + h - 1)
        else:
            e.wait_ge(k.s_sq_used, 2 + 3 * KT)
        A(til(k.sq, h % 2), til(k.a_q, h), ACT.Square).then_inc(k.s_unit_sq, 1)
        e.wait_ge(k.s_unit_sum, NORM_AQ + h + 1)
        if h >= 2:
            e.wait_ge(k.s_aq_done, h - 1)
        A(til(k.a_p, h % 2), k.ps[4 + h % 2][:], ACT.Sqrt, bias=k.eps[:, 0:1], scale=1.0 / P).then_inc(k.s_unit_std, 1)
    for h in range(HEADS):
        for half in range(2):
            u = 2 * h + half
            e.wait_ge(k.s_al_max, u + 1)
            if h:
                e.wait_ge(k.s_apt_mm, 2 * h)
            else:
                e.wait_ge(k.s_aq_done, HEADS)
            for n in range(2):
                c = 2 * half + n
                ins = A(k.a_p[:, c * MEM:(c + 1) * MEM], k.ps[half][:, n * MEM:(n + 1) * MEM], ACT.Exp,
                        scale=XA_SCALE, bias=k.tok[:, TOK_NM + c:TOK_NM + c + 1],
                        accum_out=k.tok[:, TOK_SUM + c:TOK_SUM + c + 1])
            ins.then_inc(k.s_al_exp, 1)
        for mt in range(2):
            e.wait_ge(k.s_apt_mm, 2 * h + mt + 1)
            if h:
                e.wait_ge(k.s_av_mm, h)
            A(til(k.a_pt, mt), k.ps[2 + mt][:], ACT.Copy).then_inc(k.s_apt_copied, 1)
        e.wait_ge(k.s_av_mm, h + 1)
        A(til(k.ao_hi, h), k.ps[4 + h % 2][:], ACT.Copy).then_inc(k.s_ao_hi_done, 1)
    residual_feeds("norm_mlp")

    root(4, k.rstd)
    for half in range(2):
        with e.Fori(0, MTH // 4) as i:
            for j in range(4):
                m = i * 4 + j
                e.wait_ge(k.s_up_relu, m + (half * MTH + 1))
                A(k.u_t[:, (2 + j % 2) * T:(3 + j % 2) * T], k.u_t[:, (j % 2) * T:(j % 2 + 1) * T],
                  ACT.Square).then_inc(k.s_up_sq, 1)
                e.wait_ge(k.s_up_sq, m + (half * MTH + 1))
                A(rtil(k.u_hi, m), k.u_t[:, (2 + j % 2) * T:(3 + j % 2) * T], ACT.Copy).then_inc(k.s_up_hi, 1)
    residual_feeds("ln1")

    root(5, k.rstd)
    st = lambda n: til(k.s_t, n)
    with e.Fori(0, KT) as i:
        e.wait_ge(k.s_s2_u, i + 1)
        A(k.ub_hi[:], st(0), ACT.Copy).then_inc(k.s_s2_uhi, 1)
        e.wait_ge(k.s_s2_gl, i + 1)
        A(st(2), st(1), ACT.Square).then_inc(k.s_s2_gsq, 1)
        e.wait_ge(k.s_s2_gt, i + 1)
        A(st(2), st(2), ACT.Sigmoid, scale=GELU_SCALE).then_inc(k.s_s2_gsig, 1)
        for n in range(2):
            e.wait_ge(k.s_s2_gate, i * 2 + n + 1)
            g = rtil(k.gates, i + n * KT)
            A(g, g, ACT.Sigmoid, bias=k.vec[:, bass.ds(i + (VEC["gate_b"][0] + n * KT), 1)]).then_inc(k.s_s2_gate_done, 1)
        e.wait_ge(k.s_panel_used, i * 8 + (SPLIT + PAN_S6 + MIX_GATES + 1))
        A(st(3), k.ps[2][:], ACT.Sigmoid, bias=k.vec[:, bass.ds(i + VEC["lru_ba"][0], 1)]).then_inc(k.s_s2_r, 1)
        A(st(4), k.ps[3][:], ACT.Sigmoid, bias=k.vec[:, bass.ds(i + VEC["lru_bx"][0], 1)]).then_inc(k.s_s2_i, 1)
        e.wait_ge(k.s_s2_r, i + 1)
        A(st(6), st(3), ACT.Tanh, scale=k.tok[:, bass.ds(i + TOK_P8, 1)]).then_inc(k.s_s2_th, 1)
        A(st(5), st(3), ACT.Exp, scale=k.tok[:, bass.ds(i + TOK_N8, 1)]).then_inc(k.s_s2_a, 1)
        e.wait_ge(k.s_s2_a, i + 1)
        A(st(7), st(5), ACT.Square).then_inc(k.s_s2_a2, 1)
        e.wait_ge(k.s_s2_m, i + 1)
        A(st(7), st(7), ACT.Sqrt, bias=k.eps[:, 1:2]).then_inc(k.s_s2_s, 1)
        e.wait_ge(k.s_s2_yb, i + 1)
        A(rtil(k.yb_hi, i), st(8), ACT.Copy).then_inc(k.s_s2_yb_hi, 1)
        e.wait_ge(k.s_s2_ya, i + 1)
        A(rtil(k.ya_hi, i), st(3), ACT.Copy).then_inc(k.s_s2_ya_hi, 1)
    with e.Fori(0, KT // 2) as i:
        for j in range(2):
            e.wait_ge(k.s_mg, i * 2 + j + 1)
            A(rtil(k.mg_hi, i * 2 + j), st(2 * j), ACT.Copy).then_inc(k.s_mg_hi, 1)
    residual_feeds("ln2")

    root(6, k.rstd)
    with e.Fori(0, FFN // 2) as i:
        for j in range(2):
            e.wait_ge(k.s_f_g, i * 2 + j + 1)
            A(til(k.f_t, j), til(k.f_t, j), ACT.Silu).then_inc(k.s_f_silu, 1)
            e.wait_ge(k.s_f_hid, i * 2 + j + 1)
            A(rtil(k.f_hi, i * 2 + j), til(k.f_t, j), ACT.Copy).then_inc(k.s_f_hi_done, 1)
    residual_feeds("final", split=False)
    root(7, k.rstd)


GELU_SCALE = 2.0 * 0.7978845608028654
XA_SCALE = 128 ** -0.5
PAN_S6 = 112
PAN_S7 = PAN_S6 + 64
PAN_S8 = PAN_S7 + 16
PAN_S9 = PAN_S8 + 8
PAN_DOWN = PAN_S9 + 44


def vector_program(nc, k):
    e = nc.vector
    chain = Chain(e, k.s_dve_chain)
    fed = Count()
    TS, TTn, STT = e.tensor_scalar, e.tensor_tensor, e.scalar_tensor_tensor
    for b in range(8):
        e.sem_inc(k.acc_free[b], 1)
    e.memset(k.eps[:, 0:1], EPS)
    e.memset(k.eps[:, 1:2], 1e-30)
    e.memset(k.m_sqa[:], 0.0)
    e.sem_inc(k.s_sq_used, 2)
    chain(e.memset(k.sqacc[:], 0.0))
    e.sem_inc(k.s_zeroed, 1)

    def feed(src, gain, hi, lo, w=T, split=True, sqacc=None):
        acc = (sqacc or k.sqacc)[:, 0:w]
        if split:
            e.wait_ge(k.s_fed_hi, fed.at(1))
            STT(out=lo, in0=src, scalar=gain, in1=hi.bitcast(F32), op0=ALU.mult,
                op1=ALU.subtract).then_inc(k.s_fed_lo, 1)
        e.wait_ge(k.s_fed_sq, fed.at(1))
        TTn(acc, acc, k.sq[:, (fed.n % 2) * T:(fed.n % 2) * T + w], ALU.add).then_inc(k.s_sq_used, 1)
        fed.step()
        e.wait_ge(k.s_sq_used, 2 + fed.at())

    def invert(n_norm, dst, w=T):
        e.wait_ge(k.s_std, n_norm)
        e.reciprocal(dst[:, 0:w], dst[:, 0:w]).then_inc(k.s_rstd, 1)
        e.wait_ge(k.s_rstd, n_norm)

    freed = [1 + 2 + 6, 1 + 2 + 6, 1 + 1 + 6, 1 + 1 + 6, 1, 1, 1, 1]

    e.wait_ge(k.s_ld_vec, 16)
    e.wait_ge(k.s_ld_mem, 16)
    for m in range(KT):
        feed(til(k.mem, m, w=MEM), col(k, "norm_mem", m), til(k.m_hi, m, w=MEM), til(k.m_lo, m, w=MEM), MEM,
             sqacc=k.m_sqa)
    invert(1, k.m_rstd, MEM)
    for m in range(HEADS):
        e.wait_ge(k.s_panel_used, SPLIT + m + 1)
        ins = TTn(til(k.xk, m, w=MEM), k.ps[m % 2][:, 0:MEM], k.m_rstd[:], ALU.mult)
        ins.then_inc(k.acc_free[m % 2], 1)
    e.wait_ge(k.acc_free[0], 3)
    e.wait_ge(k.acc_free[1], 3)
    e.sem_inc(k.s_xk_raw, 1)
    e.wait_ge(k.s_ld_x, 16)
    for m in range(KT):
        feed(til(k.x, m), col(k, "norm_mix", m), til(k.h_hi, m), til(k.h_lo, m))
    e.wait_ge(k.s_panel_used, SPLIT + 8)
    e.wait_ge(k.s_v_done, 1)
    for mt in range(2):
        TS(til(k.xv, mt), k.ps[2 + mt][:], k.tok[:, TOK_RTOK + mt:TOK_RTOK + mt + 1], None,
           ALU.mult).then_inc(k.acc_free[2 + mt], 1)
        e.wait_ge(k.acc_free[2 + mt], 2)
    e.sem_inc(k.s_v_done, 1)
    invert(2, k.rstd)
    e.wait_ge(k.s_unit_std, 1)
    xk_r = k.mem[:, HEADS * MEM:2 * HEADS * MEM]
    chain(e.reciprocal(xk_r, xk_r))
    STT(out=k.xk[:], in0=k.xk[:], scalar=col(k, "xa_k"), in1=xk_r, op0=ALU.mult, op1=ALU.mult).then_inc(k.s_xk_done, 1)

    with e.Fori(0, 2) as i:
        for j in range(4):
            e.wait_ge(k.s_panel_used, i * 4 + (SPLIT + 8 + j + 1))
            TTn(rtil(k.proj, i * 4 + j), k.ps[j][:], k.rstd[:], ALU.mult).then_inc(k.acc_free[j], 1)
    for j in range(4):
        e.wait_ge(k.acc_free[j], freed[j] - 4)
    e.sem_inc(k.s_proj_done, 1)
    cy = [k.c_y[:, j * (PAD + T):(j + 1) * (PAD + T)] for j in range(2)]
    e.wait_ge(k.s_c_sig, 1)
    for j in range(2):
        e.memset(cy[j][:, 0:PAD], 0.0)
        ins = TTn(cy[j][:, PAD:PAD + T], til(k.proj, UG + j), til(k.c_t, j), ALU.mult)
    chain(ins)
    for j in range(2):
        ins = TS(til(k.c_acc, j), cy[j][:, PAD:PAD + T], col(k, "dw", j * CONV_TAPS + CONV_TAPS - 1),
                 col(k, "dw_b", j), ALU.mult, ALU.add)
    chain(ins)

    def link(ins):
        ins.then_inc(k.s_dve_chain, 1)
        return chain.c.step()

    def mixer_taps(n, last, before):
        for j in range(2):
            e.wait_ge(k.s_dve_chain, before[j])
            w = k.vec[:, bass.ds(n + (VEC["dw"][0] + j * CONV_TAPS), 1)]
            acc = til(k.c_acc, j)
            ins = STT(out=acc, in0=cy[j][:, bass.ds(n + PAD - CONV_TAPS + 1, T)], scalar=w, in1=acc, op0=ALU.mult,
                      op1=ALU.add)
            if last:
                ins.then_inc(k.s_c_conv, 1)
            else:
                before[j] = link(ins)

    with e.Fori(0, 3) as i:
        chain.c.enter(i, 4 * 7)
        before = [chain.c.at(), chain.c.at()]
        for j in range(4):
            e.wait_ge(k.s_panel_used, i * 4 + (SPLIT + 16 + j + 1))
            TTn(rtil(k.proj, i * 4 + (QKV + j)), k.ps[j][:], k.rstd[:], ALU.mult).then_inc(k.acc_free[j], 1)
            mixer_taps(i * 8 + 2 * j, False, before)
            e.wait_ge(k.acc_free[j], i + (freed[j] - 3))
            dst = rtil(k.qkv, i * 4 + j)
            for s in range(4):
                w = k.vec[:, bass.ds(i * 16 + (VEC["gdn_conv"][0] + j * 4 + 3 - s), 1)]
                if s == 0:
                    tap = link(TS(dst, rtil(k.proj, i * 4 + (QKV + j)), w, None, ALU.mult))
                    mixer_taps(i * 8 + (2 * j + 1), False, before)
                else:
                    e.wait_ge(k.s_dve_chain, tap)
                    ins = STT(out=k.qkv[:, bass.ds(i * (4 * T) + (j * T + s), T - s)],
                              in0=k.proj[:, bass.ds(i * (4 * T) + (QKV + j) * T, T - s)], scalar=w,
                              in1=k.qkv[:, bass.ds(i * (4 * T) + (j * T + s), T - s)], op0=ALU.mult, op1=ALU.add)
                    if s == 3:
                        ins.then_inc(k.s_g_conv, 1)
                    else:
                        tap = link(ins)
        chain.c.leave(3)
    before = [chain.c.at(), chain.c.at()]
    for j in range(4):
        e.wait_ge(k.s_panel_used, SPLIT + 28 + j + 1)
        TTn(til(k.proj, Z + j), k.ps[j][:], k.rstd[:], ALU.mult).then_inc(k.acc_free[j], 1)
        if j < 3:
            mixer_taps(24 + 2 * j, False, before)
            mixer_taps(25 + 2 * j, j == 2, before)
    for j in range(4):
        e.wait_ge(k.acc_free[j], freed[j])
    e.sem_inc(k.s_proj_done, 1)

    e.wait_ge(k.s_dq_mm, 4)
    chain(e.memset(k.d_v[:], 0.0))
    e.wait_ge(k.s_dq_mm, 6)
    for par in range(2):
        dst = k.d_v[:].rearrange("p (t q w) -> p t q w", t=TT, q=2)[:, :, par, 64 * par:64 * par + 64]
        ins = e.tensor_copy(dst, k.ps[5][:, 0:256].rearrange("p (t w) -> p t w", t=TT))
    ins.then_inc(k.s_dv_done, 1)
    e.wait_ge(k.s_d_gates_tok, 1)
    TS(k.tok[:, TOK_W:TOK_W + 16].rearrange("p (c h) -> p c h", c=TT),
       k.tok[:, TOK_A:TOK_A + 48].rearrange("p (c w) -> p c w", c=TT)[:, :, 8:12], 1.0 / 16, None, ALU.mult)
    tok = lambda at, n: k.tok[:, at:at + n]
    v, z, t, w2, s_ = (tok(TOK_SP + 24 * n, 24) for n in range(5))
    TTn(tok(TOK_SP, 16).rearrange("p (c h) -> p c h", c=TT),
        k.tok[:, TOK_A:TOK_A + 48].rearrange("p (c w) -> p c w", c=TT)[:, :, 0:4],
        k.vec[:, VEC["dt_bias"][0]:VEC["dt_bias"][0] + 16].rearrange("p (c h) -> p c h", c=TT), ALU.add)
    chain(TS(tok(TOK_SP + 16, 8), k.vec[:, VEC["lam"][0]:VEC["lam"][0] + 8], -1.0, None, ALU.mult))
    STT(out=z, in0=v, scalar=-1.0, in1=v, op0=ALU.mult, op1=ALU.max).then_inc(k.s_sp_in, 1)

    for j in range(2):
        e.wait_ge(k.s_c_mean, 1)
        e.wait_ge(k.s_c_conv, 2)
        acc = til(k.c_acc, j)
        STT(out=acc, in0=k.ps[6][:], scalar=-1.0 / 256, in1=acc, op0=ALU.mult, op1=ALU.add).then_inc(k.s_c_cent, 1)
    for n, (raw, root, gain) in enumerate(((til(k.d_q, 0), til(k.d_relu, 0), "dsa_q"),
                                           (til(k.d_q, 1), til(k.d_relu, 1), "dsa_q"),
                                           (k.d_k[:], k.d_rk[:], "dsa_k"))):
        e.wait_ge(k.s_unit_std, NORM_DQ + n + 1)
        chain(e.reciprocal(root, root))
        STT(out=raw, in0=raw, scalar=col(k, gain), in1=root, op0=ALU.mult, op1=ALU.mult).then_inc(k.s_dq_done, 1)
    e.wait_ge(k.s_c_std, 1)
    chain(e.reciprocal(k.c_r[:], k.c_r[:]))
    for j in range(2):
        e.wait_ge(k.s_c_cent, 2)
        e.wait_ge(k.s_c_sq, 2)
        acc = til(k.c_acc, j)
        STT(out=acc, in0=acc, scalar=col(k, "cln_g", j), in1=k.c_r[:], op0=ALU.mult, op1=ALU.mult).then_inc(k.s_c_norm, 1)

    e.wait_ge(k.s_sp_exp, 1)
    chain(TS(t, z, 2.0, None, ALU.add))
    chain(e.reciprocal(t, t))
    chain(TTn(z, z, t, ALU.mult))
    chain(TTn(w2, z, z, ALU.mult))
    chain(TS(s_, w2, 1.0 / 15, 1.0 / 13, ALU.mult, ALU.add))
    for n in (11, 9, 7, 5, 3, 1):
        chain(TTn(s_, s_, w2, ALU.mult))
        chain(TS(s_, s_, 1.0 / n, None, ALU.add))
    chain(TTn(s_, s_, z, ALU.mult))
    chain(TS(v, v, 0.0, None, ALU.max))
    chain(STT(out=s_, in0=s_, scalar=2.0, in1=v, op0=ALU.mult, op1=ALU.add))
    TS(tok(TOK_N8, 8), s_[:, 16:24], -8.0, None, ALU.mult)
    TS(tok(TOK_P8, 8), s_[:, 16:24], 8.0, None, ALU.mult)
    STT(out=tok(TOK_G, 16), in0=s_[:, 0:16], scalar=-1.0, in1=tok(TOK_EA, 16), op0=ALU.mult,
        op1=ALU.mult).then_inc(k.s_g_ready, 1)
    for j in range(2):
        e.wait_ge(k.s_y_hi, j + 1)
        TTn(til(k.y_lo, 6 + j), til(k.c_t, j), til(k.y_hi, 6 + j).bitcast(F32), ALU.subtract).then_inc(k.s_y_lo, 1)
    e.wait_ge(k.s_g_conv, 12)
    e.wait_ge(k.s_g_ready, 1)
    for h in range(HEADS):
        for c in range(TT):
            t_ = TOK_G + c * HEADS + h
            ins = TS(k.g_x[:, h * T + c * P:h * T + (c + 1) * P], k.const[:, C_ONE:C_ONE + P], k.tok[:, t_:t_ + 1], None,
                     ALU.mult)
        ins.then_inc(k.s_gb_done, 1)
    for m in range(2 * HEADS):
        r = k.g_d if m % 2 == 0 else k.g_r
        e.wait_ge(k.s_unit_std, NORM_G + m + 1)
        chain(e.reciprocal(r[:], r[:]))
        q = til(k.qkv, m)
        STT(out=q, in0=q, scalar=P ** -0.5 if m < HEADS else 1.0, in1=r[:], op0=ALU.mult,
            op1=ALU.mult).then_inc(k.s_g_qk_done, 1)
    e.wait_ge(k.s_dq_done, 3)
    scores = [None, k.d_score_a[:, 0:2 * P], k.d_score_a[:, 2 * P:5 * P], k.d_score_b[:]]
    for qt in range(1, TT):
        cw, score = (qt + 1) * P, scores[qt]
        for h in range(HEADS):
            v_ = HEADS * (qt - 1) + h
            w = TOK_W + qt * HEADS + h
            e.wait_ge(k.s_idx_relu, v_ + 1)
            STT(out=score, in0=k.d_relu[:, (h % 2) * T:(h % 2) * T + cw], scalar=k.tok[:, w:w + 1],
                in1=k.const[:, C_CAUS + T - cw:C_CAUS + T] if h == 0 else score, op0=ALU.mult,
                op1=ALU.add).then_inc(k.s_idx_used, 1)
            e.wait_ge(k.s_idx_used, v_ + 1)
    e.wait_ge(k.s_dec_mm, 1)
    chain(e.tensor_copy(tok(TOK_DEC, 32), k.ps[7][:, 0:32]))
    TTn(tok(TOK_EKD, 16), tok(TOK_LAST, 16), tok(TOK_DEC, 16), ALU.subtract).then_inc(k.s_dec_copied, 1)
    tri4 = k.const[:, C_TRI:C_TRI + P].unsqueeze(1).broadcast_to([P, TT, P])
    for h in range(HEADS):
        e.wait_ge(k.s_decrow, h + 1)
        for c in range(TT):
            t_ = TOK_DEC + c * HEADS + h
            ins = TS(k.g_at[:, h * T + c * P:h * T + (c + 1) * P], k.ps[h][:, c * P:(c + 1) * P], k.tok[:, t_:t_ + 1],
                     0.0, ALU.subtract, ALU.min)
        ins.then_inc(k.s_gam_d, 1)
    for h in range(HEADS):
        e.wait_ge(k.s_gam_e, h + 1)
        g3 = til(k.g_at, h).rearrange("p (c i) -> p c i", c=TT)
        TTn(g3, g3, tri4, ALU.mult).then_inc(k.s_gam_done, 1)
    e.wait_ge(k.s_gam_done, HEADS)
    e.wait_ge(k.s_beta_done, 1)
    for h in range(HEADS):
        e.wait_ge(k.s_qk_mm, h + 1)
        TTn(til(k.g_qk, h), k.ps[4][:], til(k.g_at, h), ALU.mult).then_inc(k.s_qk_done, 1)
        e.wait_ge(k.s_qk_done, h + 1)
        e.wait_ge(k.s_kk_mm, h + 1)
        for c in range(TT):
            t_ = TOK_BETA + c * HEADS + h
            a = k.g_at[:, h * T + c * P:h * T + (c + 1) * P]
            ins = STT(out=a, in0=k.ps[5][:, c * P:(c + 1) * P], scalar=k.tok[:, t_:t_ + 1], in1=a, op0=ALU.mult,
                      op1=ALU.mult)
        ins.then_inc(k.s_at_done, 1)
    e.wait_ge(k.s_at_done, HEADS)
    for h in range(HEADS):
        e.wait_ge(k.s_edecrow, h + 1)
        e.wait_ge(k.s_kk_mm, HEADS)
        q = til(k.qkv, h)
        TTn(q, q, til(k.g_xt, h), ALU.mult).then_inc(k.s_gam_done, 1)
    def blocks(h, lev, base):
        mask = k.const[:, bass.ds(lev * P + (C_LEV + base * P), P)].unsqueeze(1).broadcast_to([P, TT, P])
        TTn(til(k.g_b, h % 2).rearrange("p (c i) -> p c i", c=TT),
            til(k.g_at, h).rearrange("p (c i) -> p c i", c=TT), mask, ALU.mult).then_inc(k.s_bt_done, 1)

    e.wait_ge(k.s_gam_done, 2 * HEADS)
    spread = lambda at: k.const[:, at:at + P].unsqueeze(1).broadcast_to([P, TT, P])
    chunks = lambda buf, h: til(buf, h).rearrange("p (c i) -> p c i", c=TT)
    for h in range(HEADS):
        chain(TTn(chunks(k.g_xt, h), chunks(k.g_at, h), spread(C_LEV), ALU.mult))
        TTn(chunks(k.g_xt, h), spread(C_ID), chunks(k.g_xt, h), ALU.subtract).then_inc(k.s_x_init, 1)
    chain(e.memset(k.g_s[:], 0.0))
    e.sem_inc(k.s_x_done, HEADS)
    e.sem_inc(k.s_st_done, 1)
    blocks(0, 0, 1)

    def level(lev, base, top_rounds, last=False):
        for h in range(HEADS):
            found = []
            if top_rounds:
                e.wait_ge(k.s_dve_chain, replaced[0])
            if h + 1 < HEADS:
                blocks(h + 1, lev, base)
            elif not last:
                blocks(0, lev, base + 1)
            if top_rounds:
                for qt in range(1, TT):
                    found.append(link(e.max(tok(TOK_M8 + 8 * qt - 8, 8), scores[qt])))
                e.wait_ge(k.s_dve_chain, found[-1])
            e.wait_ge(k.s_xp_mm, lev * HEADS + ((base - 1) * HEADS + h + 1))
            if not last:
                TTn(til(k.g_x, h), til(k.g_x, h), k.ps[2 + h % 2][:], ALU.subtract)
            TTn(til(k.g_xt, h), til(k.g_xt, h), k.ps[4 + h % 2][:], ALU.subtract).then_inc(k.s_x_done, 1)
            if top_rounds:
                for qt in range(1, TT):
                    replaced[0] = link(e.match_replace(scores[qt], tok(TOK_M8 + 8 * qt - 8, 8), scores[qt], TAKEN))

    top_levels = TOPK // 8 // HEADS
    with e.Fori(0, top_levels) as lev:
        chain.c.enter(lev, 6 * HEADS)
        replaced = [chain.c.at()]
        level(lev, 1, True)
        chain.c.leave(top_levels)
    for base in range(1 + top_levels, LEVELS - 1):
        level(0, base, False)
    e.wait_ge(k.s_dve_chain, chain.c.at())
    for qt in range(1, TT):
        ins = TS(scores[qt], scores[qt], TAKEN, MASKED, ALU.not_equal, ALU.mult)
    chain(ins)
    level(0, LEVELS - 1, False, last=True)

    def soften(qt, h):
        u, cw = qt * HEADS + h, (qt + 1) * P
        p, mx = k.d_p[:, (h % 2) * T:(h % 2) * T + cw], k.tok[:, TOK_MX + h % 2:TOK_MX + h % 2 + 1]
        bias = scores[qt] if qt else k.const[:, C_CAUS + T - P:C_CAUS + T]
        e.wait_ge(k.s_lg_mm, u + 1)
        if u >= 2:
            e.wait_ge(k.s_pt_mm, u - 1)
        chain(STT(out=p, in0=k.ps[4 + h % 2][:, 0:cw], scalar=0.125, in1=bias, op0=ALU.mult, op1=ALU.add))
        chain(e.tensor_reduce(mx, p, AX.X, ALU.max))
        TS(k.tok[:, TOK_NM + h % 2:TOK_NM + h % 2 + 1], mx, -1.0, None, ALU.mult).then_inc(k.s_lg_masked, 1)

    def normalise(qt, h):
        u, cw = qt * HEADS + h, (qt + 1) * P
        p = k.d_p[:, (h % 2) * T:(h % 2) * T + cw]
        r = k.tok[:, TOK_R + h % 2:TOK_R + h % 2 + 1]
        e.wait_ge(k.s_p_exp, u + 1)
        chain(e.reciprocal(r, k.tok[:, TOK_SUM + h % 2:TOK_SUM + h % 2 + 1]))
        TS(p, p, r, None, ALU.mult).then_inc(k.s_p_norm, 1)

    by_head = lambda ap: ap.rearrange("p (h t) -> p h t", h=HEADS)
    for c in range(TT):
        e.wait_ge(k.s_vn_mm, c + 1)
        beta = k.tok[:, TOK_BETA + c * HEADS:TOK_BETA + (c + 1) * HEADS].unsqueeze(2).broadcast_to([P, HEADS, P])
        TTn(by_head(k.g_vn[:]), by_head(k.ps[c % 2][:]), beta, ALU.mult).then_inc(k.s_vn_done, 1)
        soften(c, 0)
        soften(c, 1)
        e.wait_ge(k.s_st_mm, c + 1)
        for h in range(HEADS):
            t_ = c * HEADS + h
            s = k.g_s[:, h * P:(h + 1) * P]
            ins = STT(out=s, in0=s, scalar=k.tok[:, TOK_ELAST + t_:TOK_ELAST + t_ + 1],
                      in1=k.ps[3][:, h * P:(h + 1) * P], op0=ALU.mult, op1=ALU.add)
        ins.then_inc(k.s_st_done, 1)
        for h in range(HEADS):
            normalise(c, h)
            if h + 2 < HEADS:
                soften(c, h + 2)
        e.wait_ge(k.s_st_done, c + 2)
        e.wait_ge(k.s_y_hi, 2 + c + 1)
        cols_ = lambda y: y[:, 4 * T:6 * T].rearrange("p (j t) -> p j t", j=2)[:, :, c * P:(c + 1) * P]
        TTn(cols_(k.y_lo), k.ps[7][:, 0:2 * P].rearrange("p (j t) -> p j t", j=2), cols_(k.y_hi).bitcast(F32),
            ALU.subtract).then_inc(k.s_y_lo, 1)
    for h in range(HEADS):
        e.wait_ge(k.s_unit_std, NORM_GO + h + 1)
        r = til(k.g_xt, h)
        chain(e.reciprocal(r, r))
        o = til(k.qkv, 8 + h)
        chain(STT(out=o, in0=o, scalar=col(k, "gdn_norm"), in1=r, op0=ALU.mult, op1=ALU.mult))
        e.wait_ge(k.s_z_silu, h + 1)
        TTn(o, o, til(k.proj, Z + h), ALU.mult).then_inc(k.s_go_norm, 1)
    e.wait_ge(k.s_go_norm, HEADS)
    for h in range(HEADS):
        e.wait_ge(k.s_y_hi, 2 + TT + h + 1)
        TTn(til(k.y_lo, h), til(k.qkv, 8 + h), til(k.y_hi, h).bitcast(F32), ALU.subtract).then_inc(k.s_y_lo, 1)

    def residual(pan0, panels_per_tile, gain, banks=2, split=True, feeds=True, per=4):
        chain(e.memset(k.sqacc[:], 0.0))
        with e.Fori(0, KT // per) as i:
            fed.enter(i, per if feeds else 0)
            for j in range(per):
                m = i * per + j
                num, den = panels_per_tile
                e.wait_ge(k.s_panel_used, i * (per * num // den) + (SPLIT + pan0 + (j * num) // den + num))
                x = rtil(k.x, m)
                ins = TTn(x, x, k.ps[j % banks][:], ALU.add)
                ins.then_inc(k.acc_free[j % banks], 1)
                e.wait_ge(k.acc_free[j % banks], acc_value(i, j, banks, per))
                if feeds:
                    e.sem_inc(k.s_x_new, 1)
                    g = k.vec[:, bass.ds(i * per + (VEC[gain][0] + j), 1)]
                    feed(x, g, rtil(k.h_hi, m), rtil(k.h_lo, m), split=split)
            fed.leave(KT // per)
        for b in range(banks):
            freed[b] += KT // banks


    def acc_value(i, j, banks, per):
        return i * (per // banks) + (freed[j % banks] + j // banks + 1)

    residual(32, (1, 1), "norm_cross")

    invert(3, k.rstd)
    for j in range(HEADS):
        e.wait_ge(k.s_panel_used, SPLIT + 40 + j + 1)
        TTn(til(k.a_q, j), k.ps[j][:], k.rstd[:], ALU.mult).then_inc(k.acc_free[j], 1)
        freed[j] += 1
        e.wait_ge(k.acc_free[j], freed[j])
        e.sem_inc(k.s_aq_raw, 1)
    for h in range(HEADS):
        e.wait_ge(k.s_unit_std, NORM_AQ + h + 1)
        r = til(k.a_p, h % 2)
        chain(e.reciprocal(r, r))
        q = til(k.a_q, h)
        STT(out=q, in0=q, scalar=col(k, "xa_q"), in1=r, op0=ALU.mult, op1=ALU.mult).then_inc(k.s_aq_done, 1)
    for h in range(HEADS):
        for half in range(2):
            u = 2 * h + half
            e.wait_ge(k.s_al_mm, u + 1)
            if h:
                e.wait_ge(k.s_al_exp, u - 1)
            chain(e.tensor_reduce(tok(TOK_MX + 2 * half, 2), k.ps[half][:].rearrange("p (n m) -> p n m", n=2), AX.X,
                                  ALU.max))
            TS(tok(TOK_NM + 2 * half, 2), tok(TOK_MX + 2 * half, 2), -XA_SCALE, None, ALU.mult).then_inc(k.s_al_max, 1)
        for half in range(2):
            u = 2 * h + half
            e.wait_ge(k.s_al_exp, u + 1)
            chain(e.reciprocal(tok(TOK_R + 2 * half, 2), tok(TOK_SUM + 2 * half, 2)))
            for n in range(2):
                c = 2 * half + n
                p = k.a_p[:, c * MEM:(c + 1) * MEM]
                ins = TS(p, p, tok(TOK_R + c, 1), None, ALU.mult)
            ins.then_inc(k.s_al_norm, 1)
        e.wait_ge(k.s_ao_hi_done, h + 1)
        TTn(til(k.ao_lo, h), k.ps[4 + h % 2][:], til(k.ao_hi, h).bitcast(F32), ALU.subtract).then_inc(k.s_ao_lo_done, 1)
    residual(44, (1, 2), "norm_mlp")

    invert(4, k.rstd)
    for half in range(2):
        pan0 = 48 + 32 * half
        with e.Fori(0, MTH // 4) as i:
            for j in range(4):
                m = i * 4 + j
                e.wait_ge(k.s_panel_used, m + (SPLIT + pan0 + 1))
                STT(out=til(k.u_t, j % 2), in0=k.ps[j % 2][:], scalar=0.0, in1=k.rstd[:], op0=ALU.max,
                    op1=ALU.mult).then_inc(k.acc_free[j % 2], 1)
                e.wait_ge(k.acc_free[j % 2], i * 2 + (freed[j % 2] + j // 2 + 1))
                e.sem_inc(k.s_up_relu, 1)
                e.wait_ge(k.s_up_hi, m + (half * MTH + 1))
                TTn(rtil(k.u_lo, m), til(k.u_t, 2 + j % 2), rtil(k.u_hi, m).bitcast(F32),
                    ALU.subtract).then_inc(k.s_up_lo, 1)
        for b in range(2):
            freed[b] += MTH // 2
        residual(pan0 + 16, (2, 1), "ln1", feeds=half == 1)

    invert(5, k.rstd)
    st = lambda n: til(k.s_t, n)
    with e.Fori(0, KT) as i:
        chain.c.enter(i, 12)

        def leave(dst, bank, tile):
            e.wait_ge(k.s_panel_used, i * 8 + (SPLIT + PAN_S6 + MIX_LAST[tile] + 1))
            TTn(dst, k.ps[bank][:], k.rstd[:], ALU.mult).then_inc(k.acc_free[bank], 1)
            e.wait_ge(k.acc_free[bank], i * (2 if bank == 0 else 1) + (freed[bank] + (2 if tile == 6 else 1)))

        leave(st(7), 0, 0)
        u = st(0)
        for s in range(4):
            w = k.vec[:, bass.ds(i * 4 + (VEC["conv_b"][0] + 3 - s), 1)]
            if s == 0:
                ins = TS(u, st(7), w, k.vec[:, bass.ds(i + VEC["conv_bb"][0], 1)], ALU.mult, ALU.add)
            else:
                ins = STT(out=u[:, s:T], in0=st(7)[:, 0:T - s], scalar=w, in1=u[:, s:T], op0=ALU.mult, op1=ALU.add)
            if s == 3:
                ins.then_inc(k.s_s2_u, 1)
            else:
                chain(ins)
        e.wait_ge(k.s_s2_uhi, i + 1)
        TTn(k.ub_lo[:], u, k.ub_hi[:].bitcast(F32), ALU.subtract).then_inc(k.s_s2_ulo, 1)
        leave(st(1), 1, 1)
        e.sem_inc(k.s_s2_gl, 1)
        e.wait_ge(k.s_s2_gsq, i + 1)
        chain(TS(st(2), st(2), 0.044715, 1.0, ALU.mult, ALU.add))
        TTn(st(2), st(2), st(1), ALU.mult).then_inc(k.s_s2_gt, 1)
        for n in range(2):
            leave(rtil(k.gates, i + n * KT), 4 + n, 2 + n)
            e.sem_inc(k.s_s2_gate, 1)
        e.wait_ge(k.s_s2_gsig, i + 1)
        chain(TTn(st(1), st(1), st(2), ALU.mult))
        e.wait_ge(k.s_s2_i, i + 1)
        e.sem_inc(k.acc_free[2], 1)
        e.sem_inc(k.acc_free[3], 1)
        e.wait_ge(k.s_s2_a2, i + 1)
        e.wait_ge(k.s_s2_th, i + 1)
        STT(out=st(7), in0=st(7), scalar=1.0, in1=st(6), op0=ALU.add, op1=ALU.mult).then_inc(k.s_s2_m, 1)
        chain(TTn(st(4), st(4), st(0), ALU.mult))
        e.wait_ge(k.s_s2_s, i + 1)
        chain(TTn(st(4), st(4), st(7), ALU.mult))
        chain(e.tensor_tensor_scan(st(8), st(5), st(4), 0.0, ALU.mult, ALU.add))
        TTn(st(8), st(8), st(1), ALU.mult).then_inc(k.s_s2_yb, 1)
        e.wait_ge(k.s_s2_yb_hi, i + 1)
        TTn(rtil(k.yb_lo, i), st(8), rtil(k.yb_hi, i).bitcast(F32), ALU.subtract)
        leave(st(0), 6, 4)
        leave(st(1), 7, 5)
        leave(st(2), 0, 6)
        chain(TTn(st(2), st(2), st(1), ALU.mult))
        for s in range(3):
            w = k.vec[:, bass.ds(i * 3 + (VEC["conv_a"][0] + 2 - s), 1)]
            if s == 0:
                chain(TS(st(3), st(2), w, None, ALU.mult))
            else:
                chain(STT(out=st(3)[:, s:T], in0=st(2)[:, 0:T - s], scalar=w, in1=st(3)[:, s:T], op0=ALU.mult,
                          op1=ALU.add))
        TTn(st(3), st(3), st(0), ALU.mult).then_inc(k.s_s2_ya, 1)
        e.wait_ge(k.s_s2_ya_hi, i + 1)
        TTn(rtil(k.ya_lo, i), st(3), rtil(k.ya_hi, i).bitcast(F32), ALU.subtract).then_inc(k.s_s2_free, 1)
        assert chain.c.n == 12, chain.c.n
        chain.c.leave(KT)
    for b in range(8):
        freed[b] += KT * (2 if b == 0 else 1)

    e.wait_ge(k.s_s2_gate_done, 2 * KT)
    with e.Fori(0, KT // 2) as i:
        chain.c.enter(i, 4)
        for j in range(2):
            for n in range(2):
                b = 2 * j + n
                e.wait_ge(k.s_panel_used, i * 4 + (SPLIT + PAN_S7 + b + 1))
                TTn(st(b), k.ps[b][:], rtil(k.gates, i * 2 + (j + n * KT)), ALU.mult).then_inc(k.acc_free[b], 1)
                e.wait_ge(k.acc_free[b], i + (freed[b] + 1))
            chain(TTn(st(2 * j), st(2 * j), st(2 * j + 1), ALU.add))
            e.sem_inc(k.s_mg, 1)
            e.wait_ge(k.s_mg_hi, i * 2 + j + 1)
            ins = TTn(rtil(k.mg_lo, i * 2 + j), st(2 * j), rtil(k.mg_hi, i * 2 + j).bitcast(F32), ALU.subtract)
            chain(ins)
            e.sem_inc(k.s_mg_lo, 1)
        chain.c.leave(KT // 2)
    for b in range(4):
        freed[b] += KT // 2
    residual(PAN_S8, (1, 1), "ln2")

    invert(6, k.rstd)
    with e.Fori(0, FFN // 2) as i:
        for j in range(2):
            for n in range(2):
                b = 2 * j + n
                e.wait_ge(k.s_panel_used, i * 4 + (SPLIT + PAN_S9 + b + 1))
                TTn(til(k.f_t, j + 2 * n), k.ps[b][:], k.rstd[:], ALU.mult).then_inc(k.acc_free[b], 1)
                e.wait_ge(k.acc_free[b], i + (freed[b] + 1))
                if n == 0:
                    e.sem_inc(k.s_f_g, 1)
            e.wait_ge(k.s_f_silu, i * 2 + j + 1)
            TTn(til(k.f_t, j), til(k.f_t, j), til(k.f_t, 2 + j), ALU.mult).then_inc(k.s_f_hid, 1)
            e.wait_ge(k.s_f_hi_done, i * 2 + j + 1)
            TTn(rtil(k.f_lo, i * 2 + j), til(k.f_t, j), rtil(k.f_hi, i * 2 + j).bitcast(F32),
                ALU.subtract).then_inc(k.s_f_lo_done, 1)
    for b in range(4):
        freed[b] += FFN // 2
    residual(PAN_DOWN, (4, 1), "final", split=False)

    invert(7, k.rstd)
    for m in range(KT):
        x = til(k.x, m)
        STT(out=x, in0=x, scalar=col(k, "final", m), in1=k.rstd[:], op0=ALU.mult, op1=ALU.mult).then_inc(k.s_out_ready, 1)


def program(nc, d, out):
    with ExitStack() as ctx:
        k = plan_memory(nc, ctx)
        signals(nc, ctx, k)
        block = ctx.enter_context(nc.Block())

        @block.sync
        def _(sp):
            sync_program(nc, k, d)
            for m in range(KT):
                sp.wait_ge(k.s_out_ready, m + 1)
                sp.dma_start(out[m * P:(m + 1) * P, :], til(k.x, m)).then_inc(k.s_out_sent, 16)
            sp.wait_ge(k.s_out_sent, 16 * KT)

        @block.gpsimd
        def _(pool):
            gpsimd_program(nc, k)

        @block.scalar
        def _(act):
            scalar_program(nc, k, d)

        @block.vector
        def _(dve):
            vector_program(nc, k)

        @block.tensor
        def _(pe):
            tensor_program(nc, k)


def constants():
    import numpy as np

    j, i = np.arange(P)[:, None], np.arange(P)[None, :]
    parts = [j == i, np.ones((P, P)), j // 64 == i // 64, j <= i]
    for lev in range(LEVELS):
        s = 1 << lev
        parts.append((j // (2 * s) == i // (2 * s)) & (j % (2 * s) < s) & (i % (2 * s) >= s))
    parts.append(np.zeros((P, T - P)))
    c = np.concatenate([p.astype(np.float32) for p in parts], 1)
    return np.concatenate([c, np.where(i <= j, 0.0, MASKED).astype(np.float32)], 1)


def panels(w):
    kk, m = w.shape
    return w.reshape(kk // P, P, m // P, P).transpose(2, 1, 0, 3).reshape(m // P, P, kk)


def kernel(**inputs):
    import numpy as np
    import concourse.bacc as bacc
    from concourse.bass_utils import run_bass_kernel_spmd

    a = {n: np.asarray(v) for n, v in inputs.items()}
    f = np.float32
    cat = np.concatenate
    w = a["w_in"][0]
    last = cat([w[:, 2440:2504], w[:, 2048:2056], w[:, 2504:2508], np.zeros((D, 52), f)], 1)
    w_in = cat([w[:, 2056:2440], last, w[:, 2508:3020], w[:, 0:2048]], 1)
    kv = a["xa_wkv"][0]
    wk = panels(kv[:, 0:512])
    wv = kv[:, 512:].reshape(4, 2, P, T).transpose(0, 2, 1, 3).reshape(4, P, 2 * T)
    wo = panels(a["xa_wo"][0]).reshape(4, 2, P, T).transpose(0, 2, 1, 3).reshape(4, P, 2 * T)
    up = panels(a["mlp_w1"][0])
    dn = panels(a["mlp_w2"][0]).reshape(KT, P, 2, 2, D).transpose(2, 0, 3, 1, 4).reshape(2, 2 * KT, P, D)
    panels_a = cat([wk, wv, panels(w_in), panels(a["w_out"][0]), panels(a["xa_wq"][0]), wo,
                    up[:MTH], dn[0], up[MTH:], dn[1]], 0)
    w2 = panels(a["w_in_2"][0]).reshape(7, KT, P, D)
    lru = np.zeros((KT, 2, 64, 2, 2, 64), f)
    for n, name in enumerate(("lru_wa_2", "lru_wx_2")):
        g = a[name][0].reshape(KT, 2, 64, 64)
        for b in range(2):
            lru[:, b, :, n, b, :] = g[:, b]
    lru = lru.reshape(KT, P, 2 * P)
    mix = cat([w2[3], w2[4], w2[5], w2[6], lru, w2[0], w2[1], w2[2]], 2)
    merge = np.stack([panels(a["w_out_a_2"][0]), panels(a["w_out_b_2"][0])], 1).reshape(2 * KT, P, D)
    ffn = np.stack([panels(a["w_ffn_gate_2"][0]), panels(a["w_ffn_up_2"][0])], 1).reshape(2 * FFN, P, D)
    panels_b = cat([merge, panels(a["w_o_2"][0]), ffn], 0)
    down = panels(a["w_ffn_down_2"][0])
    kvb = a["dsa_w_kvb"][0]
    two = lambda m: m.reshape(2, P, 256).transpose(1, 0, 2).reshape(P, 512)
    small = cat([two(a["dsa_w_qb"][0]), two(a["dsa_w_qi"][0]), kvb[:, :64], kvb[:, :64], kvb[:, 64:]], 1)

    def cols(v):
        return v.reshape(-1, P).T

    def taps(v):
        n, c = v.shape
        return v.reshape(n, c // P, P).transpose(2, 1, 0).reshape(P, -1)

    def rows(v):
        return np.broadcast_to(np.tile(v, TT)[None], (P, 16))

    vec = cat([cols(a["norm_mix"]), cols(a["norm_mem"]), cols(a["norm_cross"]), cols(a["norm_mlp"]), cols(a["ln1_g_2"]),
               cols(a["ln2_g_2"]), cols(a["final_g_2"]), taps(a["gdn_conv"][0]), cols(a["gdn_norm"]),
               cols(np.tile(a["dsa_q_norm"], (1, 2))), cols(np.tile(a["dsa_k_norm"], (1, 2))), taps(a["conv_dw"][0]),
               cols(a["conv_dw_b"]), cols(a["conv_ln_g"]), cols(a["conv_ln_b"]), cols(a["xa_q_norm"]),
               cols(a["xa_k_norm"]), taps(a["conv_a_w_2"][0]), taps(a["conv_b_w_2"][0]), cols(a["conv_b_b_2"]),
               cols(a["lru_ba_2"]), cols(a["lru_bx_2"]), cols(a["lru_lambda_2"]), cols(a["gate_bias_2"]),
               rows(a["gdn_a_log"][0]), rows(a["gdn_dt_bias"][0])], 1)
    arrays = {
        "xT": a["x"][0].T, "memT": a["mem"][0].T, "const": constants(), "vec": vec, "small_w": small,
        "panels_a": panels_a, "mix": mix, "panels_b": panels_b, "down": down,
    }
    arrays = {n: np.ascontiguousarray(v) for n, v in arrays.items()}
    nc = bacc.Bacc("TRN2", target_bir_lowering=False, num_devices=1, dynamic_dma_scratch_size=1024)
    ap = {n: nc.dram_tensor(n, v.shape, F32, kind="ExternalInput").ap() for n, v in arrays.items()}
    d = Plan()
    d.x, d.mem, d.const, d.vec, d.small_w = ap["xT"], ap["memT"], ap["const"], ap["vec"], ap["small_w"]
    d.panels_a, d.mix, d.panels_b, d.down = ap["panels_a"], ap["mix"], ap["panels_b"], ap["down"]
    out = nc.dram_tensor("outT", (D, T), F32, kind="ExternalOutput").ap()
    program(nc, d, out)
    got = run_bass_kernel_spmd(nc, [arrays], core_ids=[0]).results[0]["outT"]
    return np.ascontiguousarray(got.T)[None]
```

```python
from contextlib import ExitStack

import concourse.bass as bass
from concourse import mybir

P = 128
T = 512
D = 1024
KT = D // P
MEM = 256
TT = T // P
HEADS = 4
EPS = 1e-6
BLK = 8
PANEL = BLK * P
RAW = 4
SPLIT = 2
LEVELS = 7
TOPK = 128
MASKED = -3.0e38
TAKEN = -3.3e38
MT1, MTH = 24, 16
FFN = 22
DOWN_CUTS = (0, 6, 12, 17, 22)
MIX_CUTS = (0, 7, 14, 21, 28, 36, 43, 50, 58)
MIX_TILES = [(0, 8), (8, 16), (16, 24), (24, 32), (34, 42), (42, 50), (50, 58)]
MIX_LAST = [next(p for p in range(8) if b <= MIX_CUTS[p + 1]) for _, b in MIX_TILES]
MIX_GATES = next(p for p in range(8) if 34 <= MIX_CUTS[p + 1])
CONV_TAPS = 31
PAD = 32
CQ, CKV, REST, UG, QKV, Z = 0, 2, 3, 4, 8, 20

F32 = mybir.dt.float32
F32R = mybir.dt.float32r
ACT = mybir.ActivationFunctionType
ALU = mybir.AluOpType
AX = mybir.AxisListType

VEC_WIDTHS = [
    ("norm_mix", 8), ("norm_mem", 8), ("norm_cross", 8), ("norm_mlp", 8), ("ln1", 8), ("ln2", 8), ("final", 8),
    ("gdn_conv", 48), ("gdn_norm", 1), ("dsa_q", 1), ("dsa_k", 1), ("dw", 2 * CONV_TAPS), ("dw_b", 2),
    ("cln_g", 2), ("cln_b", 2), ("xa_q", 1), ("xa_k", 1), ("conv_a", 24), ("conv_b", 32), ("conv_bb", 8),
    ("lru_ba", 8), ("lru_bx", 8), ("lam", 8), ("gate_b", 16), ("a_log", 16), ("dt_bias", 16),
]
VEC = {}
_at = 0
for _n, _w in VEC_WIDTHS:
    VEC[_n] = (_at, _w)
    _at += _w
NVEC = _at
C_ID, C_ONE, C_BLK, C_TRI, C_LEV = 0, P, 2 * P, 3 * P, 4 * P
C_CAUS = C_LEV + LEVELS * P
NCONST = C_CAUS + T


TOK_A, TOK_W, TOK_G, TOK_BETA, TOK_DEC, TOK_LAST = 0, 48, 64, 80, 96, 112
TOK_EDEC, TOK_EKD, TOK_ELAST, TOK_SP = 128, 144, 160, 176
TOK_N8, TOK_P8, TOK_RTOK, TOK_MX, TOK_NM, TOK_SUM, TOK_R, TOK_EA, TOK_M8 = 296, 304, 312, 320, 328, 336, 344, 352, 368
TOK_RDQ, TOK_RC, TOK_RG = 392, 416, 424
NTOK = 456


SQ_G, SQ_DQ, SQ_GO, SQ_AQ = 1, 9, 12, 16
GRP_G, GRP_DQ, GRP_C, GRP_GO, GRP_AQ = 1, 2, 3, 4, 5
ROW_DQ, ROW_C, ROW_G, ROW_GO, ROW_AQ = 0, 3, 4, 12, 16


class Count:

    def __init__(self, start=0):
        self.base, self.i, self.per, self.n = start, None, 0, 0

    def enter(self, i, per):
        self.base += self.n
        self.i, self.per, self.n = i, per, 0

    def leave(self, times):
        assert self.n == self.per, (self.n, self.per)
        self.base += times * self.per
        self.i, self.n = None, 0

    def at(self, k=0):
        v = self.base + self.n + k
        return v if self.i is None else self.i * self.per + v

    def step(self, k=1):
        self.n += k
        return self.at()


class Chain:

    def __init__(self, engine, sem):
        self.e, self.sem, self.c = engine, sem, Count()

    def __call__(self, ins):
        ins.then_inc(self.sem, 1)
        self.e.wait_ge(self.sem, self.c.step())
        return ins


class Plan:
    pass


def plan_memory(nc, ctx):
    k = Plan()

    top = [0]

    def sb(name, cols, dt=F32, at=None):
        cols = -(-cols // 8) * 8
        if at is None:
            at = top[0]
            top[0] += cols * 4
        return nc.alloc_sbuf_tensor_at(name, [P, cols], dt, offset=at), at + cols * 4

    base = (nc.sbuf_base + 63) // 64 * 64
    top[0] = base
    k.raw, _ = sb("raw", RAW * PANEL)
    k.w_hi, _ = sb("w_hi", SPLIT * PANEL, F32R)
    k.w_lo, _ = sb("w_lo", SPLIT * PANEL, F32R)
    k.x, _ = sb("x", KT * T)
    k.const, _ = sb("const", NCONST)
    k.vec, _ = sb("vec", NVEC)
    k.eps, _ = sb("eps", 4)
    k.rstd, _ = sb("rstd", T)
    k.sqacc, _ = sb("sqacc", T)
    k.sq, _ = sb("sq", 2 * T)
    k.tok, _ = sb("tok", NTOK)
    h0 = top[0]
    k.h_hi, _ = sb("h_hi", KT * T, F32R)
    k.h_lo, _ = sb("h_lo", KT * T, F32R)
    r0 = top[0]
    k.limit = nc.sbuf_usable_end
    k.proj, a = sb("proj", MT1 * T, at=r0)
    proj_end = a
    k.xk, a = sb("xk", HEADS * MEM, at=a)
    k.xv, a = sb("xv", 2 * T, at=a)
    q0 = a
    k.qkv, a = sb("qkv", 12 * T, at=q0)
    y0 = a
    k.mem, b = sb("mem", KT * MEM, at=q0)
    k.m_hi, b = sb("m_hi", KT * MEM, F32R, at=b)
    k.m_lo, b = sb("m_lo", KT * MEM, F32R, at=b)
    k.m_rstd, b = sb("m_rstd", MEM, at=b)
    k.m_sqa, _ = sb("m_sqa", MEM, at=b)
    k.y_hi, a = sb("y_hi", KT * T, F32R, at=y0)
    k.y_lo, a = sb("y_lo", KT * T, F32R, at=a)
    k.small_w, a = sb("small_w", 2 * 512 + P + 64, at=a)
    assert a <= k.limit, (a, k.limit)
    k.d_qi, b = sb("d_qi", 2 * T, at=h0)
    k.d_ki, b = sb("d_ki", T, at=b)
    k.d_relu, b = sb("d_relu", 2 * T, at=b)
    k.d_rk, b = sb("d_rk", T, at=b)
    k.d_v, b = sb("d_v", 2 * T, at=r0 + CQ * T * 4)
    k.d_score_a, b = sb("d_score_a", 5 * P, at=b)
    k.d_q, b = sb("d_q", 2 * T, at=r0 + UG * T * 4)
    k.d_k, b = sb("d_k", T, at=b)
    k.d_score_b, b = sb("d_score_b", T, at=b)
    assert b <= r0 + QKV * T * 4
    k.d_p, b = sb("d_p", 2 * T, at=y0)
    k.d_pt, b = sb("d_pt", 2 * T, at=b)
    k.c_acc, b = sb("c_acc", 2 * T, at=y0)
    k.c_t, b = sb("c_t", 2 * T, at=b)
    k.c_y, b = sb("c_y", 2 * (PAD + T), at=y0 + KT * T * 4)
    assert b <= y0 + (KT + 4) * T * 4
    k.g_sq = [sb(f"g_sq{n}", HEADS * T, at=y0 + (4 + KT * n) * T * 4)[0] for n in range(2)]
    k.g_ek, b = sb("g_ek", HEADS * T, at=h0)
    k.g_kdec, b = sb("g_kdec", HEADS * T, at=b)
    k.g_v, b = sb("g_v", HEADS * T, at=b)
    k.g_at, b = sb("g_at", HEADS * T, at=b)
    assert b <= r0
    k.g_qk, b = sb("g_qk", HEADS * T, at=r0 + QKV * T * 4)
    k.g_x, b = sb("g_x", HEADS * T, at=b)
    k.g_xt, b = sb("g_xt", HEADS * T, at=b)
    k.g_b, _ = sb("g_b", 2 * T, at=y0)
    k.g_p, _ = sb("g_p", 2 * T, at=y0 + 2 * T * 4)
    k.g_vn, _ = sb("g_vn", 4 * P, at=y0 + KT * T * 4)
    k.g_mask, _ = sb("g_mask", 2 * P, at=y0 + KT * T * 4 + 8 * P * 4)
    k.g_s, _ = sb("g_s", 4 * P, at=y0 + KT * T * 4 + 4 * P * 4)
    k.a_q, b = sb("a_q", HEADS * T, at=r0)
    k.a_p, b = sb("a_p", 4 * T, at=b)
    k.a_pt, b = sb("a_pt", 2 * T, at=b)
    assert b <= proj_end
    k.ao_hi, b = sb("ao_hi", HEADS * T, F32R, at=q0)
    k.ao_lo, b = sb("ao_lo", HEADS * T, F32R, at=b)
    k.u_hi, b = sb("u_hi", MTH * T, F32R, at=r0)
    k.u_lo, b = sb("u_lo", MTH * T, F32R, at=b)
    k.u_t, b = sb("u_t", 4 * T, at=b)
    assert b <= k.limit
    k.ya_hi, b = sb("ya_hi", KT * T, F32R, at=r0)
    k.ya_lo, b = sb("ya_lo", KT * T, F32R, at=b)
    k.yb_hi, b = sb("yb_hi", KT * T, F32R, at=b)
    k.yb_lo, b = sb("yb_lo", KT * T, F32R, at=b)
    k.mg_hi, _ = sb("mg_hi", KT * T, F32R, at=b)
    k.mg_lo, _ = sb("mg_lo", KT * T, F32R, at=b + KT * T * 4)
    k.gates, b = sb("gates", 2 * KT * T, at=b)
    k.ub_hi, b = sb("ub_hi", T, F32R, at=b)
    k.ub_lo, b = sb("ub_lo", T, F32R, at=b)
    k.s_t, b = sb("s_t", 9 * T, at=b)
    assert b <= k.limit, (b, k.limit)
    k.f_hi, b = sb("f_hi", FFN * T, F32R, at=r0)
    k.f_lo, b = sb("f_lo", FFN * T, F32R, at=b)
    k.f_t, b = sb("f_t", 4 * T, at=b)
    assert b <= k.limit, (b, k.limit)
    k.ps = [ctx.enter_context(nc.psum_tensor(f"acc{i}", [P, T], F32)) for i in range(8)]
    return k


def signals(nc, ctx, k):

    def sem(name):
        return ctx.enter_context(nc.semaphore(name))

    k.s_ld_x = sem("ld_x")
    k.s_ld_mem = [sem(f"ld_mem{n}") for n in range(2)]
    k.s_ld_const = sem("ld_const")
    k.s_ld_vec = sem("ld_vec")
    k.s_ld_small = sem("ld_small")
    k.s_split_done = sem("split_done")
    k.s_weights_hi = sem("weights_hi")
    k.s_panel_used = sem("panel_used")
    k.s_fed_hi = sem("fed_hi")
    k.s_fed_sq = sem("fed_sq")
    k.s_fed_lo = sem("fed_lo")
    k.s_sq_used = sem("sq_used")
    k.s_ssq = sem("ssq")
    k.s_std = sem("std")
    k.s_rstd = sem("rstd")
    k.s_x_new = sem("x_new")
    k.s_zeroed = sem("zeroed")
    k.s_act_chain = sem("act_chain")
    k.s_dve_chain = sem("dve_chain")
    k.s_xk_raw = sem("xk_raw")
    k.s_tokr_t = sem("tokr_t")
    k.s_v_done = sem("v_done")
    k.s_xk_done = sem("xk_done")
    k.s_unit_sq = sem("unit_sq")
    k.s_unit_sum = sem("unit_sum")
    k.s_unit_std = sem("unit_std")
    k.s_unit_inv = sem("unit_inv")
    k.s_unit_row = sem("unit_row")
    k.s_proj_done = sem("proj_done")
    k.s_ki_dup = sem("ki_dup")
    k.s_dq_mm = sem("dq_mm")
    k.s_dq_raw = sem("dq_raw")
    k.s_d_gates = sem("d_gates")
    k.s_d_gates_tok = sem("d_gates_tok")
    k.s_dq_done = sem("dq_done")
    k.s_dv_done = sem("dv_done")
    k.s_idx_mm = sem("idx_mm")
    k.s_idx_relu = sem("idx_relu")
    k.s_idx_used = sem("idx_used")
    k.s_lg_mm = sem("lg_mm")
    k.s_lg_masked = sem("lg_masked")
    k.s_p_exp = sem("p_exp")
    k.s_p_norm = sem("p_norm")
    k.s_pt_mm = sem("pt_mm")
    k.s_pt_copied = sem("pt_copied")
    k.s_o_mm = sem("o_mm")
    k.s_y_hi = sem("y_hi")
    k.s_y_lo = sem("y_lo")
    k.s_c_sig = sem("c_sig")
    k.s_c_conv = sem("c_conv")
    k.s_c_mean = sem("c_mean")
    k.s_c_cent = sem("c_cent")
    k.s_c_sq = sem("c_sq")
    k.s_c_norm = sem("c_norm")
    k.s_c_silu = sem("c_silu")
    k.s_g_conv = sem("g_conv")
    k.s_g_silu = sem("g_silu")
    k.s_g_qk_done = sem("g_qk_done")
    k.s_sp_in = sem("sp_in")
    k.s_sp_exp = sem("sp_exp")
    k.s_beta_done = sem("beta_done")
    k.s_g_ready = sem("g_ready")
    k.s_dec_mm = sem("dec_mm")
    k.s_dec_copied = sem("dec_copied")
    k.s_dec_exp = sem("dec_exp")
    k.s_decrow = sem("decrow")
    k.s_gam_d = sem("gam_d")
    k.s_gam_e = sem("gam_e")
    k.s_edecrow = sem("edecrow")
    k.s_gam_done = sem("gam_done")
    k.s_qk_mm = sem("qk_mm")
    k.s_qk_done = sem("qk_done")
    k.s_kk_mm = sem("kk_mm")
    k.s_at_done = sem("at_done")
    k.s_kt_mm = sem("kt_mm")
    k.s_ek_done = sem("ek_done")
    k.s_vt_mm = sem("vt_mm")
    k.s_v_tok_done = sem("v_tok_done")
    k.s_x_init = sem("x_init")
    k.s_x_turned = sem("x_turned")
    k.s_x_first = sem("x_first")
    k.s_mask = sem("mask")
    k.s_bt_done = sem("bt_done")
    k.s_p_mm = sem("p_mm")
    k.s_p_copied = sem("p_copied")
    k.s_xp_mm = sem("xp_mm")
    k.s_x_done = sem("x_done")
    k.s_wt_mm = sem("wt_mm")
    k.s_wt_done = sem("wt_done")
    k.s_vn_mm = sem("vn_mm")
    k.s_vn_done = sem("vn_done")
    k.s_o_part = sem("o_part")
    k.s_st_mm = sem("st_mm")
    k.s_st_done = sem("st_done")
    k.s_o_copied = sem("o_copied")
    k.s_go_norm = sem("go_norm")
    k.s_z_silu = sem("z_silu")
    k.s_aq_raw = sem("aq_raw")
    k.s_aq_done = sem("aq_done")
    k.s_al_mm = sem("al_mm")
    k.s_al_max = sem("al_max")
    k.s_al_exp = sem("al_exp")
    k.s_al_norm = sem("al_norm")
    k.s_apt_mm = sem("apt_mm")
    k.s_apt_copied = sem("apt_copied")
    k.s_av_mm = sem("av_mm")
    k.s_ao_hi_done = sem("ao_hi_done")
    k.s_ao_lo_done = sem("ao_lo_done")
    k.s_up_relu = sem("up_relu")
    k.s_up_sq = sem("up_sq")
    k.s_up_hi = sem("up_hi")
    k.s_up_lo = sem("up_lo")
    k.s_s2_u = sem("s2_u")
    k.s_s2_uhi = sem("s2_uhi")
    k.s_s2_ulo = sem("s2_ulo")
    k.s_s2_gl = sem("s2_gl")
    k.s_s2_gsq = sem("s2_gsq")
    k.s_s2_gt = sem("s2_gt")
    k.s_s2_gsig = sem("s2_gsig")
    k.s_s2_gate = sem("s2_gate")
    k.s_s2_gate_done = sem("s2_gate_done")
    k.s_s2_r = sem("s2_r")
    k.s_s2_i = sem("s2_i")
    k.s_s2_a = sem("s2_a")
    k.s_s2_th = sem("s2_th")
    k.s_s2_a2 = sem("s2_a2")
    k.s_s2_m = sem("s2_m")
    k.s_s2_s = sem("s2_s")
    k.s_s2_yb = sem("s2_yb")
    k.s_s2_yb_hi = sem("s2_yb_hi")
    k.s_s2_ya = sem("s2_ya")
    k.s_s2_ya_hi = sem("s2_ya_hi")
    k.s_s2_free = sem("s2_free")
    k.s_mg = sem("mg")
    k.s_mg_hi = sem("mg_hi")
    k.s_mg_lo = sem("mg_lo")
    k.s_f_g = sem("f_g")
    k.s_f_silu = sem("f_silu")
    k.s_f_hid = sem("f_hid")
    k.s_f_hi_done = sem("f_hi_done")
    k.s_f_lo_done = sem("f_lo_done")
    k.s_out_ready = sem("out_ready")
    k.s_out_sent = sem("out_sent")
    k.landed = [sem(f"landed{j}") for j in range(RAW)]
    k.acc_free = [sem(f"acc_free{b}") for b in range(8)]


STREAM = [("panels_a", 28, [PANEL] * 4),
          ("mix", 8, [(b - a) * P for a, b in zip(MIX_CUTS, MIX_CUTS[1:])]),
          ("panels_b", 17, [PANEL] * 4),
          ("down", 8, [(b - a) * P for a, b in zip(DOWN_CUTS, DOWN_CUTS[1:])])]


class Panels(Count):

    def landed(self):
        v = 16 * (self.base // RAW) + 16 * (self.n // RAW) + 16
        return v if self.i is None else self.i * (16 * (self.per // RAW)) + v


def col(k, name, j=0, rows=slice(0, P)):
    at = VEC[name][0] + j
    return k.vec[rows, at:at + 1]


def til(buf, j, n=1, w=T):
    return buf[:, j * w:(j + n) * w]


def rtil(buf, j, w=T):
    return buf[:, bass.ds(j * w, w)]


def sync_program(nc, k, d):
    e = nc.sync
    e.dma_start(k.vec[:, 0:NVEC], d.vec).then_inc(k.s_ld_vec, 16)
    for n in range(2):
        h = KT // 2
        e.dma_start(k.mem[:, n * h * MEM:(n + 1) * h * MEM].rearrange("p (k t) -> p k t", k=h),
                    d.mem[n * h * P:(n + 1) * h * P].rearrange("(k p) t -> p k t", p=P)).then_inc(k.s_ld_mem[n], 16)
    e.dma_start(k.const[:], d.const).then_inc(k.s_ld_const, 16)
    pan = Panels()
    first = True
    for name, times, widths in STREAM:
        src = stream_array(d, name)
        with e.Fori(0, times) as i:
            pan.enter(i, len(widths))
            at = 0
            for j, w in enumerate(widths):
                e.wait_ge(k.s_split_done, pan.at(1))
                if name in ("panels_a", "panels_b"):
                    part = src[bass.ds(i * 4 + j, 1)].rearrange("a p n -> (a p) n")
                else:
                    part = src[bass.ds(i, 1)].rearrange("a p n -> (a p) n")[:, at:at + w]
                e.dma_start(k.raw[:, (j % RAW) * PANEL:(j % RAW) * PANEL + w], part).then_inc(k.landed[j % RAW], 16)
                at += w
                pan.step()
            pan.leave(times)


def stream_array(d, name):
    return {"panels_a": d.panels_a, "mix": d.mix, "panels_b": d.panels_b, "down": d.down}[name]


def gpsimd_program(nc, k):
    e = nc.gpsimd
    e.sem_inc(k.s_split_done, RAW)
    one = k.eps[:, 2:3]
    e.wait_ge(k.s_zeroed, 1)
    pan = Panels()

    def split(times, widths):
        with e.Fori(0, times) as i:
            pan.enter(i, len(widths))
            for j, w in enumerate(widths):
                raw = k.raw[:, (j % RAW) * PANEL:(j % RAW) * PANEL + w]
                hi = k.w_hi[:, (j % SPLIT) * PANEL:(j % SPLIT) * PANEL + w]
                lo = k.w_lo[:, (j % SPLIT) * PANEL:(j % SPLIT) * PANEL + w]
                e.wait_ge(k.landed[j % RAW], pan.landed())
                e.wait_ge(k.s_panel_used, pan.at(1))
                e.tensor_tensor(hi, raw, one.broadcast_to([P, w]), ALU.mult).then_inc(k.s_weights_hi, 1)
                e.wait_ge(k.s_weights_hi, pan.at(1))
                e.tensor_tensor(lo, raw, hi.bitcast(F32), ALU.subtract).then_inc(k.s_split_done, 1)
                pan.step()
            pan.leave(times)

    name, times, widths = STREAM[0]
    before = (8 + MT1) // 4
    split(before, widths)
    e.wait_ge(k.s_at_done, HEADS)
    with e.Fori(0, (LEVELS - 1) // 2) as pair:
        for par in range(2):
            m = k.g_mask[:, par * P:(par + 1) * P]
            e.tensor_tensor(m, k.const[:, bass.ds(pair * (2 * P) + (C_LEV + (1 + par) * P), P)],
                            one.broadcast_to([P, P]), ALU.mult).then_inc(k.s_mask, 1)
            mask = m.unsqueeze(1).broadcast_to([P, TT, P])
            for h in range(HEADS):
                e.wait_ge(k.s_mask, pair * 2 + par + 1)
                e.wait_ge(k.s_p_copied, pair * (2 * HEADS) + (par * HEADS + h + 1))
                e.tensor_tensor(til(k.g_b, h % 2).rearrange("p (c i) -> p c i", c=TT),
                                til(k.g_at, h).rearrange("p (c i) -> p c i", c=TT), mask,
                                ALU.mult).then_inc(k.s_bt_done, 1)
    split(times - before, widths)
    for name, times, widths in STREAM[1:]:
        split(times, widths)


class Acc:

    def __init__(self, k):
        self.k, self.c = k, [Count() for _ in range(8)]

    def enter(self, i, per):
        for c, n in zip(self.c, per):
            c.enter(i, n)

    def leave(self, times):
        for c in self.c:
            c.leave(times)

    def take(self, e, b):
        e.wait_ge(self.k.acc_free[b], self.c[b].step())
        return self.k.ps[b]


def tensor_program(nc, k):
    e = nc.tensor
    pan, acc = Panels(), Acc(k)
    e.sem_inc(k.s_panel_used, SPLIT)
    ident = k.const[:, C_ID:C_ID + P]
    ones = k.const[:, C_ONE:C_ONE + P]
    blk = k.const[:, C_BLK:C_BLK + P]
    tri = k.const[:, C_TRI:C_TRI + P]

    def products(out, w_at, wn, a_hi, a_lo, first, last):
        for n, (w, a) in enumerate(((k.w_hi, a_hi), (k.w_hi, a_lo), (k.w_lo, a_hi))):
            mm = e.matmul(out, w[:, w_at:w_at + wn], a, start=first and n == 0, stop=last and n == 2)
        return mm

    def panel(out, hi, lo, tiles, first=True, last=True, at=0, done=True, w=T, ready=None):
        slot = (pan.n % SPLIT) * PANEL
        if at == 0:
            e.wait_ge(k.s_split_done, RAW + pan.at(1))
        for n, t in enumerate(tiles):
            if ready:
                e.wait_ge(ready[0], ready[1] + t + 1)
            mm = products(out, slot + (at + n) * P, P, hi[:, t * w:(t + 1) * w], lo[:, t * w:(t + 1) * w],
                          first and n == 0, last and n == len(tiles) - 1)
        if done:
            mm.then_inc(k.s_panel_used, 1)
            pan.step()

    def sum_squares(n_fed, n_norm, sqacc, w=T):
        e.wait_ge(k.s_sq_used, 2 + n_fed)
        if n_norm > 0:
            e.wait_ge(k.s_std, n_norm)
        e.matmul(k.ps[7][:, 0:w], ones, sqacc[:, 0:w], start=True, stop=True).then_inc(k.s_ssq, 1)

    e.wait_ge(k.s_ld_const, 16)
    sum_squares(KT, 0, k.m_sqa, MEM)
    e.wait_ge(k.s_fed_lo, KT)
    for m in range(HEADS):
        out = acc.take(e, m % 2)
        panel(out[:, 0:MEM], k.m_hi, k.m_lo, range(KT), w=MEM)
    for b in (2, 3):
        acc.take(e, b)
    for j in range(4):
        e.wait_ge(k.s_split_done, RAW + pan.at(1))
        slot = (pan.n % SPLIT) * PANEL
        for kk in range(2):
            t = 2 * j + kk
            for mt in range(2):
                a = t * MEM + mt * P
                for n, (m_, w) in enumerate(((k.m_hi, k.w_hi), (k.m_hi, k.w_lo), (k.m_lo, k.w_hi))):
                    mm = e.matmul(k.ps[2 + mt][:], m_[:, a:a + P], w[:, slot + kk * T:slot + (kk + 1) * T],
                                  start=t == 0 and n == 0, stop=t == KT - 1 and n == 2)
        mm.then_inc(k.s_panel_used, 1)
        pan.step()
    e.wait_ge(k.s_rstd, 1)
    for mt in range(2):
        mm = e.transpose(k.ps[4][:, mt * P:(mt + 1) * P], k.m_rstd[:, mt * P:(mt + 1) * P], ident)
    mm.then_inc(k.s_tokr_t, 1)
    e.wait_ge(k.s_unit_sq, 1)
    for j in range(2):
        mm = e.matmul(k.ps[5 + j][:], ones, k.mem[:, j * T:(j + 1) * T], start=True, stop=True)
    mm.then_inc(k.s_unit_sum, 1)

    sum_squares(2 * KT, 1, k.sqacc)
    e.wait_ge(k.s_fed_lo, 2 * KT)
    with e.Fori(0, 6) as i:
        pan.enter(i, 4)
        acc.enter(i, [1, 1, 1, 1, 0, 0, 0, 0])
        for j in range(4):
            panel(acc.take(e, j)[:], k.h_hi, k.h_lo, range(KT))
        pan.leave(6)
        acc.leave(6)

    def token_sums(bank, src):
        for h, sq in enumerate(src):
            for c in range(TT):
                mm = e.matmul(k.ps[bank][:, h * TT + c:h * TT + c + 1], sq[:, c * P:(c + 1) * P], ones[:, 0:1],
                              start=True, stop=True)
        mm.then_inc(k.s_unit_sum, 1)

    e.wait_ge(k.s_unit_sq, SQ_G + 2 * HEADS)
    e.wait_ge(k.s_std, 2)
    token_sums(7, [til(k.g_sq[m // HEADS], m % HEADS) for m in range(2 * HEADS)])

    e.wait_ge(k.s_proj_done, 1)
    e.wait_ge(k.s_ld_small, 16)
    e.wait_ge(k.s_v_done, 2)
    e.matmul(k.ps[4][:], k.small_w[:, 1024:1152], til(k.proj, CKV), start=True, stop=True).then_inc(k.s_dq_mm, 1)
    e.wait_ge(k.s_unit_std, 1)
    for t in range(TT):
        mm = e.matmul(k.ps[5][:, t * 64:(t + 1) * 64], k.proj[:, CKV * T + t * P:CKV * T + (t + 1) * P],
                      k.small_w[:, 1152:1216], start=True, stop=True)
    mm.then_inc(k.s_dq_mm, 1)
    for c in range(TT):
        mm = e.transpose(k.ps[6][:, c * P:(c + 1) * P], k.proj[:, REST * T + c * P:REST * T + (c + 1) * P], ident)
    mm.then_inc(k.s_d_gates, 1)
    for b in range(4):
        e.wait_ge(k.acc_free[b], acc.c[b].at(1))
    for m in range(4):
        for kk in range(2):
            w_at = (0 if m < 2 else 512) + kk * 256 + (m % 2) * P
            mm = e.matmul(k.ps[m][:], k.small_w[:, w_at:w_at + P], til(k.proj, CQ + kk), start=kk == 0, stop=kk == 1)
        mm.then_inc(k.s_dq_mm, 1)
    e.wait_ge(k.s_d_gates_tok, 1)
    for j in range(2):
        e.wait_ge(k.s_c_conv, j + 1)
        mm = e.matmul(k.ps[6][:], ones, til(k.c_acc, j), start=j == 0, stop=j == 1)
    mm.then_inc(k.s_c_mean, 1)
    e.wait_ge(k.s_dv_done, 1)
    for m in range(3):
        e.wait_ge(k.s_unit_sq, SQ_DQ + m + 1)
        src = til(k.d_relu, m) if m < 2 else k.d_rk[:]
        two = blk.rearrange("p (a b) -> p a b", b=64)[:, :, 0]
        for c in range(TT):
            mm = e.matmul(k.ps[5][:, (m * TT + c) * 2:(m * TT + c) * 2 + 2], src[:, c * P:(c + 1) * P], two,
                          start=True, stop=True)
    mm.then_inc(k.s_unit_sum, 1)
    e.wait_ge(k.s_c_sq, 2)
    for c in range(TT):
        for j in range(2):
            mm = e.matmul(k.ps[6][:, c:c + 1], til(k.c_t, j)[:, c * P:(c + 1) * P], ones[:, 0:1], start=j == 0,
                          stop=j == 1)
    mm.then_inc(k.s_unit_sum, 1)

    def row(bank, at, per=1):
        for c in range(TT):
            for j in range(per):
                w, t_ = P // per, at + c * per + j
                mm = e.matmul(k.ps[bank][j * w:(j + 1) * w, c * P:(c + 1) * P],
                              k.tok[:, t_:t_ + 1].broadcast_to([P, w]), ident, start=True, stop=True)
        mm.then_inc(k.s_unit_row, 1)

    e.wait_ge(k.s_dq_raw, 5)
    e.wait_ge(k.s_unit_inv, GRP_DQ)
    for m in range(3):
        row((0, 1, 4)[m], TOK_RDQ + 2 * TT * m, 2)
    e.wait_ge(k.s_unit_inv, GRP_C)
    row(6, TOK_RC)
    for m in range(2 * HEADS):
        if m in (0, 2):
            e.wait_ge(*((k.s_dq_done, 3) if m == 0 else (k.s_c_norm, 2)))
        if m >= 4:
            e.wait_ge(k.s_g_qk_done, m - 3)
        row(4 + m % 4, TOK_RG + TT * m)

    e.wait_ge(k.s_ki_dup, 32)
    e.wait_ge(k.s_dq_raw, 5)
    for qt in range(1, TT):
        cw = (qt + 1) * P
        for h in range(HEADS):
            if qt > 1:
                e.wait_ge(k.s_idx_relu, HEADS * (qt - 2) + h + 1)
            r = slice(64 * (h % 2), 64 * (h % 2) + 64)
            e.matmul(k.ps[h][:, 0:cw], k.d_qi[r, (h // 2) * T + qt * P:(h // 2) * T + (qt + 1) * P],
                     k.d_ki[r, 0:cw], start=True, stop=True).then_inc(k.s_idx_mm, 1)

    e.wait_ge(k.s_g_qk_done, 2 * HEADS)
    e.wait_ge(k.s_g_ready, 1)
    e.matmul(k.ps[7][:, 0:16], tri, k.tok[:, TOK_G:TOK_G + 16], start=True, stop=True)
    e.matmul(k.ps[7][:, 16:32], ones, k.tok[:, TOK_G:TOK_G + 16], start=True, stop=True).then_inc(k.s_dec_mm, 1)
    e.wait_ge(k.s_idx_relu, 3 * HEADS)
    for h in range(HEADS):
        for c in range(TT):
            t_ = TOK_G + c * HEADS + h
            mm = e.matmul(k.ps[h][:, c * P:(c + 1) * P], k.tok[:, t_:t_ + 1].broadcast_to([P, P]), tri, start=True,
                          stop=True)
        mm.then_inc(k.s_decrow, 1)
    for h in range(HEADS):
        if h >= 1:
            e.wait_ge(k.s_qk_done, h)
        for c in range(TT):
            at = c * P
            mm = e.matmul(k.ps[4][:, at:at + P], til(k.qkv, 4 + h)[:, at:at + P], til(k.qkv, h)[:, at:at + P],
                          start=True, stop=True)
        mm.then_inc(k.s_qk_mm, 1)
        if h >= 1:
            e.wait_ge(k.s_at_done, h)
        for c in range(TT):
            at = c * P
            mm = e.matmul(k.ps[5][:, at:at + P], til(k.qkv, 4 + h)[:, at:at + P], til(k.qkv, 4 + h)[:, at:at + P],
                          start=True, stop=True)
        mm.then_inc(k.s_kk_mm, 1)
        if h >= 1:
            e.wait_ge(k.s_ek_done, h)
        for c in range(TT):
            mm = e.transpose(k.ps[6][:, c * P:(c + 1) * P], til(k.qkv, 4 + h)[:, c * P:(c + 1) * P], ident)
        mm.then_inc(k.s_kt_mm, 1)
        if h >= 1:
            e.wait_ge(k.s_v_tok_done, h)
        else:
            e.wait_ge(k.s_dec_copied, 1)
        for c in range(TT):
            mm = e.transpose(k.ps[7][:, c * P:(c + 1) * P], til(k.qkv, 8 + h)[:, c * P:(c + 1) * P], ident)
        mm.then_inc(k.s_vt_mm, 1)
    e.wait_ge(k.s_gam_done, 2 * HEADS)
    e.wait_ge(k.s_edecrow, HEADS)
    e.wait_ge(k.s_qk_done, HEADS)
    e.wait_ge(k.s_at_done, HEADS)
    for h in range(HEADS):
        e.wait_ge(k.s_x_init, h + 1)
        for c in range(TT):
            mm = e.transpose(k.ps[h][:, c * P:(c + 1) * P], k.g_xt[:, h * T + c * P:h * T + (c + 1) * P], ident)
        mm.then_inc(k.s_x_turned, 1)
    e.wait_ge(k.s_x_first, HEADS)

    def level(lev, last):
        for h in range(HEADS):
            u = lev * HEADS + h + 1
            e.wait_ge(k.s_bt_done, u)
            e.wait_ge(k.s_p_copied, u)
            e.wait_ge(k.s_x_done, u)
            b = (h % 2) * T
            for c in range(TT):
                at = c * P
                mm = e.matmul(k.ps[h % 2][:, at:at + P], k.g_b[:, b + at:b + at + P],
                              til(k.g_x, h)[:, at:at + P], start=True, stop=True)
            mm.then_inc(k.s_p_mm, 1)
            e.wait_ge(k.s_p_copied, u + 2)
            e.wait_ge(k.s_x_done, u + 2)
            for c in range(0 if last else TT):
                at = c * P
                e.matmul(k.ps[2 + h % 2][:, at:at + P], til(k.g_xt, h)[:, at:at + P],
                         k.g_p[:, b + at:b + at + P], start=True, stop=True)
            for c in range(TT):
                at = c * P
                mm = e.matmul(k.ps[4 + h % 2][:, at:at + P], k.g_p[:, b + at:b + at + P],
                              til(k.g_xt, h)[:, at:at + P], start=True, stop=True)
            mm.then_inc(k.s_xp_mm, 1)

    with e.Fori(0, LEVELS - 2) as lev:
        level(lev, False)
    level(LEVELS - 2, True)
    U = (LEVELS - 1) * HEADS
    e.wait_ge(k.s_x_done, HEADS + U)
    e.wait_ge(k.s_ek_done, HEADS)
    e.wait_ge(k.s_v_tok_done, HEADS)
    for h in range(HEADS):
        if h >= 2:
            e.wait_ge(k.s_wt_done, h - 1)
        for c in range(TT):
            at = h * T + c * P
            mm = e.matmul(k.ps[6 + h % 2][:, c * P:(c + 1) * P], k.g_ek[:, at:at + P], k.g_xt[:, at:at + P],
                          start=True, stop=True)
        mm.then_inc(k.s_wt_mm, 1)
    e.wait_ge(k.s_wt_done, HEADS)

    def logits(qt, h):
        cw, u = (qt + 1) * P, qt * HEADS + h
        if u >= 2:
            e.wait_ge(k.s_lg_masked, u - 1)
        r = slice(64 * (h % 2), 64 * (h % 2) + 64)
        e.matmul(k.ps[4 + h % 2][:, 0:cw], k.d_q[r, (h // 2) * T + qt * P:(h // 2) * T + (qt + 1) * P],
                 k.d_k[r, 0:cw], start=True, stop=True).then_inc(k.s_lg_mm, 1)

    turn_bank = (6, 1)

    def turn(qt, h):
        u = qt * HEADS + h
        e.wait_ge(k.s_p_norm, u + 1)
        if u >= 2:
            e.wait_ge(k.s_pt_copied, u - 1)
        for t in range(qt + 1):
            mm = e.transpose(k.ps[turn_bank[h % 2]][:, t * P:(t + 1) * P],
                             k.d_p[:, (h % 2) * T + t * P:(h % 2) * T + (t + 1) * P], ident)
        mm.then_inc(k.s_pt_mm, 1)

    def outputs(qt, h):
        e.wait_ge(k.s_pt_copied, qt * HEADS + h + 1)
        if qt and h == 0:
            e.wait_ge(k.s_y_lo, 2 + qt)
        for t in range(qt + 1):
            mm = e.matmul(k.ps[7][:, (h // 2) * P:(h // 2 + 1) * P],
                          k.d_v[:, (2 * t + h % 2) * P:(2 * t + h % 2 + 1) * P],
                          k.d_pt[:, (h % 2) * T + t * P:(h % 2) * T + (t + 1) * P],
                          start=h % 2 == 0 and t == 0, stop=h % 2 == 1 and t == qt)
        if h == HEADS - 1:
            mm.then_inc(k.s_o_mm, 1)

    def new_values(c):
        e.wait_ge(k.s_st_done, c + 1)
        for h in range(HEADS):
            at = h * T + c * P
            out = k.ps[0][:, h * P:(h + 1) * P]
            e.matmul(out, k.g_xt[:, at:at + P], k.g_v[:, at:at + P], start=True, stop=False)
            mm = e.matmul(out, til(k.qkv, 4 + h)[:, c * P:(c + 1) * P], k.g_s[:, h * P:(h + 1) * P],
                          start=False, stop=True)
        mm.then_inc(k.s_vn_mm, 1)

    def outputs_and_state(c):
        e.wait_ge(k.s_vn_done, c + 1)
        for h in range(HEADS):
            at = h * T + c * P
            mm = e.matmul(k.ps[3][:, h * P:(h + 1) * P], k.g_kdec[:, at:at + P], k.g_vn[:, h * P:(h + 1) * P],
                          start=True, stop=True)
        mm.then_inc(k.s_st_mm, 1)
        if c:
            e.wait_ge(k.s_o_copied, c)
        for h in range(HEADS):
            at = h * T + c * P
            out = k.ps[2][:, h * P:(h + 1) * P]
            vn = k.g_vn[:, h * P:(h + 1) * P]
            e.matmul(out, k.g_s[:, h * P:(h + 1) * P], til(k.qkv, h)[:, c * P:(c + 1) * P], start=True, stop=False)
            mm = e.matmul(out, vn, k.g_qk[:, at:at + P], start=False, stop=True)
        mm.then_inc(k.s_o_part, 1)

    logits(0, 0)
    logits(0, 1)
    for c in range(TT):
        new_values(c)
        if c:
            outputs(c - 1, 2)
            outputs(c - 1, 3)
        turn(c, 0)
        logits(c, 2)
        outputs_and_state(c)
        turn(c, 1)
        logits(c, 3)
        outputs(c, 0)
        turn(c, 2)
        if c + 1 < TT:
            logits(c + 1, 0)
        outputs(c, 1)
        turn(c, 3)
        if c + 1 < TT:
            logits(c + 1, 1)
    outputs(TT - 1, 2)
    outputs(TT - 1, 3)
    e.wait_ge(k.s_vn_done, TT)
    e.wait_ge(k.s_unit_sq, SQ_GO + TT)
    token_sums(0, [til(k.g_x, h) for h in range(HEADS)])
    e.wait_ge(k.s_unit_inv, GRP_GO)
    e.wait_ge(k.s_lg_masked, HEADS * TT)
    e.wait_ge(k.s_y_lo, 2 + TT)
    for h in range(HEADS):
        row(4 + h, TOK_RG + TT * h)

    e.wait_ge(k.s_y_lo, 2 + TT + HEADS)
    e.wait_ge(k.s_st_done, TT + 1)
    with e.Fori(0, 2) as i:
        pan.enter(i, 4)
        acc.enter(i, [2, 2, 0, 0, 0, 0, 0, 0])
        for j in range(4):
            panel(acc.take(e, j % 2)[:], k.y_hi, k.y_lo, range(KT))
        pan.leave(2)
        acc.leave(2)

    for j in range(4):
        panel(acc.take(e, j)[:], k.h_hi, k.h_lo, range(KT), ready=(k.s_fed_lo, 2 * KT))
        if j == 0:
            sum_squares(3 * KT, 2, k.sqacc)
    e.wait_ge(k.s_unit_sq, SQ_AQ + HEADS)
    token_sums(4, [til(k.a_p, h) for h in range(HEADS)])
    e.wait_ge(k.s_unit_inv, GRP_AQ)
    for h in range(HEADS):
        row(4 + h, TOK_RG + TT * h)
    e.wait_ge(k.s_xk_done, 1)

    def logits(h):
        e.wait_ge(k.s_aq_done, h + 1)
        for half in range(2):
            u = 2 * h + half
            if u >= 2:
                e.wait_ge(k.s_al_exp, u - 1)
            for n in range(2):
                qt = 2 * half + n
                mm = e.matmul(k.ps[half][:, n * MEM:(n + 1) * MEM], til(k.a_q, h)[:, qt * P:(qt + 1) * P],
                              k.xk[:, h * MEM:(h + 1) * MEM], start=True, stop=True)
            mm.then_inc(k.s_al_mm, 1)

    logits(0)
    for h in range(HEADS):
        if h + 1 < HEADS:
            logits(h + 1)
        e.wait_ge(k.s_al_norm, 2 * h + 2)
        if h:
            e.wait_ge(k.s_apt_copied, 2 * h)
        for mt in range(2):
            for qt in range(TT):
                at = (h % 2) * TT * MEM + qt * MEM + mt * P
                mm = e.transpose(k.ps[2 + mt][:, qt * P:(qt + 1) * P], k.a_p[:, at:at + P], ident)
            mm.then_inc(k.s_apt_mm, 1)
        if h >= 2:
            e.wait_ge(k.s_ao_lo_done, h - 1)
        else:
            e.wait_ge(k.s_aq_done, h + 1)
        for mt in range(2):
            e.wait_ge(k.s_apt_copied, 2 * h + mt + 1)
            mm = e.matmul(k.ps[4 + h % 2][:], k.xv[:, mt * T + h * P:mt * T + (h + 1) * P], til(k.a_pt, mt),
                          start=mt == 0, stop=mt == 1)
        mm.then_inc(k.s_av_mm, 1)
    e.wait_ge(k.s_aq_done, HEADS)
    e.wait_ge(k.s_ao_lo_done, HEADS)
    for j in range(4):
        for n in range(2):
            panel(acc.take(e, n)[:], k.ao_hi, k.ao_lo, range(HEADS), at=HEADS * n, done=n == 1)

    for j in range(4):
        panel(acc.take(e, j % 2)[:], k.h_hi, k.h_lo, range(KT), ready=(k.s_fed_lo, 3 * KT))
        if j == 0:
            sum_squares(4 * KT, 3, k.sqacc)
    for half in range(2):
        with e.Fori(0, MTH // 4 - (half == 0)) as i:
            pan.enter(i, 4)
            acc.enter(i, [2, 2, 0, 0, 0, 0, 0, 0])
            for j in range(4):
                panel(acc.take(e, j % 2)[:], k.h_hi, k.h_lo, range(KT))
            pan.leave(MTH // 4 - (half == 0))
            acc.leave(MTH // 4 - (half == 0))
        with e.Fori(0, KT // 2) as i:
            pan.enter(i, 4)
            acc.enter(i, [1, 1, 0, 0, 0, 0, 0, 0])
            for j in range(2):
                out = acc.take(e, j)[:]
                ready = (k.s_up_lo, MTH * half)
                panel(out, k.u_hi, k.u_lo, range(0, 8), last=False, ready=ready)
                panel(out, k.u_hi, k.u_lo, range(8, 16), first=False, ready=ready)
            pan.leave(KT // 2)
            acc.leave(KT // 2)

    sum_squares(5 * KT, 4, k.sqacc)
    e.wait_ge(k.s_fed_lo, 5 * KT)
    with e.Fori(0, KT) as i:
        pan.enter(i, 8)
        acc.enter(i, [2, 1, 1, 1, 1, 1, 1, 1])
        blocks = [(b, k.h_hi, k.h_lo, t, t == 0, t == KT - 1) for b in (0, 1, 4, 5) for t in range(KT)]
        blocks += [(b, k.ub_hi, k.ub_lo, 0, True, True) for b in (2, 3)]
        blocks += [(b, k.h_hi, k.h_lo, t, t == 0, t == KT - 1) for b in (6, 7, 0) for t in range(KT)]
        for a, b in zip(MIX_CUTS, MIX_CUTS[1:]):
            e.wait_ge(k.s_split_done, RAW + pan.at(1))
            slot = (pan.n % SPLIT) * PANEL
            for n, (bank, hi, lo, t, first, last) in enumerate(blocks[a:b]):
                if bank == 2:
                    e.wait_ge(k.s_s2_ulo, i + 1)
                out = acc.take(e, bank) if first else k.ps[bank]
                mm = products(out[:], slot + n * P, P, til(hi, t), til(lo, t), first, last)
            mm.then_inc(k.s_panel_used, 1)
            pan.step()
        pan.leave(KT)
        acc.leave(KT)

    with e.Fori(0, KT // 2) as i:
        pan.enter(i, 4)
        acc.enter(i, [1, 1, 1, 1, 0, 0, 0, 0])
        for j in range(2):
            panel(acc.take(e, 2 * j)[:], k.ya_hi, k.ya_lo, range(KT), ready=(k.s_s2_free, 0))
            panel(acc.take(e, 2 * j + 1)[:], k.yb_hi, k.yb_lo, range(KT), ready=(k.s_s2_free, 0))
        pan.leave(KT // 2)
        acc.leave(KT // 2)

    with e.Fori(0, 2) as i:
        pan.enter(i, 4)
        acc.enter(i, [2, 2, 0, 0, 0, 0, 0, 0])
        for j in range(4):
            panel(acc.take(e, j % 2)[:], k.mg_hi, k.mg_lo, range(KT), ready=(k.s_mg_lo, 0))
        pan.leave(2)
        acc.leave(2)

    for j in range(4):
        panel(acc.take(e, j)[:], k.h_hi, k.h_lo, range(KT), ready=(k.s_fed_lo, 5 * KT))
        if j == 0:
            sum_squares(6 * KT, 5, k.sqacc)
    with e.Fori(0, FFN // 2 - 1) as i:
        pan.enter(i, 4)
        acc.enter(i, [1, 1, 1, 1, 0, 0, 0, 0])
        for j in range(4):
            panel(acc.take(e, j)[:], k.h_hi, k.h_lo, range(KT))
        pan.leave(FFN // 2 - 1)
        acc.leave(FFN // 2 - 1)
    with e.Fori(0, KT // 2) as i:
        pan.enter(i, 8)
        acc.enter(i, [1, 1, 0, 0, 0, 0, 0, 0])
        for j in range(2):
            out = acc.take(e, j)[:]
            for a, b in zip(DOWN_CUTS, DOWN_CUTS[1:]):
                panel(out, k.f_hi, k.f_lo, range(a, b), first=a == 0, last=b == FFN,
                      ready=(k.s_f_lo_done, 0))
        pan.leave(KT // 2)
        acc.leave(KT // 2)
    sum_squares(7 * KT, 6, k.sqacc)


def scalar_program(nc, k, d):
    e = nc.scalar
    A = e.activation
    chain = Chain(e, k.s_act_chain)
    e.wait_ge(k.s_ld_mem[0], 16)
    e.dma_start(k.x[:].rearrange("p (k t) -> p k t", k=KT), d.x.rearrange("(k p) t -> p k t", p=P)).then_inc(k.s_ld_x, 16)
    e.dma_start(k.small_w[:], d.small_w).then_inc(k.s_ld_small, 16)
    fed = Count()

    def feed(src, gain, hi, w=T, split=True):
        e.wait_ge(k.s_sq_used, fed.at(1))
        if split:
            A(hi, src, ACT.Copy, scale=gain).then_inc(k.s_fed_hi, 1)
        A(k.sq[:, (fed.n % 2) * T:(fed.n % 2) * T + w], src, ACT.Square).then_inc(k.s_fed_sq, 1)
        fed.step()

    def root(n_norm, dst, w=T):
        e.wait_ge(k.s_ssq, n_norm)
        A(dst[:, 0:w], k.ps[7][:, 0:w], ACT.Sqrt, bias=k.eps[:, 0:1], scale=1.0 / D).then_inc(k.s_std, 1)

    e.wait_ge(k.s_ld_vec, 16)
    for m in range(KT):
        if m % (KT // 2) == 0:
            e.wait_ge(k.s_ld_mem[m // (KT // 2)], 16)
        feed(til(k.mem, m, w=MEM), col(k, "norm_mem", m), til(k.m_hi, m, w=MEM), MEM)
    e.wait_ge(k.s_zeroed, 1)
    root(1, k.m_rstd, MEM)
    e.wait_ge(k.s_ld_x, 16)
    for m in range(KT):
        feed(til(k.x, m), col(k, "norm_mix", m), til(k.h_hi, m))
    e.wait_ge(k.s_tokr_t, 1)
    for mt in range(2):
        ins = A(k.tok[:, TOK_RTOK + mt:TOK_RTOK + mt + 1], k.ps[4][:, mt * P:mt * P + 1], ACT.Copy)
    ins.then_inc(k.s_v_done, 1)
    e.wait_ge(k.s_xk_raw, 1)
    A(k.mem[:, 0:HEADS * MEM], k.xk[:], ACT.Square).then_inc(k.s_unit_sq, 1)
    root(2, k.rstd)
    e.wait_ge(k.s_unit_sum, 1)
    for j in range(2):
        ins = A(k.mem[:, HEADS * MEM + j * T:HEADS * MEM + (j + 1) * T], k.ps[5 + j][:], ACT.Sqrt,
                bias=k.eps[:, 0:1], scale=1.0 / P)
    ins.then_inc(k.s_unit_std, 1)

    e.wait_ge(k.s_proj_done, 1)
    A(k.c_t[:], til(k.proj, UG + 2, 2), ACT.Sigmoid).then_inc(k.s_c_sig, 1)
    for n in range(3):
        with e.Fori(0, HEADS) as m:
            e.wait_ge(k.s_g_conv, m + (HEADS * n + 1))
            A(rtil(k.qkv, m + HEADS * n), rtil(k.qkv, m + HEADS * n), ACT.Silu).then_inc(k.s_g_silu, 1)
            if n < 2:
                e.wait_ge(k.s_g_silu, m + (HEADS * n + 1))
                A(rtil(k.g_sq[n], m), rtil(k.qkv, m + HEADS * n), ACT.Square).then_inc(k.s_unit_sq, 1)
    e.wait_ge(k.s_proj_done, 2)
    for h in range(HEADS):
        A(til(k.proj, Z + h), til(k.proj, Z + h), ACT.Silu).then_inc(k.s_z_silu, 1)

    for half in range(2):
        e.dma_start(k.d_ki[64 * half:64 * half + 64, :],
                    k.proj[0:64, REST * T:(REST + 1) * T]).then_inc(k.s_ki_dup, 16)
    for n, bank, dst in ((1, 4, k.d_k[:]), (3, 0, til(k.d_q, 0)), (4, 1, til(k.d_q, 1)), (5, 2, til(k.d_qi, 0)),
                         (6, 3, til(k.d_qi, 1))):
        e.wait_ge(k.s_dq_mm, n)
        A(dst, k.ps[bank][:], ACT.Copy).then_inc(k.s_dq_raw, 1)
    for n, (src, dst) in enumerate(((til(k.d_q, 0), til(k.d_relu, 0)), (til(k.d_q, 1), til(k.d_relu, 1)),
                                    (k.d_k[:], k.d_rk[:]))):
        e.wait_ge(k.s_dq_raw, (2, 3, 1)[n])
        A(dst, src, ACT.Square).then_inc(k.s_unit_sq, 1)
    e.wait_ge(k.s_d_gates, 1)
    A(k.tok[:, TOK_A:TOK_A + 48].rearrange("p (c w) -> p c w", c=TT),
      k.ps[6][:].rearrange("p (c w) -> p c w", c=TT)[:, :, 64:76], ACT.Copy).then_inc(k.s_d_gates_tok, 1)
    def unit_root(group, bank, at, n, scale):
        e.wait_ge(k.s_unit_sum, group + 1)
        A(k.tok[:, at:at + n], k.ps[bank][:, 0:n], ACT.Sqrt, bias=k.eps[:, 0:1], scale=scale).then_inc(k.s_unit_std, 1)

    unit_root(GRP_G, 7, TOK_RG, 2 * HEADS * TT, 1.0)
    for j in range(2):
        e.wait_ge(k.s_c_cent, j + 1)
        A(til(k.c_t, j), til(k.c_acc, j), ACT.Square).then_inc(k.s_c_sq, 1)
    unit_root(GRP_DQ, 5, TOK_RDQ, 6 * TT, 1.0 / 64)
    unit_root(GRP_C, 6, TOK_RC, TT, 1.0 / 256)
    e.wait_ge(k.s_sp_in, 1)
    A(k.tok[:, TOK_SP + 24:TOK_SP + 48], k.tok[:, TOK_SP + 24:TOK_SP + 48], ACT.Exp, scale=-1.0)
    A(k.tok[:, TOK_EA:TOK_EA + 16], k.vec[:, VEC["a_log"][0]:VEC["a_log"][0] + 16],
      ACT.Exp).then_inc(k.s_sp_exp, 1)
    for j in range(2):
        e.wait_ge(k.s_c_norm, j + 1)
        A(til(k.c_t, j), til(k.c_acc, j), ACT.Silu, bias=col(k, "cln_b", j)).then_inc(k.s_c_silu, 1)
    for j in range(2):
        e.wait_ge(k.s_c_silu, j + 1)
        A(til(k.y_hi, 6 + j), til(k.c_t, j), ACT.Copy).then_inc(k.s_y_hi, 1)

    A(k.tok[:, TOK_BETA:TOK_BETA + 16].rearrange("p (c h) -> p c h", c=TT),
      k.tok[:, TOK_A:TOK_A + 48].rearrange("p (c w) -> p c w", c=TT)[:, :, 4:8], ACT.Sigmoid).then_inc(k.s_beta_done, 1)

    for qt in range(1, TT):
        cw = (qt + 1) * P
        for h in range(HEADS):
            v = HEADS * (qt - 1) + h
            e.wait_ge(k.s_idx_mm, v + 1)
            if v >= 2:
                e.wait_ge(k.s_idx_used, v - 1)
            else:
                e.wait_ge(k.s_unit_sum, GRP_DQ + 1)
            A(k.d_relu[:, (h % 2) * T:(h % 2) * T + cw], k.ps[h][:, 0:cw], ACT.Relu).then_inc(k.s_idx_relu, 1)

    e.wait_ge(k.s_dec_copied, 1)
    A(k.tok[:, TOK_EDEC:TOK_EDEC + 16], k.tok[:, TOK_DEC:TOK_DEC + 16], ACT.Exp)
    A(k.tok[:, TOK_EKD:TOK_EKD + 16], k.tok[:, TOK_EKD:TOK_EKD + 16], ACT.Exp)
    A(k.tok[:, TOK_ELAST:TOK_ELAST + 16], k.tok[:, TOK_LAST:TOK_LAST + 16], ACT.Exp).then_inc(k.s_dec_exp, 1)
    for h in range(HEADS):
        e.wait_ge(k.s_gam_d, h + 1)
        A(til(k.g_xt, h), k.ps[h][:], ACT.Exp).then_inc(k.s_edecrow, 1)
        A(til(k.g_at, h), til(k.g_at, h), ACT.Exp).then_inc(k.s_gam_e, 1)
    e.wait_ge(k.s_dec_exp, 1)
    e.wait_ge(k.s_idx_used, 3 * HEADS)
    for h in range(HEADS):
        e.wait_ge(k.s_kt_mm, h + 1)
        for c in range(TT):
            t = TOK_EDEC + c * HEADS + h
            A(k.g_ek[:, h * T + c * P:h * T + (c + 1) * P], k.ps[6][:, c * P:(c + 1) * P], ACT.Copy,
              scale=k.tok[:, t:t + 1])
        for c in range(TT):
            t = TOK_EKD + c * HEADS + h
            ins = A(k.g_kdec[:, h * T + c * P:h * T + (c + 1) * P], k.ps[6][:, c * P:(c + 1) * P], ACT.Copy,
                    scale=k.tok[:, t:t + 1])
        ins.then_inc(k.s_ek_done, 1)
        e.wait_ge(k.s_vt_mm, h + 1)
        A(til(k.g_v, h), k.ps[7][:], ACT.Copy).then_inc(k.s_v_tok_done, 1)
    e.sem_inc(k.s_p_copied, 2)
    for h in range(HEADS):
        e.wait_ge(k.s_x_turned, h + 1)
        A(til(k.g_x, h), k.ps[h][:], ACT.Copy).then_inc(k.s_x_first, 1)
    with e.Fori(0, LEVELS - 1) as lev:
        for h in range(HEADS):
            e.wait_ge(k.s_p_mm, lev * HEADS + h + 1)
            e.wait_ge(k.s_x_done, lev * HEADS + h + 3)
            A(til(k.g_p, h % 2), k.ps[h % 2][:], ACT.Copy).then_inc(k.s_p_copied, 1)
    for h in range(HEADS):
        e.wait_ge(k.s_wt_mm, h + 1)
        A(til(k.qkv, 4 + h), k.ps[6 + h % 2][:], ACT.Copy, scale=-1.0).then_inc(k.s_wt_done, 1)

    def exps(qt, h):
        u, cw = qt * HEADS + h, (qt + 1) * P
        p = k.d_p[:, (h % 2) * T:(h % 2) * T + cw]
        e.wait_ge(k.s_lg_masked, u + 1)
        A(p, p, ACT.Exp, bias=k.tok[:, TOK_NM + h % 2:TOK_NM + h % 2 + 1],
          accum_out=k.tok[:, TOK_SUM + h % 2:TOK_SUM + h % 2 + 1]).then_inc(k.s_p_exp, 1)

    def turned(qt, h):
        u, cw = qt * HEADS + h, (qt + 1) * P
        e.wait_ge(k.s_pt_mm, u + 1)
        A(k.d_pt[:, (h % 2) * T:(h % 2) * T + cw], k.ps[(6, 1)[h % 2]][:, 0:cw], ACT.Copy).then_inc(k.s_pt_copied, 1)

    def attended(c):
        e.wait_ge(k.s_o_mm, c + 1)
        A(k.y_hi[:, 4 * T:6 * T].rearrange("p (j t) -> p j t", j=2)[:, :, c * P:(c + 1) * P],
          k.ps[7][:, 0:2 * P].rearrange("p (j t) -> p j t", j=2), ACT.Copy).then_inc(k.s_y_hi, 1)

    exps(0, 0)
    exps(0, 1)
    for c in range(TT):
        if c:
            attended(c - 1)
        turned(c, 0)
        exps(c, 2)
        part = lambda buf, t: buf[:, t * T:(t + 4) * T].rearrange("p (h t) -> p h t", h=HEADS)[:, :, c * P:(c + 1) * P]
        e.wait_ge(k.s_o_part, c + 1)
        A(part(k.qkv, 8), k.ps[2][:].rearrange("p (h t) -> p h t", h=HEADS), ACT.Copy).then_inc(k.s_o_copied, 1)
        turned(c, 1)
        exps(c, 3)
        e.wait_ge(k.s_o_copied, c + 1)
        A(part(k.g_x, 0), part(k.qkv, 8), ACT.Square).then_inc(k.s_unit_sq, 1)
        turned(c, 2)
        if c + 1 < TT:
            exps(c + 1, 0)
        turned(c, 3)
        if c + 1 < TT:
            exps(c + 1, 1)
    attended(TT - 1)
    unit_root(GRP_GO, 0, TOK_RG, HEADS * TT, 1.0 / P)
    for h in range(HEADS):
        e.wait_ge(k.s_go_norm, h + 1)
        A(til(k.y_hi, h), til(k.qkv, 8 + h), ACT.Copy).then_inc(k.s_y_hi, 1)

    def residual_feeds(gain, times=KT, split=True, per=4):
        with e.Fori(0, times // per) as i:
            fed.enter(i, per)
            for j in range(per):
                e.wait_ge(k.s_x_new, fed.at(1) - 2 * KT)
                g = k.vec[:, bass.ds(i * per + (VEC[gain][0] + j), 1)]
                feed(rtil(k.x, i * per + j), g, rtil(k.h_hi, i * per + j), split=split)
            fed.leave(times // per)

    residual_feeds("norm_cross")

    root(3, k.rstd)
    for h in range(HEADS):
        e.wait_ge(k.s_aq_raw, h + 1)
        A(til(k.a_p, h), til(k.a_q, h), ACT.Square).then_inc(k.s_unit_sq, 1)
    unit_root(GRP_AQ, 4, TOK_RG, HEADS * TT, 1.0 / P)

    def exps(h):
        for half in range(2):
            u = 2 * h + half
            e.wait_ge(k.s_al_max, u + 1)
            if h >= 2:
                e.wait_ge(k.s_apt_mm, 2 * (h - 1))
            for n in range(2):
                c = 2 * half + n
                t_ = TT * (h % 2) + c
                at = (h % 2) * TT * MEM + c * MEM
                ins = A(k.a_p[:, at:at + MEM], k.ps[half][:, n * MEM:(n + 1) * MEM], ACT.Exp,
                        scale=XA_SCALE, bias=k.tok[:, TOK_NM + t_:TOK_NM + t_ + 1],
                        accum_out=k.tok[:, TOK_SUM + t_:TOK_SUM + t_ + 1])
            ins.then_inc(k.s_al_exp, 1)

    exps(0)
    for h in range(HEADS):
        for mt in range(2):
            e.wait_ge(k.s_apt_mm, 2 * h + mt + 1)
            if h:
                e.wait_ge(k.s_av_mm, h)
            A(til(k.a_pt, mt), k.ps[2 + mt][:], ACT.Copy).then_inc(k.s_apt_copied, 1)
        if h + 1 < HEADS:
            exps(h + 1)
        e.wait_ge(k.s_av_mm, h + 1)
        A(til(k.ao_hi, h), k.ps[4 + h % 2][:], ACT.Copy).then_inc(k.s_ao_hi_done, 1)
    residual_feeds("norm_mlp")

    root(4, k.rstd)
    for half in range(2):
        with e.Fori(0, MTH // 4) as i:
            for j in range(4):
                m = i * 4 + j
                e.wait_ge(k.s_up_relu, m + (half * MTH + 1))
                A(k.u_t[:, (2 + j % 2) * T:(3 + j % 2) * T], k.u_t[:, (j % 2) * T:(j % 2 + 1) * T],
                  ACT.Square).then_inc(k.s_up_sq, 1)
                e.wait_ge(k.s_up_sq, m + (half * MTH + 1))
                A(rtil(k.u_hi, m), k.u_t[:, (2 + j % 2) * T:(3 + j % 2) * T], ACT.Copy).then_inc(k.s_up_hi, 1)
    residual_feeds("ln1")

    root(5, k.rstd)
    st = lambda n: til(k.s_t, n)
    with e.Fori(0, KT) as i:
        e.wait_ge(k.s_s2_u, i + 1)
        A(k.ub_hi[:], st(0), ACT.Copy).then_inc(k.s_s2_uhi, 1)
        e.wait_ge(k.s_s2_gl, i + 1)
        A(st(2), st(1), ACT.Square).then_inc(k.s_s2_gsq, 1)
        e.wait_ge(k.s_s2_gt, i + 1)
        A(st(2), st(2), ACT.Sigmoid, scale=GELU_SCALE).then_inc(k.s_s2_gsig, 1)
        for n in range(2):
            e.wait_ge(k.s_s2_gate, i * 2 + n + 1)
            g = rtil(k.gates, i + n * KT)
            A(g, g, ACT.Sigmoid, bias=k.vec[:, bass.ds(i + (VEC["gate_b"][0] + n * KT), 1)]).then_inc(k.s_s2_gate_done, 1)
        e.wait_ge(k.s_panel_used, i * 8 + (SPLIT + PAN_S6 + MIX_GATES + 1))
        A(st(3), k.ps[2][:], ACT.Sigmoid, bias=k.vec[:, bass.ds(i + VEC["lru_ba"][0], 1)]).then_inc(k.s_s2_r, 1)
        A(st(4), k.ps[3][:], ACT.Sigmoid, bias=k.vec[:, bass.ds(i + VEC["lru_bx"][0], 1)]).then_inc(k.s_s2_i, 1)
        e.wait_ge(k.s_s2_r, i + 1)
        A(st(6), st(3), ACT.Tanh, scale=k.tok[:, bass.ds(i + TOK_P8, 1)]).then_inc(k.s_s2_th, 1)
        A(st(5), st(3), ACT.Exp, scale=k.tok[:, bass.ds(i + TOK_N8, 1)]).then_inc(k.s_s2_a, 1)
        e.wait_ge(k.s_s2_a, i + 1)
        A(st(7), st(5), ACT.Square).then_inc(k.s_s2_a2, 1)
        e.wait_ge(k.s_s2_m, i + 1)
        A(st(7), st(7), ACT.Sqrt, bias=k.eps[:, 1:2]).then_inc(k.s_s2_s, 1)
        e.wait_ge(k.s_s2_yb, i + 1)
        A(rtil(k.yb_hi, i), st(8), ACT.Copy).then_inc(k.s_s2_yb_hi, 1)
        e.wait_ge(k.s_s2_ya, i + 1)
        A(rtil(k.ya_hi, i), st(3), ACT.Copy).then_inc(k.s_s2_ya_hi, 1)
    with e.Fori(0, KT // 2) as i:
        for j in range(2):
            e.wait_ge(k.s_mg, i * 2 + j + 1)
            A(rtil(k.mg_hi, i * 2 + j), st(2 * j), ACT.Copy).then_inc(k.s_mg_hi, 1)
    residual_feeds("ln2")

    root(6, k.rstd)
    with e.Fori(0, FFN // 2) as i:
        for j in range(2):
            e.wait_ge(k.s_f_g, i * 2 + j + 1)
            A(til(k.f_t, j), til(k.f_t, j), ACT.Silu).then_inc(k.s_f_silu, 1)
            e.wait_ge(k.s_f_hid, i * 2 + j + 1)
            A(rtil(k.f_hi, i * 2 + j), til(k.f_t, j), ACT.Copy).then_inc(k.s_f_hi_done, 1)
    residual_feeds("final", split=False)
    root(7, k.rstd)


GELU_SCALE = 2.0 * 0.7978845608028654
XA_SCALE = 128 ** -0.5
PAN_S6 = 112
PAN_S7 = PAN_S6 + 64
PAN_S8 = PAN_S7 + 16
PAN_S9 = PAN_S8 + 8
PAN_DOWN = PAN_S9 + 44


def vector_program(nc, k):
    e = nc.vector
    chain = Chain(e, k.s_dve_chain)
    fed = Count()
    TS, TTn, STT = e.tensor_scalar, e.tensor_tensor, e.scalar_tensor_tensor
    for b in range(8):
        e.sem_inc(k.acc_free[b], 1)
    e.memset(k.eps[:, 0:1], EPS)
    e.memset(k.eps[:, 1:2], 1e-30)
    e.memset(k.eps[:, 2:3], 1.0)
    e.memset(k.m_sqa[:], 0.0)
    e.sem_inc(k.s_sq_used, 2)
    chain(e.memset(k.sqacc[:], 0.0))
    e.sem_inc(k.s_zeroed, 1)

    def feed(src, gain, hi, lo, w=T, split=True, sqacc=None):
        acc = (sqacc or k.sqacc)[:, 0:w]
        if split:
            e.wait_ge(k.s_fed_hi, fed.at(1))
            STT(out=lo, in0=src, scalar=gain, in1=hi.bitcast(F32), op0=ALU.mult,
                op1=ALU.subtract).then_inc(k.s_fed_lo, 1)
        e.wait_ge(k.s_fed_sq, fed.at(1))
        TTn(acc, acc, k.sq[:, (fed.n % 2) * T:(fed.n % 2) * T + w], ALU.add).then_inc(k.s_sq_used, 1)
        fed.step()
        e.wait_ge(k.s_sq_used, 2 + fed.at())

    def invert(n_norm, dst, w=T):
        e.wait_ge(k.s_std, n_norm)
        e.reciprocal(dst[:, 0:w], dst[:, 0:w]).then_inc(k.s_rstd, 1)
        e.wait_ge(k.s_rstd, n_norm)

    freed = [1 + 2 + 6, 1 + 2 + 6, 1 + 1 + 6, 1 + 1 + 6, 1, 1, 1, 1]

    e.wait_ge(k.s_ld_vec, 16)
    for m in range(KT):
        if m % (KT // 2) == 0:
            e.wait_ge(k.s_ld_mem[m // (KT // 2)], 16)
        feed(til(k.mem, m, w=MEM), col(k, "norm_mem", m), til(k.m_hi, m, w=MEM), til(k.m_lo, m, w=MEM), MEM,
             sqacc=k.m_sqa)
    invert(1, k.m_rstd, MEM)
    for m in range(HEADS):
        e.wait_ge(k.s_panel_used, SPLIT + m + 1)
        ins = TTn(til(k.xk, m, w=MEM), k.ps[m % 2][:, 0:MEM], k.m_rstd[:], ALU.mult)
        ins.then_inc(k.acc_free[m % 2], 1)
    e.wait_ge(k.acc_free[0], 3)
    e.wait_ge(k.acc_free[1], 3)
    e.sem_inc(k.s_xk_raw, 1)
    e.wait_ge(k.s_ld_x, 16)
    for m in range(KT):
        feed(til(k.x, m), col(k, "norm_mix", m), til(k.h_hi, m), til(k.h_lo, m))
    e.wait_ge(k.s_panel_used, SPLIT + 8)
    e.wait_ge(k.s_v_done, 1)
    for mt in range(2):
        TS(til(k.xv, mt), k.ps[2 + mt][:], k.tok[:, TOK_RTOK + mt:TOK_RTOK + mt + 1], None,
           ALU.mult).then_inc(k.acc_free[2 + mt], 1)
        e.wait_ge(k.acc_free[2 + mt], 2)
    e.sem_inc(k.s_v_done, 1)
    invert(2, k.rstd)
    e.wait_ge(k.s_unit_std, 1)
    xk_r = k.mem[:, HEADS * MEM:2 * HEADS * MEM]
    chain(e.reciprocal(xk_r, xk_r))
    STT(out=k.xk[:], in0=k.xk[:], scalar=col(k, "xa_k"), in1=xk_r, op0=ALU.mult, op1=ALU.mult).then_inc(k.s_xk_done, 1)

    with e.Fori(0, 2) as i:
        for j in range(4):
            e.wait_ge(k.s_panel_used, i * 4 + (SPLIT + 8 + j + 1))
            TTn(rtil(k.proj, i * 4 + j), k.ps[j][:], k.rstd[:], ALU.mult).then_inc(k.acc_free[j], 1)
    for j in range(4):
        e.wait_ge(k.acc_free[j], freed[j] - 4)
    e.sem_inc(k.s_proj_done, 1)
    cy = [k.c_y[:, j * (PAD + T):(j + 1) * (PAD + T)] for j in range(2)]
    e.wait_ge(k.s_c_sig, 1)
    for j in range(2):
        e.memset(cy[j][:, 0:PAD], 0.0)
        ins = TTn(cy[j][:, PAD:PAD + T], til(k.proj, UG + j), til(k.c_t, j), ALU.mult)
    chain(ins)
    for j in range(2):
        ins = TS(til(k.c_acc, j), cy[j][:, PAD:PAD + T], col(k, "dw", j * CONV_TAPS + CONV_TAPS - 1),
                 col(k, "dw_b", j), ALU.mult, ALU.add)
    chain(ins)

    def link(ins):
        ins.then_inc(k.s_dve_chain, 1)
        return chain.c.step()

    def mixer_taps(n, last, before):
        for j in range(2):
            e.wait_ge(k.s_dve_chain, before[j])
            w = k.vec[:, bass.ds(n + (VEC["dw"][0] + j * CONV_TAPS), 1)]
            acc = til(k.c_acc, j)
            ins = STT(out=acc, in0=cy[j][:, bass.ds(n + PAD - CONV_TAPS + 1, T)], scalar=w, in1=acc, op0=ALU.mult,
                      op1=ALU.add)
            if last:
                ins.then_inc(k.s_c_conv, 1)
            else:
                before[j] = link(ins)

    with e.Fori(0, 3) as i:
        chain.c.enter(i, 4 * 7)
        before = [chain.c.at(), chain.c.at()]
        for j in range(4):
            e.wait_ge(k.s_panel_used, i * 4 + (SPLIT + 16 + j + 1))
            TTn(rtil(k.proj, i * 4 + (QKV + j)), k.ps[j][:], k.rstd[:], ALU.mult).then_inc(k.acc_free[j], 1)
            mixer_taps(i * 8 + 2 * j, False, before)
            e.wait_ge(k.acc_free[j], i + (freed[j] - 3))
            dst = rtil(k.qkv, i * 4 + j)
            for s in range(4):
                w = k.vec[:, bass.ds(i * 16 + (VEC["gdn_conv"][0] + j * 4 + 3 - s), 1)]
                if s == 0:
                    tap = link(TS(dst, rtil(k.proj, i * 4 + (QKV + j)), w, None, ALU.mult))
                    mixer_taps(i * 8 + (2 * j + 1), False, before)
                else:
                    e.wait_ge(k.s_dve_chain, tap)
                    ins = STT(out=k.qkv[:, bass.ds(i * (4 * T) + (j * T + s), T - s)],
                              in0=k.proj[:, bass.ds(i * (4 * T) + (QKV + j) * T, T - s)], scalar=w,
                              in1=k.qkv[:, bass.ds(i * (4 * T) + (j * T + s), T - s)], op0=ALU.mult, op1=ALU.add)
                    if s == 3:
                        ins.then_inc(k.s_g_conv, 1)
                    else:
                        tap = link(ins)
        chain.c.leave(3)
    before = [chain.c.at(), chain.c.at()]
    for j in range(4):
        e.wait_ge(k.s_panel_used, SPLIT + 28 + j + 1)
        TTn(til(k.proj, Z + j), k.ps[j][:], k.rstd[:], ALU.mult).then_inc(k.acc_free[j], 1)
        if j < 3:
            mixer_taps(24 + 2 * j, False, before)
            mixer_taps(25 + 2 * j, j == 2, before)
    for j in range(4):
        e.wait_ge(k.acc_free[j], freed[j])
    e.sem_inc(k.s_proj_done, 1)

    e.wait_ge(k.s_dq_mm, 6)
    chain(e.memset(k.d_v[:], 0.0))
    for par in range(2):
        dst = k.d_v[:].rearrange("p (t q w) -> p t q w", t=TT, q=2)[:, :, par, 64 * par:64 * par + 64]
        ins = e.tensor_copy(dst, k.ps[5][:, 0:256].rearrange("p (t w) -> p t w", t=TT))
    ins.then_inc(k.s_dv_done, 1)
    e.wait_ge(k.s_d_gates_tok, 1)
    TS(k.tok[:, TOK_W:TOK_W + 16].rearrange("p (c h) -> p c h", c=TT),
       k.tok[:, TOK_A:TOK_A + 48].rearrange("p (c w) -> p c w", c=TT)[:, :, 8:12], 1.0 / 16, None, ALU.mult)
    tok = lambda at, n: k.tok[:, at:at + n]
    v, z, t, w2, s_ = (tok(TOK_SP + 24 * n, 24) for n in range(5))
    TTn(tok(TOK_SP, 16).rearrange("p (c h) -> p c h", c=TT),
        k.tok[:, TOK_A:TOK_A + 48].rearrange("p (c w) -> p c w", c=TT)[:, :, 0:4],
        k.vec[:, VEC["dt_bias"][0]:VEC["dt_bias"][0] + 16].rearrange("p (c h) -> p c h", c=TT), ALU.add)
    chain(TS(tok(TOK_SP + 16, 8), k.vec[:, VEC["lam"][0]:VEC["lam"][0] + 8], -1.0, None, ALU.mult))
    STT(out=z, in0=v, scalar=-1.0, in1=v, op0=ALU.mult, op1=ALU.max).then_inc(k.s_sp_in, 1)

    for j in range(2):
        e.wait_ge(k.s_c_mean, 1)
        e.wait_ge(k.s_c_conv, 2)
        acc = til(k.c_acc, j)
        STT(out=acc, in0=k.ps[6][:], scalar=-1.0 / 256, in1=acc, op0=ALU.mult, op1=ALU.add).then_inc(k.s_c_cent, 1)

    def unit_inverse(group, at, n):
        e.wait_ge(k.s_unit_std, group + 1)
        e.reciprocal(k.tok[:, at:at + n], k.tok[:, at:at + n]).then_inc(k.s_unit_inv, 1)

    unit_inverse(GRP_G, TOK_RG, 2 * HEADS * TT)
    unit_inverse(GRP_DQ, TOK_RDQ, 6 * TT)
    unit_inverse(GRP_C, TOK_RC, TT)
    for n, (raw, bank, gain) in enumerate(((til(k.d_q, 0), 0, "dsa_q"), (til(k.d_q, 1), 1, "dsa_q"),
                                           (k.d_k[:], 4, "dsa_k"))):
        e.wait_ge(k.s_unit_row, ROW_DQ + n + 1)
        STT(out=raw, in0=raw, scalar=col(k, gain), in1=k.ps[bank][:], op0=ALU.mult,
            op1=ALU.mult).then_inc(k.s_dq_done, 1)
    e.wait_ge(k.s_unit_row, ROW_C + 1)
    for j in range(2):
        e.wait_ge(k.s_c_cent, 2)
        e.wait_ge(k.s_c_sq, 2)
        acc = til(k.c_acc, j)
        STT(out=acc, in0=acc, scalar=col(k, "cln_g", j), in1=k.ps[6][:], op0=ALU.mult,
            op1=ALU.mult).then_inc(k.s_c_norm, 1)

    e.wait_ge(k.s_sp_exp, 1)
    chain(TS(t, z, 2.0, None, ALU.add))
    chain(e.reciprocal(t, t))
    chain(TTn(z, z, t, ALU.mult))
    chain(TTn(w2, z, z, ALU.mult))
    chain(TS(s_, w2, 1.0 / 15, 1.0 / 13, ALU.mult, ALU.add))
    for n in (11, 9, 7, 5, 3, 1):
        chain(TTn(s_, s_, w2, ALU.mult))
        chain(TS(s_, s_, 1.0 / n, None, ALU.add))
    chain(TTn(s_, s_, z, ALU.mult))
    chain(TS(v, v, 0.0, None, ALU.max))
    chain(STT(out=s_, in0=s_, scalar=2.0, in1=v, op0=ALU.mult, op1=ALU.add))
    TS(tok(TOK_N8, 8), s_[:, 16:24], -8.0, None, ALU.mult)
    TS(tok(TOK_P8, 8), s_[:, 16:24], 8.0, None, ALU.mult)
    STT(out=tok(TOK_G, 16), in0=s_[:, 0:16], scalar=-1.0, in1=tok(TOK_EA, 16), op0=ALU.mult,
        op1=ALU.mult).then_inc(k.s_g_ready, 1)
    for j in range(2):
        e.wait_ge(k.s_y_hi, j + 1)
        TTn(til(k.y_lo, 6 + j), til(k.c_t, j), til(k.y_hi, 6 + j).bitcast(F32), ALU.subtract).then_inc(k.s_y_lo, 1)
    e.wait_ge(k.s_g_conv, 12)
    for m in range(2 * HEADS):
        e.wait_ge(k.s_unit_row, ROW_G + m + 1)
        q = til(k.qkv, m)
        STT(out=q, in0=q, scalar=P ** -0.5 if m < HEADS else 1.0, in1=k.ps[4 + m % 4][:], op0=ALU.mult,
            op1=ALU.mult).then_inc(k.s_g_qk_done, 1)
    e.wait_ge(k.s_dq_done, 3)
    scores = [None, k.d_score_a[:, 0:2 * P], k.d_score_a[:, 2 * P:5 * P], k.d_score_b[:]]
    for qt in range(1, TT):
        cw, score = (qt + 1) * P, scores[qt]
        for h in range(HEADS):
            v_ = HEADS * (qt - 1) + h
            w = TOK_W + qt * HEADS + h
            e.wait_ge(k.s_idx_relu, v_ + 1)
            STT(out=score, in0=k.d_relu[:, (h % 2) * T:(h % 2) * T + cw], scalar=k.tok[:, w:w + 1],
                in1=k.const[:, C_CAUS + T - cw:C_CAUS + T] if h == 0 else score, op0=ALU.mult,
                op1=ALU.add).then_inc(k.s_idx_used, 1)
            e.wait_ge(k.s_idx_used, v_ + 1)
    e.wait_ge(k.s_dec_mm, 1)
    chain(e.tensor_copy(tok(TOK_DEC, 32), k.ps[7][:, 0:32]))
    TTn(tok(TOK_EKD, 16), tok(TOK_LAST, 16), tok(TOK_DEC, 16), ALU.subtract).then_inc(k.s_dec_copied, 1)
    tri4 = k.const[:, C_TRI:C_TRI + P].unsqueeze(1).broadcast_to([P, TT, P])
    for h in range(HEADS):
        e.wait_ge(k.s_decrow, h + 1)
        for c in range(TT):
            t_ = TOK_DEC + c * HEADS + h
            ins = TS(k.g_at[:, h * T + c * P:h * T + (c + 1) * P], k.ps[h][:, c * P:(c + 1) * P], k.tok[:, t_:t_ + 1],
                     0.0, ALU.subtract, ALU.min)
        ins.then_inc(k.s_gam_d, 1)
    for h in range(HEADS):
        e.wait_ge(k.s_gam_e, h + 1)
        g3 = til(k.g_at, h).rearrange("p (c i) -> p c i", c=TT)
        TTn(g3, g3, tri4, ALU.mult).then_inc(k.s_gam_done, 1)
    e.wait_ge(k.s_gam_done, HEADS)
    e.wait_ge(k.s_beta_done, 1)
    for h in range(HEADS):
        e.wait_ge(k.s_qk_mm, h + 1)
        TTn(til(k.g_qk, h), k.ps[4][:], til(k.g_at, h), ALU.mult).then_inc(k.s_qk_done, 1)
        e.wait_ge(k.s_qk_done, h + 1)
        e.wait_ge(k.s_kk_mm, h + 1)
        for c in range(TT):
            t_ = TOK_BETA + c * HEADS + h
            a = k.g_at[:, h * T + c * P:h * T + (c + 1) * P]
            ins = STT(out=a, in0=k.ps[5][:, c * P:(c + 1) * P], scalar=k.tok[:, t_:t_ + 1], in1=a, op0=ALU.mult,
                      op1=ALU.mult)
        ins.then_inc(k.s_at_done, 1)
    e.wait_ge(k.s_at_done, HEADS)
    for h in range(HEADS):
        e.wait_ge(k.s_edecrow, h + 1)
        e.wait_ge(k.s_kk_mm, HEADS)
        q = til(k.qkv, h)
        TTn(q, q, til(k.g_xt, h), ALU.mult).then_inc(k.s_gam_done, 1)
    e.wait_ge(k.s_gam_done, 2 * HEADS)
    spread = lambda at: k.const[:, at:at + P].unsqueeze(1).broadcast_to([P, TT, P])
    chunks = lambda buf, h: til(buf, h).rearrange("p (c i) -> p c i", c=TT)
    for h in range(HEADS):
        chain(TTn(chunks(k.g_xt, h), chunks(k.g_at, h), spread(C_LEV), ALU.mult))
        TTn(chunks(k.g_xt, h), spread(C_ID), chunks(k.g_xt, h), ALU.subtract).then_inc(k.s_x_init, 1)
    chain(e.memset(k.g_s[:], 0.0))
    e.sem_inc(k.s_x_done, HEADS)
    e.sem_inc(k.s_st_done, 1)

    def level(lev, base, top_rounds, last=False):
        for h in range(HEADS):
            if top_rounds:
                e.wait_ge(k.s_dve_chain, replaced[0])
            e.wait_ge(k.s_xp_mm, lev * HEADS + ((base - 1) * HEADS + h + 1))
            if not last:
                TTn(til(k.g_x, h), til(k.g_x, h), k.ps[2 + h % 2][:], ALU.subtract)
            if top_rounds:
                for qt in range(1, TT):
                    found = link(e.max(tok(TOK_M8 + 8 * qt - 8, 8), scores[qt]))
                e.wait_ge(k.s_dve_chain, found)
            TTn(til(k.g_xt, h), til(k.g_xt, h), k.ps[4 + h % 2][:], ALU.subtract).then_inc(k.s_x_done, 1)
            if top_rounds:
                for qt in range(1, TT):
                    replaced[0] = link(e.match_replace(scores[qt], tok(TOK_M8 + 8 * qt - 8, 8), scores[qt], TAKEN))

    top_levels = TOPK // 8 // HEADS
    with e.Fori(0, top_levels) as lev:
        chain.c.enter(lev, 6 * HEADS)
        replaced = [chain.c.at()]
        level(lev, 1, True)
        chain.c.leave(top_levels)
    for base in range(1 + top_levels, LEVELS - 1):
        level(0, base, False)
    e.wait_ge(k.s_dve_chain, chain.c.at())
    for qt in range(1, TT):
        ins = TS(scores[qt], scores[qt], TAKEN, MASKED, ALU.not_equal, ALU.mult)
    chain(ins)
    level(0, LEVELS - 1, False, last=True)

    def soften(qt, h):
        u, cw = qt * HEADS + h, (qt + 1) * P
        p, mx = k.d_p[:, (h % 2) * T:(h % 2) * T + cw], k.tok[:, TOK_MX + h % 2:TOK_MX + h % 2 + 1]
        bias = scores[qt] if qt else k.const[:, C_CAUS + T - P:C_CAUS + T]
        e.wait_ge(k.s_lg_mm, u + 1)
        if u >= 2:
            e.wait_ge(k.s_pt_mm, u - 1)
        chain(STT(out=p, in0=k.ps[4 + h % 2][:, 0:cw], scalar=0.125, in1=bias, op0=ALU.mult, op1=ALU.add))
        chain(e.tensor_reduce(mx, p, AX.X, ALU.max))
        TS(k.tok[:, TOK_NM + h % 2:TOK_NM + h % 2 + 1], mx, -1.0, None, ALU.mult).then_inc(k.s_lg_masked, 1)

    def normalise(qt, h):
        u, cw = qt * HEADS + h, (qt + 1) * P
        p = k.d_p[:, (h % 2) * T:(h % 2) * T + cw]
        r = k.tok[:, TOK_R + h % 2:TOK_R + h % 2 + 1]
        e.wait_ge(k.s_p_exp, u + 1)
        chain(e.reciprocal(r, k.tok[:, TOK_SUM + h % 2:TOK_SUM + h % 2 + 1]))
        TS(p, p, r, None, ALU.mult).then_inc(k.s_p_norm, 1)

    by_head = lambda ap: ap.rearrange("p (h t) -> p h t", h=HEADS)

    def attended(c):
        e.wait_ge(k.s_y_hi, 2 + c + 1)
        cols_ = lambda y: y[:, 4 * T:6 * T].rearrange("p (j t) -> p j t", j=2)[:, :, c * P:(c + 1) * P]
        TTn(cols_(k.y_lo), k.ps[7][:, 0:2 * P].rearrange("p (j t) -> p j t", j=2), cols_(k.y_hi).bitcast(F32),
            ALU.subtract).then_inc(k.s_y_lo, 1)

    soften(0, 0)
    soften(0, 1)
    for c in range(TT):
        e.wait_ge(k.s_vn_mm, c + 1)
        beta = k.tok[:, TOK_BETA + c * HEADS:TOK_BETA + (c + 1) * HEADS].unsqueeze(2).broadcast_to([P, HEADS, P])
        TTn(by_head(k.g_vn[:]), by_head(k.ps[0][:]), beta, ALU.mult).then_inc(k.s_vn_done, 1)
        normalise(c, 0)
        if c:
            attended(c - 1)
        soften(c, 2)
        e.wait_ge(k.s_st_mm, c + 1)
        e.wait_ge(k.s_o_part, c + 1)
        for h in range(HEADS):
            t_ = c * HEADS + h
            s = k.g_s[:, h * P:(h + 1) * P]
            ins = STT(out=s, in0=s, scalar=k.tok[:, TOK_ELAST + t_:TOK_ELAST + t_ + 1],
                      in1=k.ps[3][:, h * P:(h + 1) * P], op0=ALU.mult, op1=ALU.add)
        ins.then_inc(k.s_st_done, 1)
        normalise(c, 1)
        soften(c, 3)
        normalise(c, 2)
        if c + 1 < TT:
            soften(c + 1, 0)
        normalise(c, 3)
        if c + 1 < TT:
            soften(c + 1, 1)
        e.wait_ge(k.s_st_done, c + 2)
    attended(TT - 1)
    unit_inverse(GRP_GO, TOK_RG, HEADS * TT)
    for h in range(HEADS):
        e.wait_ge(k.s_unit_row, ROW_GO + h + 1)
        o = til(k.qkv, 8 + h)
        chain(STT(out=o, in0=o, scalar=col(k, "gdn_norm"), in1=k.ps[4 + h][:], op0=ALU.mult, op1=ALU.mult))
        e.wait_ge(k.s_z_silu, h + 1)
        TTn(o, o, til(k.proj, Z + h), ALU.mult).then_inc(k.s_go_norm, 1)
    e.wait_ge(k.s_go_norm, HEADS)
    for h in range(HEADS):
        e.wait_ge(k.s_y_hi, 2 + TT + h + 1)
        TTn(til(k.y_lo, h), til(k.qkv, 8 + h), til(k.y_hi, h).bitcast(F32), ALU.subtract).then_inc(k.s_y_lo, 1)

    def residual(pan0, panels_per_tile, gain, banks=2, split=True, feeds=True, per=4):
        chain(e.memset(k.sqacc[:], 0.0))
        with e.Fori(0, KT // per) as i:
            fed.enter(i, per if feeds else 0)
            for j in range(per):
                m = i * per + j
                num, den = panels_per_tile
                e.wait_ge(k.s_panel_used, i * (per * num // den) + (SPLIT + pan0 + (j * num) // den + num))
                x = rtil(k.x, m)
                ins = TTn(x, x, k.ps[j % banks][:], ALU.add)
                ins.then_inc(k.acc_free[j % banks], 1)
                e.wait_ge(k.acc_free[j % banks], acc_value(i, j, banks, per))
                if feeds:
                    e.sem_inc(k.s_x_new, 1)
                    g = k.vec[:, bass.ds(i * per + (VEC[gain][0] + j), 1)]
                    feed(x, g, rtil(k.h_hi, m), rtil(k.h_lo, m), split=split)
            fed.leave(KT // per)
        for b in range(banks):
            freed[b] += KT // banks


    def acc_value(i, j, banks, per):
        return i * (per // banks) + (freed[j % banks] + j // banks + 1)

    residual(32, (1, 1), "norm_cross")

    invert(3, k.rstd)
    for j in range(HEADS):
        e.wait_ge(k.s_panel_used, SPLIT + 40 + j + 1)
        TTn(til(k.a_q, j), k.ps[j][:], k.rstd[:], ALU.mult).then_inc(k.acc_free[j], 1)
        freed[j] += 1
        e.wait_ge(k.acc_free[j], freed[j])
        e.sem_inc(k.s_aq_raw, 1)
    unit_inverse(GRP_AQ, TOK_RG, HEADS * TT)
    for h in range(HEADS):
        e.wait_ge(k.s_unit_row, ROW_AQ + h + 1)
        q = til(k.a_q, h)
        STT(out=q, in0=q, scalar=col(k, "xa_q"), in1=k.ps[4 + h][:], op0=ALU.mult, op1=ALU.mult).then_inc(k.s_aq_done, 1)

    def maxima(h):
        for half in range(2):
            t_ = TT * (h % 2) + 2 * half
            e.wait_ge(k.s_al_mm, 2 * h + half + 1)
            chain(e.tensor_reduce(tok(TOK_MX + t_, 2), k.ps[half][:].rearrange("p (n m) -> p n m", n=2), AX.X,
                                  ALU.max))
            TS(tok(TOK_NM + t_, 2), tok(TOK_MX + t_, 2), -XA_SCALE, None, ALU.mult).then_inc(k.s_al_max, 1)

    maxima(0)
    for h in range(HEADS):
        for half in range(2):
            t_ = TT * (h % 2) + 2 * half
            e.wait_ge(k.s_al_exp, 2 * h + half + 1)
            chain(e.reciprocal(tok(TOK_R + t_, 2), tok(TOK_SUM + t_, 2)))
            for n in range(2):
                at = (h % 2) * TT * MEM + (2 * half + n) * MEM
                ins = TS(k.a_p[:, at:at + MEM], k.a_p[:, at:at + MEM], tok(TOK_R + t_ + n, 1), None, ALU.mult)
            ins.then_inc(k.s_al_norm, 1)
        if h + 1 < HEADS:
            maxima(h + 1)
        e.wait_ge(k.s_ao_hi_done, h + 1)
        TTn(til(k.ao_lo, h), k.ps[4 + h % 2][:], til(k.ao_hi, h).bitcast(F32), ALU.subtract).then_inc(k.s_ao_lo_done, 1)
    residual(44, (1, 2), "norm_mlp")

    invert(4, k.rstd)
    for half in range(2):
        pan0 = 48 + 32 * half
        with e.Fori(0, MTH // 4) as i:
            for j in range(4):
                m = i * 4 + j
                e.wait_ge(k.s_panel_used, m + (SPLIT + pan0 + 1))
                STT(out=til(k.u_t, j % 2), in0=k.ps[j % 2][:], scalar=0.0, in1=k.rstd[:], op0=ALU.max,
                    op1=ALU.mult).then_inc(k.acc_free[j % 2], 1)
                e.wait_ge(k.acc_free[j % 2], i * 2 + (freed[j % 2] + j // 2 + 1))
                e.sem_inc(k.s_up_relu, 1)
                e.wait_ge(k.s_up_hi, m + (half * MTH + 1))
                TTn(rtil(k.u_lo, m), til(k.u_t, 2 + j % 2), rtil(k.u_hi, m).bitcast(F32),
                    ALU.subtract).then_inc(k.s_up_lo, 1)
        for b in range(2):
            freed[b] += MTH // 2
        residual(pan0 + 16, (2, 1), "ln1", feeds=half == 1)

    invert(5, k.rstd)
    st = lambda n: til(k.s_t, n)
    with e.Fori(0, KT) as i:
        chain.c.enter(i, 12)

        def leave(dst, bank, tile):
            e.wait_ge(k.s_panel_used, i * 8 + (SPLIT + PAN_S6 + MIX_LAST[tile] + 1))
            TTn(dst, k.ps[bank][:], k.rstd[:], ALU.mult).then_inc(k.acc_free[bank], 1)
            e.wait_ge(k.acc_free[bank], i * (2 if bank == 0 else 1) + (freed[bank] + (2 if tile == 6 else 1)))

        leave(st(7), 0, 0)
        u = st(0)
        for s in range(4):
            w = k.vec[:, bass.ds(i * 4 + (VEC["conv_b"][0] + 3 - s), 1)]
            if s == 0:
                ins = TS(u, st(7), w, k.vec[:, bass.ds(i + VEC["conv_bb"][0], 1)], ALU.mult, ALU.add)
            else:
                ins = STT(out=u[:, s:T], in0=st(7)[:, 0:T - s], scalar=w, in1=u[:, s:T], op0=ALU.mult, op1=ALU.add)
            if s == 3:
                ins.then_inc(k.s_s2_u, 1)
            else:
                chain(ins)
        e.wait_ge(k.s_s2_uhi, i + 1)
        TTn(k.ub_lo[:], u, k.ub_hi[:].bitcast(F32), ALU.subtract).then_inc(k.s_s2_ulo, 1)
        leave(st(1), 1, 1)
        e.sem_inc(k.s_s2_gl, 1)
        e.wait_ge(k.s_s2_gsq, i + 1)
        chain(TS(st(2), st(2), 0.044715, 1.0, ALU.mult, ALU.add))
        TTn(st(2), st(2), st(1), ALU.mult).then_inc(k.s_s2_gt, 1)
        for n in range(2):
            leave(rtil(k.gates, i + n * KT), 4 + n, 2 + n)
            e.sem_inc(k.s_s2_gate, 1)
        e.wait_ge(k.s_s2_gsig, i + 1)
        chain(TTn(st(1), st(1), st(2), ALU.mult))
        e.wait_ge(k.s_s2_i, i + 1)
        e.sem_inc(k.acc_free[2], 1)
        e.sem_inc(k.acc_free[3], 1)
        e.wait_ge(k.s_s2_a2, i + 1)
        e.wait_ge(k.s_s2_th, i + 1)
        STT(out=st(7), in0=st(7), scalar=1.0, in1=st(6), op0=ALU.add, op1=ALU.mult).then_inc(k.s_s2_m, 1)
        chain(TTn(st(4), st(4), st(0), ALU.mult))
        e.wait_ge(k.s_s2_s, i + 1)
        chain(TTn(st(4), st(4), st(7), ALU.mult))
        chain(e.tensor_tensor_scan(st(8), st(5), st(4), 0.0, ALU.mult, ALU.add))
        TTn(st(8), st(8), st(1), ALU.mult).then_inc(k.s_s2_yb, 1)
        e.wait_ge(k.s_s2_yb_hi, i + 1)
        TTn(rtil(k.yb_lo, i), st(8), rtil(k.yb_hi, i).bitcast(F32), ALU.subtract)
        leave(st(0), 6, 4)
        leave(st(1), 7, 5)
        leave(st(2), 0, 6)
        chain(TTn(st(2), st(2), st(1), ALU.mult))
        for s in range(3):
            w = k.vec[:, bass.ds(i * 3 + (VEC["conv_a"][0] + 2 - s), 1)]
            if s == 0:
                chain(TS(st(3), st(2), w, None, ALU.mult))
            else:
                chain(STT(out=st(3)[:, s:T], in0=st(2)[:, 0:T - s], scalar=w, in1=st(3)[:, s:T], op0=ALU.mult,
                          op1=ALU.add))
        TTn(st(3), st(3), st(0), ALU.mult).then_inc(k.s_s2_ya, 1)
        e.wait_ge(k.s_s2_ya_hi, i + 1)
        TTn(rtil(k.ya_lo, i), st(3), rtil(k.ya_hi, i).bitcast(F32), ALU.subtract).then_inc(k.s_s2_free, 1)
        assert chain.c.n == 12, chain.c.n
        chain.c.leave(KT)
    for b in range(8):
        freed[b] += KT * (2 if b == 0 else 1)

    e.wait_ge(k.s_s2_gate_done, 2 * KT)
    with e.Fori(0, KT // 2) as i:
        chain.c.enter(i, 4)
        for j in range(2):
            for n in range(2):
                b = 2 * j + n
                e.wait_ge(k.s_panel_used, i * 4 + (SPLIT + PAN_S7 + b + 1))
                TTn(st(b), k.ps[b][:], rtil(k.gates, i * 2 + (j + n * KT)), ALU.mult).then_inc(k.acc_free[b], 1)
                e.wait_ge(k.acc_free[b], i + (freed[b] + 1))
            chain(TTn(st(2 * j), st(2 * j), st(2 * j + 1), ALU.add))
            e.sem_inc(k.s_mg, 1)
            e.wait_ge(k.s_mg_hi, i * 2 + j + 1)
            ins = TTn(rtil(k.mg_lo, i * 2 + j), st(2 * j), rtil(k.mg_hi, i * 2 + j).bitcast(F32), ALU.subtract)
            chain(ins)
            e.sem_inc(k.s_mg_lo, 1)
        chain.c.leave(KT // 2)
    for b in range(4):
        freed[b] += KT // 2
    residual(PAN_S8, (1, 1), "ln2")

    invert(6, k.rstd)
    with e.Fori(0, FFN // 2) as i:
        for j in range(2):
            for n in range(2):
                b = 2 * j + n
                e.wait_ge(k.s_panel_used, i * 4 + (SPLIT + PAN_S9 + b + 1))
                TTn(til(k.f_t, j + 2 * n), k.ps[b][:], k.rstd[:], ALU.mult).then_inc(k.acc_free[b], 1)
                e.wait_ge(k.acc_free[b], i + (freed[b] + 1))
                if n == 0:
                    e.sem_inc(k.s_f_g, 1)
            e.wait_ge(k.s_f_silu, i * 2 + j + 1)
            TTn(til(k.f_t, j), til(k.f_t, j), til(k.f_t, 2 + j), ALU.mult).then_inc(k.s_f_hid, 1)
            e.wait_ge(k.s_f_hi_done, i * 2 + j + 1)
            TTn(rtil(k.f_lo, i * 2 + j), til(k.f_t, j), rtil(k.f_hi, i * 2 + j).bitcast(F32),
                ALU.subtract).then_inc(k.s_f_lo_done, 1)
    for b in range(4):
        freed[b] += FFN // 2
    residual(PAN_DOWN, (4, 1), "final", split=False)

    invert(7, k.rstd)
    for m in range(KT):
        x = til(k.x, m)
        STT(out=x, in0=x, scalar=col(k, "final", m), in1=k.rstd[:], op0=ALU.mult, op1=ALU.mult).then_inc(k.s_out_ready, 1)


def program(nc, d, out):
    with ExitStack() as ctx:
        k = plan_memory(nc, ctx)
        signals(nc, ctx, k)
        block = ctx.enter_context(nc.Block())

        @block.sync
        def _(sp):
            sync_program(nc, k, d)
            for m in range(KT):
                sp.wait_ge(k.s_out_ready, m + 1)
                sp.dma_start(out[m * P:(m + 1) * P, :], til(k.x, m)).then_inc(k.s_out_sent, 16)
            sp.wait_ge(k.s_out_sent, 16 * KT)

        @block.gpsimd
        def _(pool):
            gpsimd_program(nc, k)

        @block.scalar
        def _(act):
            scalar_program(nc, k, d)

        @block.vector
        def _(dve):
            vector_program(nc, k)

        @block.tensor
        def _(pe):
            tensor_program(nc, k)


def constants():
    import numpy as np

    j, i = np.arange(P)[:, None], np.arange(P)[None, :]
    parts = [j == i, np.ones((P, P)), j // 64 == i // 64, j <= i]
    for lev in range(LEVELS):
        s = 1 << lev
        parts.append((j // (2 * s) == i // (2 * s)) & (j % (2 * s) < s) & (i % (2 * s) >= s))
    parts.append(np.zeros((P, T - P)))
    c = np.concatenate([p.astype(np.float32) for p in parts], 1)
    return np.concatenate([c, np.where(i <= j, 0.0, MASKED).astype(np.float32)], 1)


def panels(w):
    kk, m = w.shape
    return w.reshape(kk // P, P, m // P, P).transpose(2, 1, 0, 3).reshape(m // P, P, kk)


def kernel(**inputs):
    import numpy as np
    import concourse.bacc as bacc
    from concourse.bass_utils import run_bass_kernel_spmd

    a = {n: np.asarray(v) for n, v in inputs.items()}
    f = np.float32
    cat = np.concatenate
    w = a["w_in"][0]
    last = cat([w[:, 2440:2504], w[:, 2048:2056], w[:, 2504:2508], np.zeros((D, 52), f)], 1)
    w_in = cat([w[:, 2056:2440], last, w[:, 2508:3020], w[:, 0:2048]], 1)
    kv = a["xa_wkv"][0]
    wk = panels(kv[:, 0:512])
    wv = kv[:, 512:].reshape(4, 2, P, T).transpose(0, 2, 1, 3).reshape(4, P, 2 * T)
    wo = panels(a["xa_wo"][0]).reshape(4, 2, P, T).transpose(0, 2, 1, 3).reshape(4, P, 2 * T)
    up = panels(a["mlp_w1"][0])
    dn = panels(a["mlp_w2"][0]).reshape(KT, P, 2, 2, D).transpose(2, 0, 3, 1, 4).reshape(2, 2 * KT, P, D)
    panels_a = cat([wk, wv, panels(w_in), panels(a["w_out"][0]), panels(a["xa_wq"][0]), wo,
                    up[:MTH], dn[0], up[MTH:], dn[1]], 0)
    w2 = panels(a["w_in_2"][0]).reshape(7, KT, P, D)
    lru = np.zeros((KT, 2, 64, 2, 2, 64), f)
    for n, name in enumerate(("lru_wa_2", "lru_wx_2")):
        g = a[name][0].reshape(KT, 2, 64, 64)
        for b in range(2):
            lru[:, b, :, n, b, :] = g[:, b]
    lru = lru.reshape(KT, P, 2 * P)
    mix = cat([w2[3], w2[4], w2[5], w2[6], lru, w2[0], w2[1], w2[2]], 2)
    merge = np.stack([panels(a["w_out_a_2"][0]), panels(a["w_out_b_2"][0])], 1).reshape(2 * KT, P, D)
    ffn = np.stack([panels(a["w_ffn_gate_2"][0]), panels(a["w_ffn_up_2"][0])], 1).reshape(2 * FFN, P, D)
    panels_b = cat([merge, panels(a["w_o_2"][0]), ffn], 0)
    down = panels(a["w_ffn_down_2"][0])
    kvb = a["dsa_w_kvb"][0]
    two = lambda m: m.reshape(2, P, 256).transpose(1, 0, 2).reshape(P, 512)
    small = cat([two(a["dsa_w_qb"][0]), two(a["dsa_w_qi"][0]), kvb[:, :64], kvb[:, :64], kvb[:, 64:]], 1)

    def cols(v):
        return v.reshape(-1, P).T

    def taps(v):
        n, c = v.shape
        return v.reshape(n, c // P, P).transpose(2, 1, 0).reshape(P, -1)

    def rows(v):
        return np.broadcast_to(np.tile(v, TT)[None], (P, 16))

    vec = cat([cols(a["norm_mix"]), cols(a["norm_mem"]), cols(a["norm_cross"]), cols(a["norm_mlp"]), cols(a["ln1_g_2"]),
               cols(a["ln2_g_2"]), cols(a["final_g_2"]), taps(a["gdn_conv"][0]), cols(a["gdn_norm"]),
               cols(np.tile(a["dsa_q_norm"], (1, 2))), cols(np.tile(a["dsa_k_norm"], (1, 2))), taps(a["conv_dw"][0]),
               cols(a["conv_dw_b"]), cols(a["conv_ln_g"]), cols(a["conv_ln_b"]), cols(a["xa_q_norm"]),
               cols(a["xa_k_norm"]), taps(a["conv_a_w_2"][0]), taps(a["conv_b_w_2"][0]), cols(a["conv_b_b_2"]),
               cols(a["lru_ba_2"]), cols(a["lru_bx_2"]), cols(a["lru_lambda_2"]), cols(a["gate_bias_2"]),
               rows(a["gdn_a_log"][0]), rows(a["gdn_dt_bias"][0])], 1)
    arrays = {
        "xT": a["x"][0].T, "memT": a["mem"][0].T, "const": constants(), "vec": vec, "small_w": small,
        "panels_a": panels_a, "mix": mix, "panels_b": panels_b, "down": down,
    }
    arrays = {n: np.ascontiguousarray(v) for n, v in arrays.items()}
    nc = bacc.Bacc("TRN2", target_bir_lowering=False, num_devices=1, dynamic_dma_scratch_size=1024)
    ap = {n: nc.dram_tensor(n, v.shape, F32, kind="ExternalInput").ap() for n, v in arrays.items()}
    d = Plan()
    d.x, d.mem, d.const, d.vec, d.small_w = ap["xT"], ap["memT"], ap["const"], ap["vec"], ap["small_w"]
    d.panels_a, d.mix, d.panels_b, d.down = ap["panels_a"], ap["mix"], ap["panels_b"], ap["down"]
    out = nc.dram_tensor("outT", (D, T), F32, kind="ExternalOutput").ap()
    program(nc, d, out)
    got = run_bass_kernel_spmd(nc, [arrays], core_ids=[0]).results[0]["outT"]
    return np.ascontiguousarray(got.T)[None]
```
